# Optimizing a Trainium2 kernel written in Bass

```python
import jax, jax.numpy as jnp
from jax import lax
import numpy as np

D_MODEL = 1024
BATCH = 1
SEQ = 128
DEPTH = 2
DEC_BATCH = 1
DEC_SEQ = 512
PAST_LEN = 128

GRID_W = 64
N_DIR = 2
N_ADA = 6
RMS_EPS = 1e-6
N_A_LAYERS = (DEPTH + 1) // 2
N_B_LAYERS = DEPTH // 2
A_HEADS = 8
A_DK = D_MODEL // 16
A_DV = D_MODEL // A_HEADS
A_CHUNK = 64
A_QK = A_HEADS * A_DK
A_V = A_HEADS * A_DV
A_COLS = 2 * A_QK + 2 * A_V + 2 * N_DIR * A_HEADS
B_HEAD_DIM = 64
B_HEADS = D_MODEL // B_HEAD_DIM
B_LORA_W = 64
B_LORA_A = 64
B_LORA_G = 128
B_DECAY_SCALE = 0.606531
B_LN_EPS = 64e-5
D_FF = 128 * ((8 * D_MODEL // 3 + 127) // 128)
N_EXPERTS = 8
TOP_K = 2
D_FF_EXPERT = D_FF // 2

kernel_name = 'bidir_mlstm_rwkv7_prefix_diffusion_step'

def rmsnorm(x, g):
    xf = x.astype(jnp.float32)
    y = xf * lax.rsqrt(jnp.mean(xf * xf, -1, keepdims=True) + RMS_EPS)
    return y.astype(x.dtype) * g

def swiglu(h, w_gu, w_down):
    gate, up = jnp.split(h @ w_gu, 2, axis=-1)
    return (jax.nn.silu(gate) * up) @ w_down

def moe_swiglu(h, w_router, b_router, w_gu, w_down):
    B, T, D = h.shape
    hf = h.reshape(B * T, D)
    logits = (hf @ w_router).astype(jnp.float32) + b_router.astype(jnp.float32)
    top_logit, top_idx = lax.top_k(logits, TOP_K)
    top_w = jax.nn.softmax(top_logit, axis=-1)
    combine = jnp.sum(jax.nn.one_hot(top_idx, N_EXPERTS, dtype=jnp.float32) * top_w[..., None], axis=1).astype(h.dtype)
    out = jnp.zeros_like(hf)
    for e in range(N_EXPERTS):
        out = out + combine[:, e:e + 1] * swiglu(hf, w_gu[e], w_down[e])
    return out.reshape(B, T, D)

def shift_1d(x):
    half = x.shape[-1] // 2
    prev = jnp.pad(x[:, :-1, :half], ((0, 0), (1, 0), (0, 0)))
    nxt = jnp.pad(x[:, 1:, half:], ((0, 0), (0, 1), (0, 0)))
    return jnp.concatenate([prev, nxt], axis=-1)

def shift_grid(x):
    B, T, D = x.shape
    rows = T // GRID_W
    g = x.reshape(B, rows, GRID_W, D)
    q = D // 4
    left = jnp.pad(g[:, :, :-1, :q], ((0, 0), (0, 0), (1, 0), (0, 0)))
    right = jnp.pad(g[:, :, 1:, q:2 * q], ((0, 0), (0, 0), (0, 1), (0, 0)))
    up = jnp.pad(g[:, :-1, :, 2 * q:3 * q], ((0, 0), (1, 0), (0, 0), (0, 0)))
    down = jnp.pad(g[:, 1:, :, 3 * q:], ((0, 0), (0, 1), (0, 0), (0, 0)))
    return jnp.concatenate([left, right, up, down], axis=-1).reshape(B, T, D)

def mlstm_scan(q, k, v, log_i, log_f, C0, n0, m0):
    B, H, T, _ = q.shape
    nc = T // A_CHUNK

    def chunks(a):
        a = a.reshape((B, H, nc, A_CHUNK) + a.shape[3:])
        return jnp.moveaxis(a, 2, 0)

    tril = jnp.tril(jnp.ones((A_CHUNK, A_CHUNK), dtype=bool))

    def step(carry, inp):
        C, n, m = carry
        qc, kc, vc, ic, fc = inp
        b = jnp.cumsum(fc, axis=-1)
        logw = jnp.where(tril, b[..., :, None] - b[..., None, :] + ic[..., None, :], -jnp.inf)
        inter = b + m[..., None]
        m_row = jnp.maximum(inter, jnp.max(logw, axis=-1))
        w_intra = jnp.exp(logw - m_row[..., None])
        w_inter = jnp.exp(inter - m_row)
        s = jnp.einsum('bhjd,bhsd->bhjs', qc, kc) * w_intra
        num = jnp.einsum('bhjs,bhsv->bhjv', s, vc) + w_inter[..., None] * jnp.einsum('bhjd,bhdv->bhjv', qc, C)
        den = jnp.sum(s, axis=-1) + w_inter * jnp.einsum('bhjd,bhd->bhj', qc, n)
        h = num / jnp.maximum(jnp.abs(den), jnp.exp(-m_row))[..., None]
        b_end = b[..., -1]
        log_g = b_end[..., None] - b + ic
        m_new = jnp.maximum(b_end + m, jnp.max(log_g, axis=-1))
        decay = jnp.exp(b_end + m - m_new)
        w_s = jnp.exp(log_g - m_new[..., None])
        C = decay[..., None, None] * C + jnp.einsum('bhs,bhsd,bhsv->bhdv', w_s, kc, vc)
        n = decay[..., None] * n + jnp.einsum('bhs,bhsd->bhd', w_s, kc)
        return (C, n, m_new), h

    (C, n, m), h = lax.scan(step, (C0, n0, m0), (chunks(q), chunks(k), chunks(v), chunks(log_i), chunks(log_f)))
    h = jnp.moveaxis(h, 0, 2).reshape(B, H, T, -1)
    return h, (C, n, m)

def mlstm_mixer(h, w_in, b_in, g_head, w_out, C0, n0, m0):
    B, T, _ = h.shape
    f32 = jnp.float32
    z = h @ w_in + b_in
    cuts = [A_QK, 2 * A_QK, 2 * A_QK + A_V, 2 * A_QK + 2 * A_V, 2 * A_QK + 2 * A_V + N_DIR * A_HEADS]
    q, k, v, o, gi, gf = jnp.split(z, cuts, axis=-1)

    def heads(a, d):
        return a.reshape(B, T, A_HEADS, d).transpose(0, 2, 1, 3).astype(f32)

    q = heads(q, A_DK)
    k = heads(k, A_DK) * (A_DK ** -0.5)
    v = heads(v, A_DV)
    log_i = gi.astype(f32).reshape(B, T, N_DIR, A_HEADS).transpose(2, 0, 3, 1)
    log_f = jax.nn.log_sigmoid(gf.astype(f32).reshape(B, T, N_DIR, A_HEADS).transpose(2, 0, 3, 1))
    C0, n0, m0 = C0.astype(f32), n0.astype(f32), m0.astype(f32)
    h_f, st_f = mlstm_scan(q, k, v, log_i[0], log_f[0], C0[:, 0], n0[:, 0], m0[:, 0])
    flip = lambda a: jnp.flip(a, axis=2)
    h_b, st_b = mlstm_scan(flip(q), flip(k), flip(v), flip(log_i[1]), flip(log_f[1]), C0[:, 1], n0[:, 1], m0[:, 1])
    hs = h_f + flip(h_b)
    hs = hs * lax.rsqrt(jnp.mean(hs * hs, axis=-1, keepdims=True) + RMS_EPS)
    hs = hs.transpose(0, 2, 1, 3).reshape(B, T, A_V).astype(h.dtype) * g_head
    out = (hs * jax.nn.sigmoid(o)) @ w_out
    C = jnp.stack([st_f[0], st_b[0]], axis=1)
    n = jnp.stack([st_f[1], st_b[1]], axis=1)
    m = jnp.stack([st_f[2], st_b[2]], axis=1)
    return out, (C, n, m)

def rwkv_scan(r, w, k, v, kk, a, S0):
    def step(S, inp):
        r_t, w_t, k_t, v_t, kk_t, a_t = inp
        S = (S * w_t[:, :, None, :]
             - jnp.einsum('bhvk,bhk->bhv', S, kk_t)[..., None] * (kk_t * a_t)[:, :, None, :]
             + v_t[..., None] * k_t[:, :, None, :])
        return S, jnp.einsum('bhvk,bhk->bhv', S, r_t)
    return lax.scan(step, S0, (r, w, k, v, kk, a))

def rwkv_mixer(h, mu, w_rkv, w0, w1, w2, a0, a1, a2, g1, g2, k_k, k_a, r_k, ln_g, ln_b, w_out, S0, grid):
    B, T, D = h.shape
    f32 = jnp.float32
    xx = (shift_grid(h) if grid else shift_1d(h)) - h
    xm = h[None] + xx[None] * mu[:, None, None, :]
    rkv = jnp.einsum('cbtd,cde->cbte', xm[:3], w_rkv).astype(f32)
    r, k, v = rkv[0], rkv[1], rkv[2]
    xw, xa, xg = xm[3], xm[4], xm[5]
    g = jax.nn.sigmoid(xg @ g1) @ g2
    lora_w = jnp.einsum('zbtl,zld->zbtd', jnp.tanh(jnp.einsum('btd,zdl->zbtl', xw, w1)), w2)
    log_w = -B_DECAY_SCALE * jax.nn.sigmoid((w0[:, None, None, :] + lora_w).astype(f32))
    lora_a = jnp.einsum('zbtl,zld->zbtd', jnp.einsum('btd,zdl->zbtl', xa, a1), a2)
    a = jax.nn.sigmoid((a0[:, None, None, :] + lora_a).astype(f32))
    heads = lambda t: t.reshape(t.shape[:-1] + (B_HEADS, B_HEAD_DIM))
    kk = heads(k * k_k.astype(f32))
    kk = kk / jnp.maximum(jnp.sqrt(jnp.sum(kk * kk, axis=-1, keepdims=True)), 1e-12)
    k_dir = heads(k[None] * (1.0 + (a - 1.0) * k_a.astype(f32)))
    r_h, v_h, a_h, w_h = heads(r), heads(v), heads(a), heads(jnp.exp(log_w))
    tm = lambda t: jnp.swapaxes(t, 0, 1)
    flip = lambda t: jnp.flip(t, axis=0)
    S0 = S0.astype(f32)
    S_f, y_f = rwkv_scan(tm(r_h), tm(w_h[0]), tm(k_dir[0]), tm(v_h), tm(kk), tm(a_h[0]), S0[:, 0])
    S_b, y_b = rwkv_scan(flip(tm(r_h)), flip(tm(w_h[1])), flip(tm(k_dir[1])), flip(tm(v_h)), flip(tm(kk)), flip(tm(a_h[1])), S0[:, 1])
    y = tm(y_f) + tm(flip(y_b))
    bonus = jnp.sum(jnp.sum(r_h[None] * k_dir * r_k.astype(f32), axis=-1, keepdims=True) * v_h[None], axis=0)
    y = y + bonus
    mean = jnp.mean(y, axis=-1, keepdims=True)
    var = jnp.mean(jnp.square(y - mean), axis=-1, keepdims=True)
    y = ((y - mean) * lax.rsqrt(var + B_LN_EPS)).reshape(B, T, D).astype(h.dtype) * ln_g + ln_b
    out = (y * g) @ w_out
    return out, jnp.stack([S_f, S_b], axis=1)

def setup_inputs(seed: int = 0) -> dict:
    key = jax.random.key(seed)
    ks = iter(jax.random.split(key, 64))
    nrm = lambda shape, scale: jax.random.normal(next(ks), shape, jnp.float32) * scale
    D = D_MODEL
    NA, NB = N_A_LAYERS, N_B_LAYERS
    f_bias = jnp.tile(jnp.linspace(3.0, 6.0, A_HEADS), N_DIR)
    b_m_in = nrm((NA, A_COLS), 0.02).at[:, A_COLS - N_DIR * A_HEADS:].add(f_bias)
    return {
        'x_prompt': nrm((BATCH, SEQ, D), 1.0),
        'x_sample': nrm((DEC_BATCH, DEC_SEQ, D), 1.0),
        'state_mlstm_C': nrm((DEC_BATCH, NA, N_DIR, A_HEADS, A_DK, A_DV), 0.05),
        'state_mlstm_n': nrm((DEC_BATCH, NA, N_DIR, A_HEADS, A_DK), 0.1),
        'state_mlstm_m': nrm((DEC_BATCH, NA, N_DIR, A_HEADS), 1.0),
        'state_rwkv_S': nrm((DEC_BATCH, NB, N_DIR, B_HEADS, B_HEAD_DIM, B_HEAD_DIM), 0.1),
        'c': nrm((DEC_BATCH, D), 1.0),
        'c_ctx': nrm((D,), 1.0),
        'w_ada': nrm((DEPTH, D, N_ADA * D), 0.5 * D ** -0.5),
        'b_ada': nrm((DEPTH, N_ADA * D), 0.02),
        'g_norm1': 1.0 + nrm((DEPTH, D), 0.02),
        'g_norm2': 1.0 + nrm((DEPTH, D), 0.02),
        'w_m_in': nrm((NA, D, A_COLS), D ** -0.5),
        'b_m_in': b_m_in,
        'g_m_head': 1.0 + nrm((NA, A_V), 0.02),
        'w_m_out': nrm((NA, A_V, D), A_V ** -0.5),
        'mu_rwkv': jax.random.uniform(next(ks), (NB, 6, D), jnp.float32),
        'w_rkv': nrm((NB, 3, D, D), D ** -0.5),
        'w_decay0': jax.random.uniform(next(ks), (NB, N_DIR, D), jnp.float32, -3.0, 3.0),
        'w_decay1': nrm((NB, N_DIR, D, B_LORA_W), D ** -0.5),
        'w_decay2': nrm((NB, N_DIR, B_LORA_W, D), 0.5 * B_LORA_W ** -0.5),
        'w_iclr0': nrm((NB, N_DIR, D), 0.5),
        'w_iclr1': nrm((NB, N_DIR, D, B_LORA_A), D ** -0.5),
        'w_iclr2': nrm((NB, N_DIR, B_LORA_A, D), 0.5 * B_LORA_A ** -0.5),
        'w_gate1': nrm((NB, D, B_LORA_G), D ** -0.5),
        'w_gate2': nrm((NB, B_LORA_G, D), B_LORA_G ** -0.5),
        'k_k': 0.85 + nrm((NB, D), 0.02),
        'k_a': 1.0 + nrm((NB, D), 0.02),
        'r_k': nrm((NB, B_HEADS, B_HEAD_DIM), 0.1),
        'g_ln_x': 1.0 + nrm((NB, D), 0.02),
        'b_ln_x': nrm((NB, D), 0.02),
        'w_rwkv_out': nrm((NB, D, D), D ** -0.5),
        'w_ff_gu': nrm((NA, D, 2 * D_FF), D ** -0.5),
        'w_ff_down': nrm((NA, D_FF, D), D_FF ** -0.5),
        'w_router': nrm((NB, D, N_EXPERTS), D ** -0.5),
        'b_router': nrm((NB, N_EXPERTS), 0.01),
        'w_exp_gu': nrm((NB, N_EXPERTS, D, 2 * D_FF_EXPERT), D ** -0.5),
        'w_exp_down': nrm((NB, N_EXPERTS, D_FF_EXPERT, D), D_FF_EXPERT ** -0.5),
        'g_final': 1.0 + nrm((D,), 0.02),
    }

def reference(x_prompt, x_sample, state_mlstm_C, state_mlstm_n, state_mlstm_m, state_rwkv_S, c, c_ctx,
              w_ada, b_ada, g_norm1, g_norm2, w_m_in, b_m_in, g_m_head, w_m_out,
              mu_rwkv, w_rkv, w_decay0, w_decay1, w_decay2, w_iclr0, w_iclr1, w_iclr2,
              w_gate1, w_gate2, k_k, k_a, r_k, g_ln_x, b_ln_x, w_rwkv_out,
              w_ff_gu, w_ff_down, w_router, b_router, w_exp_gu, w_exp_down, g_final):

    def layer_stack(x, cond, init_C, init_n, init_m, init_S, grid):
        new_A, new_B = [], []
        for i in range(DEPTH):
            j = i // 2
            mod = (jax.nn.silu(cond) @ w_ada[i] + b_ada[i]).reshape(cond.shape[0], N_ADA, 1, D_MODEL)
            sh1, sc1, ga1, sh2, sc2, ga2 = (mod[:, t] for t in range(N_ADA))
            hn = rmsnorm(x, g_norm1[i]) * (1.0 + sc1) + sh1
            if i % 2 == 0:
                out, st = mlstm_mixer(hn, w_m_in[j], b_m_in[j], g_m_head[j], w_m_out[j],
                                      init_C[:, j], init_n[:, j], init_m[:, j])
                new_A.append(st)
            else:
                out, st = rwkv_mixer(hn, mu_rwkv[j], w_rkv[j], w_decay0[j], w_decay1[j], w_decay2[j],
                                     w_iclr0[j], w_iclr1[j], w_iclr2[j], w_gate1[j], w_gate2[j],
                                     k_k[j], k_a[j], r_k[j], g_ln_x[j], b_ln_x[j], w_rwkv_out[j],
                                     init_S[:, j], grid)
                new_B.append(st)
            x = x + ga1 * out
            hn = rmsnorm(x, g_norm2[i]) * (1.0 + sc2) + sh2
            if i % 2 == 0:
                ff = swiglu(hn, w_ff_gu[j], w_ff_down[j])
            else:
                ff = moe_swiglu(hn, w_router[j], b_router[j], w_exp_gu[j], w_exp_down[j])
            x = x + ga2 * ff
        return rmsnorm(x, g_final), new_A, new_B

    nb = x_prompt.shape[0]
    zC = jnp.zeros((nb, N_A_LAYERS, N_DIR, A_HEADS, A_DK, A_DV), jnp.float32)
    zn = jnp.zeros((nb, N_A_LAYERS, N_DIR, A_HEADS, A_DK), jnp.float32)
    zm = jnp.zeros((nb, N_A_LAYERS, N_DIR, A_HEADS), jnp.float32)
    zS = jnp.zeros((nb, N_B_LAYERS, N_DIR, B_HEADS, B_HEAD_DIM, B_HEAD_DIM), jnp.float32)
    y_prompt, ctx_A, ctx_B = layer_stack(x_prompt, c_ctx[None, :], zC, zn, zm, zS, False)
    y_sample, _, _ = layer_stack(x_sample, c, state_mlstm_C, state_mlstm_n, state_mlstm_m, state_rwkv_S, True)
    new_mlstm_C = jnp.stack([s[0] for s in ctx_A], axis=1)
    new_mlstm_n = jnp.stack([s[1] for s in ctx_A], axis=1)
    new_mlstm_m = jnp.stack([s[2] for s in ctx_A], axis=1)
    new_rwkv_S = jnp.stack(ctx_B, axis=1)
    return (y_prompt, y_sample, new_mlstm_C, new_mlstm_n, new_mlstm_m, new_rwkv_S)


_drawn_inputs = setup_inputs


def setup_inputs(seed=0):
    import zlib

    import numpy as np

    out = dict(_drawn_inputs(seed))
    spreads = {}
    factors = {'state_mlstm_C': 7.29,
     'state_mlstm_n': 8.0,
     'state_mlstm_m': 8.0,
     'state_rwkv_S': 8.0,
     'g_norm2': 3.937,
     'g_m_head': 7.721,
     'k_k': 140.707,
     'r_k': 4.474,
     'g_ln_x': 43.034,
     'b_ln_x': 64.0,
     'b_router': 28.975,
     'g_final': 23.173}
    for name, (base, spread) in spreads.items():
        noise = np.random.default_rng([zlib.crc32(name.encode()), seed]).standard_normal(out[name].shape)
        drawn = base * np.exp(spread * noise) if base else spread * noise
        out[name] = __import__('jax').numpy.asarray(drawn.astype(out[name].dtype))
    for name, factor in factors.items():
        out[name] = (out[name] * factor).astype(out[name].dtype)
    return out
```

```python
from contextlib import ExitStack

import numpy as np

import concourse.bass as bass
from concourse import mybir

F32 = mybir.dt.float32
ALU = mybir.AluOpType
ACT = mybir.ActivationFunctionType
AX = mybir.AxisListType

P = 128
D = 1024
KT = D // P
LAT, CTX = 512, 128
TOK = LAT + CTX
HALVES = ((0, LAT), (LAT, TOK))
NADA = 6
EPS = 1e-6
AH, DK, DV = 8, 64, 128
CH = TOK // P
BH, HD = 16, 64
C64 = TOK // HD
DECAY = 0.606531
LN_EPS = 64e-5
DFF = 2816
FT = DFF // P
NE = 8
ET = DFF // 2 // P
IN_TILES = 26
RING = 3
SLAB = 22 * P
NEG = -1e30

CONST = {}
_at = 0
for _name, _w in (("ident", 128), ("ident2", 128), ("ones", 128), ("headones", 128), ("headmean", 128),
                  ("neg0", 128), ("neg1", 128), ("strict0", 128), ("strict1", 128), ("incl0", 64), ("incl1", 64),
                  ("bd2", 128), ("bd4", 128), ("bd8", 128), ("bd16", 128), ("bd32", 128),
                  ("reset", TOK + 1), ("mreset", TOK + 1), ("in_scale", IN_TILES), ("eps", 1), ("ln_eps", 1), ("code", NE)):
    CONST[_name] = (_at, _w)
    _at += _w
N_CONST = _at
VEC = {}
_at = 0
for _name, _w in (("cond", KT * 2), ("b_ada", 2 * NADA * KT), ("gn1", 2 * KT), ("gn2", 2 * KT), ("gf", KT),
                  ("b_in", IN_TILES), ("g_head", KT), ("mu", 6 * KT), ("w0", 2 * KT), ("a0", 2 * KT),
                  ("k_k", KT), ("k_a", KT), ("r_k", KT), ("ln_g", KT), ("ln_b", KT), ("b_router", NE), ("m0", 1)):
    VEC[_name] = (_at, _w)
    _at += _w
N_VEC = _at


class Steps:

    def __init__(self, sem, names):
        self.sem, self.names, self.at = sem, names, {n: k + 1 for k, n in enumerate(names)}
        assert len(self.at) == len(names)
        self.next = 0

    def done(self, ins, name):
        assert self.names[self.next] == name, (self.names[self.next], name)
        self.next += 1
        ins.then_inc(self.sem, 1)

    def wait(self, eng, name, lap=0):
        eng.wait_ge(self.sem, lap * len(self.names) + self.at[name])


def repeat(eng, count, body):
    laps = count // RING
    if laps > 1:
        with eng.Fori(0, laps) as i:
            for u in range(RING):
                body(i * RING + u, u)
    else:
        laps = 0
    for k in range(laps * RING, count):
        body(k, k % RING)


MGRP = [(0, 0), (1, 3), (0, 1), (1, 2), (0, 2), (1, 1), (0, 3), (1, 0), (0, 4), (1, 4)]
VK = [(c, kind) for c in range(CH) for kind in ("v0", "v1", "k")]


def mlstm_steps():
    pe, act, dve, pool = [], [], [], []
    pe += [f"T{c}{k}" for c, k in VK]
    act += [f"T{c}{k}" for c, k in VK]
    act += ["absf", "expf", "lnf", "em"] + [f"winter{c}" for c in range(CH)] + [f"ws{c}" for c in range(CH)] + ["dec"]
    dve += ["minf", "lf", "b0", "b1", "g", "m00", "m01", "m10", "m11", "negG"]
    dve += [f"mprev{k}" for k in range(6)] + [f"gend{k}" for k in range(2)] + ["decx"]
    pe += ["cols0", "cols1", "decb"]
    dve += ["cols0", "cols1"] + [f"decp{k}" for k in range(4)]
    for n, (d, c) in enumerate(MGRP):
        pool += [f"kw{n}"]
        for g in range(2):
            pe += [f"D{n}{g}", f"S{n}{g}"]
            act += [f"W{n}{g}"]
            dve += [f"P{n}{g}"]
            pe += [f"num{n}{g}"]
            dve += [f"comb{n}{g}", f"absd{n}{g}", f"den{n}{g}", f"rden{n}{g}", f"h{n}{g}"]
        pe += [f"C{n}"]
        dve += [f"C{n}"]
    act += ["sigo"]
    for c in range(CH):
        pool += [f"sq{c}"]
        dve += [f"ms{c}"]
        act += [f"sd{c}"]
        dve += [f"rs{c}", f"hn{c}"]
    for h in range(AH):
        pe += [f"hT{h}"]
        dve += [f"mo{h}"]
    return pe, act, dve, pool


LEVELS = (4, 8, 16, 32, 64)
GR = ((0, 4), (4, 8), (8, 10))
CHAINS = ((0, tuple(range(8))), (1, tuple(range(7, -1, -1))), (0, (8, 9)), (1, (9, 8)))


def chain_steps(t):
    return [i for i in range(4) if t < len(CHAINS[i][1])]


def rwkv_steps():
    pe, act, dve = [], [], []
    dve += ["kk0", "sq", "vT0", "vT1"]
    pe += ["knorm", "gate", "w0", "a0"]
    act += ["gate", "knorm", "thw0", "tha0"]
    dve += ["kmax", "krec", "kk"]
    for d in range(2):
        if d:
            pe += ["w1", "a1"]
            act += ["thw1", "tha1"]
        dve += [f"lw{d}", f"c{d}", f"ce{d}", f"a{d}", f"f{d}", f"kd{d}", f"b{d}"]
        act += [f"e1{d}", f"e2{d}", f"e3{d}", f"pend{d}"]
        if d == 0:
            pe += [f"V{g}" for g in range(3)]
            act += [f"V{g}" for g in range(3)]
        dve += [f"R{d}"] + [f"{x}{h}{d}" for x in "QKB" for h in range(2)]
        pe += [f"Kt{d}{g}" for g in range(3)] + [f"Bt{d}{g}" for g in range(3)]
        act += [f"Kt{d}{g}" for g in range(3)] + [f"Bt{d}{g}" for g in range(3)]
        pe += [f"GK{d}{q}" for q in range(5)] + [f"GB{d}{q}" for q in range(5)]
        for q in range(5):
            dve += [f"MkT{d}{q}", f"Ark{d}{q}"]
        for q in range(5):
            dve += [f"LT{d}{q}", f"Arb{d}{q}"]
        dve += [f"LTI{d}", f"XTa{d}", f"XT2{d}"]
    dve += ["kds", "rk", "rkk"]
    pe += ["bonus"]
    dve += ["y0"]
    for lv in LEVELS:
        for ph in ("X", "Y", "Z"):
            for d in range(2):
                for g in range(3):
                    pe += [f"{ph}{lv}{d}{g}"]
                    (act if ph == "X" or (ph == "Z" and lv == 64) else dve).append(f"{ph}{lv}{d}{g}")
    for t in range(8):
        for i in chain_steps(t):
            pe += [f"rhs{t}{i}"]
        for i in chain_steps(t):
            (act if CHAINS[i][0] else dve).append(f"rhs{t}{i}")
        for i in chain_steps(t):
            pe += [f"U{t}{i}"]
        for i in chain_steps(t):
            (act if CHAINS[i][0] else dve).append(f"U{t}{i}")
        for i in chain_steps(t):
            pe += [f"S{t}{i}"]
        for i in chain_steps(t):
            (act if CHAINS[i][0] else dve).append(f"S{t}{i}")
            dve += [f"y{t}{i}"]
    pe += ["mean", "var"]
    dve += ["yc", "ysq", "rv", "yn", "yl", "yg"]
    act += ["std"]
    return pe, act, dve


def build(nc, A, upto=99):
    with ExitStack() as ctx:
        def sb(name, shape):
            return ctx.enter_context(nc.sbuf_tensor(name, shape, F32))

        def sem(name):
            return ctx.enter_context(nc.semaphore(name))

        x = sb("x", [P, KT, TOK])
        ring = sb("ring", [P, RING, SLAB])
        const = sb("const", [P, N_CONST])
        vec = sb("vec", [P, N_VEC])
        wrouter = sb("wrouter", [P, KT, NE])
        scond = sb("scond", [P, KT, 2])
        mods = sb("mods", [P, 2, NADA, KT, 2])
        gs = sb("gs", [P, 2, 2, KT, 2])
        w0h = sb("w0h", [P, 2 * 2 * KT])
        omka = sb("omka", [P, KT])
        bs_in = sb("bs_in", [P, IN_TILES])
        rstd = sb("rstd", [P, TOK])
        NA = 34400
        arena = sb("arena", [P, NA])
        PS = ctx.enter_context(nc.psum_tensor("PS", [P, 8, 512], F32))
        psf = PS[:].rearrange("p b n -> p (b n)")

        def cst(name, rows=slice(0, P)):
            a, w = CONST[name]
            return const[rows, a:a + w]

        def vcol(name, k, n=1):
            a, _ = VEC[name]
            if isinstance(k, int):
                return vec[:, a + k:a + k + n]
            return vec[:, bass.ds(k + a, n)]

        class Region:
            def __init__(self):
                self.at = 0

            def __call__(self, *shape):
                n = int(np.prod(shape))
                v = arena[:, self.at:self.at + n]
                self.at += n
                assert self.at <= NA, self.at
                if len(shape) == 2:
                    v = v.rearrange("p (a b) -> p a b", a=shape[0])
                if len(shape) == 3:
                    v = v.rearrange("p (a b c) -> p a b c", a=shape[0], b=shape[1])
                if len(shape) == 4:
                    v = v.rearrange("p (a b c d) -> p a b c d", a=shape[0], b=shape[1], c=shape[2])
                return v

        def acc(k):
            return psf[:, k * 1024:k * 1024 + TOK]

        stats = psf[:, 3072:3072 + TOK]

        r = Region()
        hn = r(KT, TOK)
        z = r(IN_TILES, TOK)
        vaug = r(CH, AH, DV + 1)
        ktok = r(CH, AH * DK)
        colw = r(CH, 3, 64)
        mprev, gend, dec = r(CH), r(CH), r(CH)
        decx = r(CH, 64)
        decp = r(CH, 2, 4)
        winter_r, ws_r = r(TOK), r(TOK)
        smalls = r(64)
        g_row, negG = r(TOK), r(TOK)
        tmp_row, b_row = winter_r, ws_r
        hs_t = hn.rearrange("p a b -> p (a b)").rearrange("p (c f) -> p c f", c=CH)
        q_, k_ = z[:, 0:4], z[:, 4:8]
        v_, o_ = z[:, 8:16], z[:, 16:24]
        gi, gf = z[:, 24], z[:, 25]
        gm = gf
        vr = z[:, 8:16].rearrange("p a b -> p (a b)")
        Wt = vr[:, 0:1024].rearrange("p (a h n) -> p a h n", a=2, h=4)
        kw = vr[:, 1024:2048].rearrange("p (a n) -> p a n", a=2)
        comb = vr[:, 2048:2048 + 516].rearrange("p (h n) -> p h n", h=4)
        Cst = vr[:, 2564:2564 + 2064].rearrange("p (d s n) -> p d s n", d=2, s=2)
        rden = smalls[:, 0:4]
        ms, rs = smalls[:, 8:16], smalls[:, 16:24]
        sqt = vr[:, 0:1024].rearrange("p (h n) -> p h n", h=AH)

        r = Region()
        hn_f = r(KT, TOK)
        hid_f = r(FT, TOK)
        sg_f = r(RING, TOK)

        r = Region()
        QR = [r(C64, 192) for _ in range(2)]
        KX = [r(C64, P) for _ in range(2)]
        BY = [r(C64, P) for _ in range(2)]
        Ktok = [r(C64, P) for _ in range(2)]
        Btok = [r(C64, P) for _ in range(2)]
        MkT = [r(C64, P) for _ in range(2)]
        Ark = [r(C64, HD) for _ in range(2)]
        Arb = [r(C64, HD) for _ in range(2)]
        LT = [r(C64, P) for _ in range(2)]
        XT = [r(C64, P) for _ in range(2)]
        Vbd = r(C64, P)
        St = r(4, P)
        RU = r(4, P)
        pend = r(2, C64)
        split = r.at
        lhid = r(3, TOK)
        l2 = r(3, P)
        gk = r(KT, TOK)
        tr = ring[:].rearrange("p a b -> p (a b)")
        T = [tr[:, n * TOK:(n + 1) * TOK] for n in range(10)]
        rkv = tr[:, 10 * TOK:13 * TOK].rearrange("p (s n) -> p s n", s=3)
        r = Region()
        hn1 = r(KT, TOK)
        xx = r(KT, TOK)
        xm = [r(KT, TOK) for _ in range(3)]
        stage = gk[:, 0:3]
        assert r.at <= split, (r.at, split)

        r = Region()
        hn2 = r(KT, TOK)
        cb = r(NE, TOK)
        hid = r(ET, TOK)
        sg = r(RING, TOK)
        lg = r(CH, NE)
        eq = r(CH, NE)
        oh1, oh2, l2g, comb_w, code = r(CH, NE), r(CH, NE), r(CH, NE), r(CH, NE), r(CH, NE)
        mx1, mx2, e12, p1, p2 = r(CH), r(CH), r(CH), r(CH), r(CH)

        loaded = sem("loaded")
        slab_ready = [sem(f"slab_ready{k}") for k in range(RING)]
        tiles_done = sem("tiles_done")
        cond_ready = sem("cond_ready")
        mods_ready = sem("mods_ready")
        dve_chain = sem("dve_chain")
        norm_sq, norm_sum, norm_std, norm_rstd = sem("norm_sq"), sem("norm_sum"), sem("norm_std"), sem("norm_rstd")
        norm_x, norm_done = sem("norm_x"), sem("norm_done")
        cb_full = sem("cb_full")
        free = {n: sem(f"{n}_free") for n in ("in", "mout", "ffg", "ffu", "ffd", "rkv", "lora", "rout", "cb",
                                              "moeg", "moeu", "moed")}
        state_loaded = sem("state_loaded")
        ones_set = sem("ones_set")
        zero_set = sem("zero_set")
        st_loaded = sem("st_loaded")
        mpe, mact, mdve, mpool = (Steps(sem(f"mlstm_{n}"), s) for n, s in zip(("pe", "act", "dve", "pool"), mlstm_steps()))
        rpe, ract, rdve = (Steps(sem(f"rwkv_{n}"), s) for n, s in zip(("pe", "act", "dve"), rwkv_steps()))
        out_done = sem("out_done")
        xx_ready, xm_ready = sem("xx_ready"), sem("xm_ready")
        staged = sem("staged")
        stored = [sem(f"stored{k}") for k in range(3)]
        rkv_in = [sem(f"rkv_in{k}") for k in range(1)]
        states_out = sem("states_out")
        logits_full, comb_ready = sem("logits_full"), sem("comb_ready")
        hid_ready = sem("hid_ready")
        exp_in, exp_done = sem("exp_in"), sem("exp_done")
        y_ready = sem("y_ready")

        slab_n = {"sp": 0, "pe": 0}
        base, after = {}, []
        for name, slab_tiles in (("ada", [2] * 48), ("in", [2] * 13), ("mout", [2] * 4), ("ff", [2] * FT), ("ffd", [1] * 8),
                                 ("rkv", [2] * 12), ("lora", [2, 1]), ("rout", [2] * 4), ("moe", [2] * 15 * NE)):
            base[name] = after[-1] if after else 0
            for t in slab_tiles:
                after.append((after[-1] if after else 0) + t)

        def tile_done(eng, name, t):
            eng.wait_ge(tiles_done, t + (base[name] + 1))

        def stream(sp, dram, first, count, width):
            n0 = slab_n["sp"]
            laps = count // RING

            def load(k, slot):
                src = dram[k + first] if isinstance(k, int) else dram[bass.ds(k + first, 1)].rearrange("a p n -> p (a n)")
                sp.dma_start(ring[:, slot, 0:width], src).then_inc(slab_ready[slot], 16)

            need = lambda n: after[n - RING] if n >= RING else 0
            k = 0
            while k < count:
                rest = (count - k) // RING
                step = {need(n0 + k + RING * i + u) - need(n0 + k + RING * (i - 1) + u)
                        for i in range(1, rest) for u in range(RING)}
                if rest > 1 and len(step) == 1 and need(n0 + k) > 0:
                    grow = step.pop()
                    with sp.Fori(0, rest) as i:
                        for u in range(RING):
                            sp.wait_ge(tiles_done, i * grow + need(n0 + k + u))
                            load(i * RING + (k + u), (n0 + k + u) % RING)
                    k += rest * RING
                else:
                    if need(n0 + k):
                        sp.wait_ge(tiles_done, need(n0 + k))
                    load(k, (n0 + k) % RING)
                    k += 1
            slab_n["sp"] += count

        def slabs(pe, count, body):
            n0 = slab_n["pe"]

            def one(k, u):
                slot = (n0 + u) % RING
                lap = (k - u) // RING if isinstance(k, int) else None
                if lap is not None:
                    pe.wait_ge(slab_ready[slot], 16 * (lap + (n0 + u) // RING + 1))
                else:
                    pe.wait_ge(slab_ready[slot], wait_lap(k, u, (n0 + u) // RING))
                body(k, u, slot)
            repeat2(pe, count, one)
            slab_n["pe"] += count

        lap_reg = {}

        def wait_lap(k, u, off):
            return lap_reg["i"] * 16 + 16 * (off + 1)

        def repeat2(eng, count, body):
            laps = count // RING
            if laps > 1:
                with eng.Fori(0, laps) as i:
                    lap_reg["i"] = i
                    for u in range(RING):
                        body(i * RING + u, u)
            else:
                laps = 0
            for k in range(laps * RING, count):
                body(k, k % RING)

        def credit(eng, s, n):
            eng.sem_inc(s, n)

        def mm_tile(pe, a, w, src, kt_n, last_wait=None):
            for kt in range(kt_n):
                if last_wait and kt == kt_n - 1:
                    last_wait()
                for lo, hi in HALVES:
                    m = pe.matmul(acc(a)[:, lo:hi], w(kt), src(kt, lo, hi), start=kt == 0, stop=kt == kt_n - 1)
            return m

        block = ctx.enter_context(nc.Block())

        @block.sync
        def _(sp):
            sp.dma_start(vec[:], A["vec"]).then_inc(loaded, 16)
            sp.dma_start(const[:], A["const"]).then_inc(loaded, 16)
            sp.dma_start(x[:], A["x"]).then_inc(loaded, 16)
            sp.dma_start(wrouter[:], A["wrouter"]).then_inc(loaded, 16)
            k8 = A["k8"]
            W8 = KT * 256
            stream(sp, k8, 0, 48, W8)
            if upto < 2: return
            stream(sp, k8, 48, 13, W8)
            if upto < 3: return
            mact.wait(sp, f"T{CH-1}k")
            sp.dma_start(Cst[:, :, 0, :], A["C0"]).then_inc(state_loaded, 16)
            stream(sp, k8, 61, 4, W8)
            mdve.wait(sp, "m11")
            sp.dma_start(A["m_out"][0:32], gf[0:32, TOK - 1:TOK], allow_slow_non_contiguous=True).then_inc(out_done, 16)
            sp.dma_start(A["m_out"][32:64], gf[32:64, LAT:LAT + 1], allow_slow_non_contiguous=True).then_inc(out_done, 16)
            mdve.wait(sp, "C9")
            sp.dma_start(A["C_out"], Cst[:, :, 1, :]).then_inc(out_done, 16)
            sp.wait_ge(out_done, 48)
            credit(sp, states_out, 1)
            if upto < 4: return
            stream(sp, k8, 65, 22, W8)
            stream(sp, A["ffd"], 0, 8, SLAB)
            if upto < 5: return
            stream(sp, k8, 87, 12, W8)
            stream(sp, k8, 99, 2, W8)
            if upto < 6: return
            for s in stored:
                sp.wait_ge(s, 16 * 9)
            sp.sem_inc(st_loaded, 16)
            with sp.Fori(0, KT) as j:
                sp.wait_ge(st_loaded, j * 16 + 16)
                ract.wait(sp, "std", j)
                rdve.wait(sp, "yg", j)
                jj = bass.ds(j, 1)
                sp.dma_start(rkv, A["rkv_s"][jj].rearrange("a p s n -> p (a s) n")).then_inc(rkv_in[0], 16)
                sp.dma_start(l2, A["l2"][jj].rearrange("a p s n -> p (a s) n")).then_inc(rkv_in[0], 16)
                sp.dma_start(St[:, 0:2], A["S0"][jj].rearrange("a p s n -> p (a s) n")).then_inc(rkv_in[0], 16)
                rdve.wait(sp, "S12", j + 1)
                ract.wait(sp, "S13", j + 1)
                sp.dma_start(A["S_out"][jj].rearrange("a p s n -> p (a s) n"), St[:, 2:4]).then_inc(st_loaded, 16)
            sp.wait_ge(st_loaded, 16 * (KT + 1))
            ract.wait(sp, "std", KT)
            rdve.wait(sp, "yg", KT)
            stream(sp, k8, 101, 4, W8)
            if upto < 7: return
            with sp.Fori(0, NE) as e:
                n0 = slab_n["sp"]
                per = 15
                for k in range(per):
                    slot = (n0 + k) % RING
                    sp.wait_ge(tiles_done, e * 30 + after[n0 + k - RING])
                    if k < ET:
                        src = k8[bass.ds(e * ET + (105 + k), 1)].rearrange("a p n -> p (a n)")
                        w = W8
                    else:
                        src = A["exd"][bass.ds(e * 4 + (k - ET), 1)].rearrange("a p n -> p (a n)")
                        w = SLAB
                    sp.dma_start(ring[:, slot, 0:w], src).then_inc(slab_ready[slot], 16)
            for kt in range(KT):
                sp.wait_ge(y_ready, kt + 1)
                sp.dma_start(A["y"][:, kt], hn2[:, kt]).then_inc(out_done, 16)
            sp.wait_ge(out_done, 48 + 16 * KT)

        @block.gpsimd
        def _(pool):
            if upto < 3: return
            pool.wait_ge(free["in"], 3 + IN_TILES)
            pool.memset(vaug[:, :, :, DV:DV + 1], 1.0).then_inc(ones_set, 1)
            mact.wait(pool, f"T{CH-1}k")
            pool.wait_ge(ones_set, 1)
            pool.memset(Cst[:, :, 1, :], 0.0).then_inc(ones_set, 1)
            pool.wait_ge(ones_set, 2)
            mdve.wait(pool, "cols1")
            for n, (d, c) in enumerate(MGRP):
                if n >= 2:
                    mpe.wait(pool, f"C{n-2}")
                if n >= 1:
                    mpool.wait(pool, f"kw{n-1}")
                mpool.done(pool.tensor_tensor(
                    kw[:, n % 2].rearrange("p (h k) -> p h k", h=AH), ktok[:, c].rearrange("p (h k) -> p h k", h=AH),
                    colw[:, c, 1, d * 32:d * 32 + AH].unsqueeze(2).to_broadcast([P, AH, DK]), ALU.mult), f"kw{n}")
            for c in range(CH):
                mdve.wait(pool, "h91")
                mpool.wait(pool, f"kw9" if c == 0 else f"sq{c-1}")
                if c:
                    mdve.wait(pool, f"ms{c-1}")
                mpool.done(pool.tensor_tensor(sqt.rearrange("p h n -> p (h n)"), hs_t[:, c], hs_t[:, c], ALU.mult), f"sq{c}")
            if upto < 6: return
            pool.wait_ge(free["lora"], 3 + 3)
            n = 0
            for buf in (QR[0], QR[1], KX[0], KX[1], BY[0], BY[1]):
                if n:
                    pool.wait_ge(zero_set, n)
                pool.memset(buf, 0.0).then_inc(zero_set, 1)
                n += 1
            

        @block.tensor
        def _(pe):
            pe.wait_ge(cond_ready, 1)

            def ada(k, u, slot):
                w = ring[:, slot, 0:KT * 256].rearrange("p (kt n) -> p kt n", kt=KT)
                for t in range(2):
                    out = psf[:, 4 * k + 2 * t:4 * k + 2 * t + 2] if isinstance(k, int) else psf[:, bass.ds(k * 4 + 2 * t, 2)]
                    for kt in range(KT):
                        m = pe.matmul(out, w[:, kt, t * P:(t + 1) * P], scond[:, kt, :], start=kt == 0, stop=kt == KT - 1)
                    m.then_inc(tiles_done, 1)
            slabs(pe, 48, ada)

            def norm(n):
                for kt in range(KT):
                    pe.wait_ge(norm_sq, 8 * n + kt + 1)
                    for lo, hi in HALVES:
                        m = pe.matmul(stats[:, lo:hi], cst("ones"), sq_buf[n][:, kt, lo:hi], start=kt == 0, stop=kt == KT - 1)
                m.then_inc(norm_sum, 1)

            def dense8(count, src, name, credits=3):
                def one(k, u, slot):
                    w = ring[:, slot, 0:KT * 256].rearrange("p (kt n) -> p kt n", kt=KT)
                    for t in range(2):
                        pe.wait_ge(free[name], k * 2 + (t + 1))
                        m = mm_tile(pe, (2 * u + t) % 3, lambda kt: w[:, kt, t * P:(t + 1) * P],
                                    lambda kt, lo, hi: src[:, kt, lo:hi], KT)
                        m.then_inc(tiles_done, 1)
                slabs(pe, count, one)

            sq_buf = [hn, hn_f, hn1, hn2, hn2]
            if upto < 2: return
            norm(0)
            pe.wait_ge(norm_done, 16)
            dense8(13, hn, "in")
            if upto < 3: return
            pe.wait_ge(free["in"], 3 + IN_TILES)
            for n, (c, kind) in enumerate(VK):
                if n >= 6:
                    mact.wait(pe, "T%d%s" % VK[n - 6])
                src = {"v0": v_[:, 0:4], "v1": v_[:, 4:8], "k": k_}[kind]
                for t in range(4):
                    m = pe.transpose(PS[:, n % 6, t * P:(t + 1) * P], src[:, t, c * P:(c + 1) * P], cst("ident"))
                mpe.done(m, f"T{c}{kind}")
            mact.wait(pe, "dec")
            for n in range(15):
                c, kind = n // 3, n % 3
                src = (winter_r, ws_r, gi)[kind]
                m = pe.transpose(PS[:, 6 + n // 8, (n % 8) * 64:(n % 8) * 64 + 64], src[0:64, c * P:(c + 1) * P],
                                 cst("ident", slice(0, 64))[:, 0:64])
                if n in (7, 14):
                    mpe.done(m, f"cols{n // 8}")
            mdve.wait(pe, "decx")
            mact.wait(pe, "T%d%s" % VK[-1])
            mpe.done(pe.matmul(PS[:, 0, 0:CH * 64], cst("ones", slice(0, 64)), decx[0:64].rearrange("p c r -> p (c r)"),
                               start=True, stop=True), "decb")
            mdve.wait(pe, "decp3")
            pe.wait_ge(state_loaded, 16)
            pe.wait_ge(ones_set, 2)
            for n, (d, c) in enumerate(MGRP):
                seq = 0 if c < 4 else 1
                tok = slice(c * P, (c + 1) * P)
                for g in range(2):
                    prev = (n, 0) if g else (n - 1, 1)
                    if n or g:
                        mact.wait(pe, f"W{prev[0]}{prev[1]}")
                    for h in range(4):
                        row = d * 32 + 2 * h + g
                        pick = cst("ident", slice(0, 64))[:, row:row + 1].to_broadcast([64, P])
                        o = PS[:, 0, h * P:(h + 1) * P]
                        pe.matmul(o, pick, negG[0:64, tok], start=True, stop=False)
                        pe.matmul(o, g_row[0:64, tok], pick, start=False, stop=False)
                        m = pe.matmul(o, cst("ident"), cst(f"neg{d}"), start=False, stop=True)
                    mpe.done(m, f"D{n}{g}")
                    if n or g:
                        mdve.wait(pe, f"P{prev[0]}{prev[1]}")
                    for h in range(4):
                        hh = 2 * h + g
                        pr = slice(64 * g, 64 * g + 64)
                        m = pe.matmul(PS[:, 1, h * P:(h + 1) * P], k_[pr, hh // 2, tok], q_[pr, hh // 2, tok],
                                      start=True, stop=True)
                    mpe.done(m, f"S{n}{g}")
                    if n or g:
                        mdve.wait(pe, f"comb{prev[0]}{prev[1]}")
                    if n >= 2 and not g:
                        mdve.wait(pe, f"C{n-2}")
                    mdve.wait(pe, f"P{n}{g}")
                    for h in range(4):
                        hh = 2 * h + g
                        pr = slice(64 * g, 64 * g + 64)
                        pe.matmul(PS[:, 4 + h // 2, (h % 2) * 129:(h % 2) * 129 + 129], q_[pr, hh // 2, tok],
                                  Cst[pr, d, seq, (hh // 2) * 129:(hh // 2) * 129 + 129], start=True, stop=True)
                        m = pe.matmul(PS[:, 2 + h // 2, (h % 2) * 129:(h % 2) * 129 + 129], Wt[:, g, h, :],
                                      vaug[:, c, hh, :], start=True, stop=True)
                    mpe.done(m, f"num{n}{g}")
                mpool.wait(pe, f"kw{n}")
                if n:
                    mdve.wait(pe, f"C{n-1}")
                for hh in range(AH):
                    p0 = 64 * (hh % 2)
                    pair = hh // 2
                    m = pe.matmul(PS[p0:p0 + 64, 6 + pair // 2, (pair % 2) * 129:(pair % 2) * 129 + 129],
                                  kw[:, n % 2, hh * DK:(hh + 1) * DK], vaug[:, c, hh, :], start=True, stop=True)
                mpe.done(m, f"C{n}")
            for h in range(AH):
                if h >= 3:
                    mdve.wait(pe, f"mo{h-3}")
                for c in range(CH):
                    mdve.wait(pe, f"hn{c}")
                    m = pe.transpose(acc(h % 3)[:, c * P:(c + 1) * P], hs_t[:, c, h * DV:(h + 1) * DV], cst("ident"))
                mpe.done(m, f"hT{h}")
            mdve.wait(pe, "mo7")
            dense8(4, o_, "mout")
            if upto < 4: return
            norm(1)
            pe.wait_ge(norm_done, 32)

            def ff(k, u, slot):
                w = ring[:, slot, 0:KT * 256].rearrange("p (kt n) -> p kt n", kt=KT)
                for t in range(2):
                    pe.wait_ge(free["ffu"] if t == 0 else free["ffg"], k + 1)
                    m = mm_tile(pe, (2 * u + t) % 3, lambda kt: w[:, kt, t * P:(t + 1) * P],
                                lambda kt, lo, hi: hn_f[:, kt, lo:hi], KT)
                    m.then_inc(tiles_done, 1)
            slabs(pe, FT, ff)
            pe.wait_ge(free["ffu"], 2 + FT)

            def ffd(k, u, slot):
                w = ring[:, slot, :].rearrange("p (kt n) -> p kt n", kt=FT)
                pe.wait_ge(free["ffd"], k + 1)
                m = mm_tile(pe, u % 3, lambda kt: w[:, kt, :], lambda kt, lo, hi: hid_f[:, kt, lo:hi], FT)
                m.then_inc(tiles_done, 1)
            slabs(pe, 8, ffd)
            if upto < 5: return
            norm(2)

            pe.wait_ge(xm_ready, 3)

            def rkvp(k, u, slot):
                w = ring[:, slot, 0:KT * 256].rearrange("p (kt n) -> p kt n", kt=KT)
                for t in range(2):
                    pe.wait_ge(free["rkv"], k * 2 + (t + 1))
                    m = mm_tile(pe, (2 * u + t) % 3, lambda kt: w[:, kt, t * P:(t + 1) * P],
                                lambda kt, lo, hi: xm[u][:, kt, lo:hi], KT)
                    m.then_inc(tiles_done, 1)
            slabs(pe, 12, rkvp)
            pe.wait_ge(xm_ready, 6)

            def lora(k, u, slot):
                w = ring[:, slot, 0:KT * 256].rearrange("p (kt n) -> p kt n", kt=KT)
                for t in range(2):
                    if 2 * k + t > 2:
                        break
                    pe.wait_ge(free["lora"], 2 * k + t + 1)
                    m = mm_tile(pe, 2 * k + t, lambda kt: w[:, kt, t * P:(t + 1) * P],
                                lambda kt, lo, hi: xm[2 * k + t][:, kt, lo:hi], KT)
                    m.then_inc(tiles_done, 1)
            slabs(pe, 2, lora)
            if upto < 6: return
            pe.wait_ge(free["lora"], 3 + 3)
            pe.wait_ge(zero_set, 6)
            pe.sem_inc(rpe.sem, len(rpe.names))
            with pe.Fori(0, KT) as j:
                J = j + 1
                rdve.wait(pe, "yg", j)
                ract.wait(pe, "std", j)
                wide = lambda b: psf[:, b * 512:b * 512 + TOK]

                def two(b, lhsT, rhs):
                    for lo, hi in HALVES:
                        m = pe.matmul(wide(b)[:, lo:hi], lhsT, rhs[:, lo:hi], start=True, stop=True)
                    return m
                rdve.wait(pe, "sq", J)
                rpe.done(two(0, cst("headones"), T[1]), "knorm")
                pe.wait_ge(rkv_in[0], j * 48 + 48)
                rpe.done(two(2, l2[:, 2], lhid[:, 2]), "gate")

                def lora2(d):
                    dd = slice(64 * d, 64 * d + 64)
                    rpe.done(two(4, l2[dd, 0], lhid[dd, 0]), f"w{d}")
                    rpe.done(two(6, l2[dd, 1], lhid[dd, 1]), f"a{d}")
                lora2(0)

                def tr(src, b0, label, before):
                    for g, (c0, c1) in enumerate(GR):
                        before(g)
                        for c in range(c0, c1):
                            m = pe.transpose(PS[:, b0 + g, (c - c0) * P:(c - c0 + 1) * P], src[:, c], cst("ident"))
                        rpe.done(m, f"{label}{g}")
                for d in range(2):
                    if d:
                        rdve.wait(pe, "Arb04", J)
                        lora2(1)
                    else:
                        rdve.wait(pe, "vT1", J)
                        ract.wait(pe, "knorm", J)
                        tr(BY[1], 0, "V", lambda g: ract.wait(pe, "gate", J) if g == 2 else None)
                    rdve.wait(pe, f"B1{d}", J)
                    tr(KX[d], 0, f"Kt{d}", lambda g: ract.wait(pe, f"V{g}", J) if d == 0 else
                       rdve.wait(pe, "Arb04", J))
                    ract.wait(pe, f"tha{d}", J)
                    if d:
                        pass
                    tr(BY[d], 3, f"Bt{d}", lambda g: None)
                    for nm, src, banks in (("GK", KX[d], (6, 7, 0, 1, 2)), ("GB", BY[d], (3, 4, 5, 6, 7))):
                        for q in range(5):
                            b = banks[q]
                            if nm == "GK" and b < 3:
                                ract.wait(pe, f"Kt{d}{b}", J)
                            if nm == "GB" and b < 6:
                                ract.wait(pe, f"Bt{d}{b-3}", J)
                            if nm == "GB" and b >= 6:
                                rdve.wait(pe, f"Ark{d}{b-6}", J)
                            for i in range(2):
                                c = 2 * q + i
                                m = pe.matmul(PS[:, b, i * 192:(i + 1) * 192], src[:, c], QR[d][:, c, :], start=True, stop=True)
                            rpe.done(m, f"{nm}{d}{q}")
                rdve.wait(pe, "rkk", J)
                rdve.wait(pe, "Ark13", J)
                rpe.done(two(0, cst("headones"), T[5]), "bonus")
                for n, lv in enumerate(LEVELS):
                    for ph in ("X", "Y", "Z"):
                        for d in range(2):
                            for g, (c0, c1) in enumerate(GR):
                                b = d * 3 + g
                                if ph == "X":
                                    if n == 0:
                                        rdve.wait(pe, f"XT2{d}", J)
                                        rdve.wait(pe, "y0", J)
                                    else:
                                        rdve.wait(pe, f"Z{LEVELS[n-1]}{d}{g}", J)
                                elif ph == "Y":
                                    ract.wait(pe, f"X{lv}{d}{g}", J)
                                else:
                                    rdve.wait(pe, f"Y{lv}{d}{g}", J)
                                for c in range(c0, c1):
                                    o = PS[:, b, (c - c0) * P:(c - c0 + 1) * P]
                                    if ph == "X":
                                        m = pe.transpose(o, XT[d][:, c], cst("ident"))
                                    elif ph == "Y":
                                        m = pe.matmul(o, LT[d][:, c], KX[d][:, c], start=True, stop=True)
                                    else:
                                        m = pe.matmul(o, BY[d][:, c], XT[d][:, c], start=True, stop=True)
                                rpe.done(m, f"{ph}{lv}{d}{g}")
                for d in range(2):
                    for g in range(3):
                        ract.wait(pe, f"Z64{d}{g}", J)
                for t in range(8):
                    for i in chain_steps(t):
                        d, cs = CHAINS[i]
                        eng = ract if d else rdve
                        if t:
                            eng.wait(pe, f"S{t-1}{i}", J)
                        o = PS[:, i, 0:P]
                        pe.matmul(o, MkT[d][:, cs[t]], Vbd[:, cs[t]], start=True, stop=False)
                        rpe.done(pe.matmul(o, QR[d][:, cs[t], 0:P], St[:, i], start=False, stop=True), f"rhs{t}{i}")
                    for i in chain_steps(t):
                        d, cs = CHAINS[i]
                        (ract if d else rdve).wait(pe, f"rhs{t}{i}", J)
                        rpe.done(pe.matmul(PS[:, i, 0:P], XT[d][:, cs[t]], RU[:, i], start=True, stop=True), f"U{t}{i}")
                    for i in chain_steps(t):
                        d, cs = CHAINS[i]
                        c = cs[t]
                        if t:
                            rdve.wait(pe, f"y{t-1}{i}", J)
                        elif i < 2:
                            pass
                        yo, so = PS[:, 4 + i, 0:HD], PS[:, 4 + i, 128:256]
                        pe.matmul(yo, Vbd[:, c], Ark[d][:, c], start=True, stop=False)
                        pe.matmul(yo, St[:, i], QR[d][:, c, P:192], start=False, stop=False)
                        (ract if d else rdve).wait(pe, f"U{t}{i}", J)
                        pe.matmul(yo, RU[:, i], Arb[d][:, c], start=False, stop=True)
                        pe.matmul(so, cst("ident"), St[:, i], start=True, stop=False)
                        pe.matmul(so, Ktok[d][:, c], Vbd[:, c], start=False, stop=False)
                        rpe.done(pe.matmul(so, Btok[d][:, c], RU[:, i], start=False, stop=True), f"S{t}{i}")
                rdve.wait(pe, "y71", J)
                rpe.done(two(0, cst("headmean"), T[4]), "mean")
                rdve.wait(pe, "ysq", J)
                rpe.done(two(2, cst("headmean"), T[3]), "var")
                rpe.next = 0
            rdve.wait(pe, "yg", KT)
            dense8(4, gk, "rout")
            if upto < 7: return
            norm(3)
            pe.wait_ge(norm_done, 64)
            pe.wait_ge(free["rout"], 3 + 8)
            for c in range(CH):
                for kt in range(KT):
                    m = pe.matmul(psf[:, c * NE:(c + 1) * NE], hn2[:, kt, c * P:(c + 1) * P], wrouter[:, kt, :],
                                  start=kt == 0, stop=kt == KT - 1)
            m.then_inc(logits_full, 1)
            pe.wait_ge(comb_ready, 1)
            for e in range(NE):
                pe.wait_ge(free["cb"], e + 1)
                for c in range(CH):
                    m = pe.matmul(acc(e % 3)[:, c * P:(c + 1) * P], comb_w[:, c, e:e + 1].to_broadcast([P, P]), cst("ident"),
                                  start=True, stop=True)
                m.then_inc(cb_full, 1)
            pe.wait_ge(free["cb"], 3 + NE)
            n0 = slab_n["pe"]
            with pe.Fori(0, NE) as e:
                for k in range(15):
                    slot = (n0 + k) % RING
                    pe.wait_ge(slab_ready[slot], e * 80 + 16 * ((n0 + k) // RING + 1))
                    if k < ET:
                        w = ring[:, slot, 0:KT * 256].rearrange("p (kt n) -> p kt n", kt=KT)
                    else:
                        w = ring[:, slot, :].rearrange("p (kt n) -> p kt n", kt=ET)
                    for t in range(2):
                        tile = 2 * k + t
                        a = tile % 3
                        if k < ET:
                            if tile < 3:
                                pe.wait_ge(free["moed"], e * 8 + (1 + tile))
                            elif tile % 2 == 0:
                                pe.wait_ge(free["moeu"], e * ET + (tile - 4) // 2 + 1)
                            else:
                                pe.wait_ge(free["moeg"], e * ET + (tile - 3) // 2 + 1)
                            m = mm_tile(pe, a, lambda kt: w[:, kt, t * P:(t + 1) * P], lambda kt, lo, hi: hn2[:, kt, lo:hi], KT)
                        else:
                            o = tile - 2 * ET
                            last = None
                            if o == 1:
                                pe.wait_ge(free["moeg"], e * ET + ET)
                            elif o < 3:
                                pe.wait_ge(free["moeu"], e * ET + (tile - 4) // 2 + 1)
                            if o == 0:
                                pe.wait_ge(hid_ready, e * ET + ET - 1)
                            if o >= 3:
                                pe.wait_ge(free["moed"], e * 8 + (o + 1))
                            if o == 0:
                                last = lambda: pe.wait_ge(hid_ready, e * ET + ET)
                            m = mm_tile(pe, a, lambda kt: w[:, kt, t * P:(t + 1) * P], lambda kt, lo, hi: hid[:, kt, lo:hi], ET, last)
                        m.then_inc(tiles_done, 1)
            norm(4)

        @block.scalar
        def _(act):
            act.wait_ge(loaded, 64)
            act.activation(scond[:].rearrange("p a b -> p (a b)"), vcol("cond", 0, 2 * KT), ACT.Silu).then_inc(cond_ready, 1)

            def norm_a(n, buf):
                for kt in range(KT):
                    act.activation(buf[:, kt], x[:, kt], ACT.Square).then_inc(norm_sq, 1)
                act.wait_ge(norm_sum, n + 1)
                act.activation(rstd[:], stats, ACT.Sqrt, bias=cst("eps"), scale=1.0 / D).then_inc(norm_std, 1)

            def norm_b(n, buf, layer, which):
                for kt in range(KT):
                    act.wait_ge(norm_x, 8 * n + kt + 1)
                    for s, (lo, hi) in enumerate(HALVES):
                        act.activation(buf[:, kt, lo:hi], buf[:, kt, lo:hi], ACT.Identity,
                                       bias=mods[:, layer, 3 * which, kt, s:s + 1],
                                       scale=gs[:, layer, which, kt, s:s + 1]).then_inc(norm_done, 1)

            if upto < 2: return
            norm_a(0, hn)
            act.wait_ge(mods_ready, 1)
            norm_b(0, hn, 0, 0)
            act.sem_inc(free["in"], 3)

            def one(k, u):
                for t in range(2):
                    n = 2 * k + t if isinstance(k, int) else k * 2 + t
                    tile_done(act, "in", n)
                    zz = z[:, n] if isinstance(n, int) else z[:, bass.ds(n, 1)].rearrange("p a n -> p (a n)")
                    a0 = CONST["in_scale"][0]
                    sc = const[:, a0 + n:a0 + n + 1] if isinstance(n, int) else const[:, bass.ds(n + a0, 1)]
                    act.activation(zz, acc((2 * u + t) % 3), ACT.Identity, bias=b_in_col(n), scale=sc).then_inc(free["in"], 1)

            def b_in_col(n):
                return bs_in[:, n:n + 1] if isinstance(n, int) else bs_in[:, bass.ds(n, 1)]
            repeat(act, 13, one)
            if upto < 3: return
            act.wait_ge(free["in"], 3 + IN_TILES)
            for n, (c, kind) in enumerate(VK):
                mpe.wait(act, f"T{c}{kind}")
                dst = ktok[:, c] if kind == "k" else vaug[:, c, 4 * int(kind[1]):4 * int(kind[1]) + 4, 0:DV]
                src = PS[:, n % 6, :] if kind == "k" else PS[:, n % 6, :].rearrange("p (h n) -> p h n", h=4)
                mact.done(act.activation(dst, src, ACT.Copy), f"T{c}{kind}")
            R = slice(0, 64)
            mact.done(act.activation(tmp_row[R], gf[R], ACT.Abs), "absf")
            mact.wait(act, "absf")
            mact.done(act.activation(tmp_row[R], tmp_row[R], ACT.Exp, scale=-1.0), "expf")
            mact.wait(act, "expf")
            mact.done(act.activation(tmp_row[R], tmp_row[R], ACT.Ln, bias=1.0), "lnf")
            mdve.wait(act, "m11")
            mdve.wait(act, "g")
            mact.done(act.activation(gi[R], gf[R], ACT.Exp, scale=-1.0), "em")
            mdve.wait(act, "gend1")
            for c in range(CH):
                mact.done(act.activation(winter_r[R, c * P:(c + 1) * P], negG[R, c * P:(c + 1) * P], ACT.Exp,
                                         bias=mprev[R, c:c + 1]), f"winter{c}")
            for c in range(CH):
                mact.done(act.activation(ws_r[R, c * P:(c + 1) * P], g_row[R, c * P:(c + 1) * P], ACT.Exp,
                                         bias=gend[R, c:c + 1]), f"ws{c}")
            mact.done(act.activation(dec[R], dec[R], ACT.Exp), "dec")
            for n, (d, c) in enumerate(MGRP):
                for g in range(2):
                    mpe.wait(act, f"D{n}{g}")
                    if n:
                        mpe.wait(act, f"num{n-1}{g}")
                    mact.done(act.activation(Wt[:, g].rearrange("p h n -> p (h n)"), PS[:, 0, :], ACT.Exp), f"W{n}{g}")
            mact.done(act.activation(o_.rearrange("p a n -> p (a n)"), o_.rearrange("p a n -> p (a n)"), ACT.Sigmoid), "sigo")
            for c in range(CH):
                mdve.wait(act, f"ms{c}")
                mact.done(act.activation(ms, ms, ACT.Sqrt, bias=cst("eps"), scale=1.0 / DV), f"sd{c}")
            if upto < 4: return
            act.wait_ge(free["mout"], 3 + 8)
            act.wait_ge(states_out, 1)
            norm_a(1, hn_f)
            norm_b(1, hn_f, 0, 1)
            act.sem_inc(free["ffg"], 1)

            def ffg(k, u):
                tile_done(act, "ff", k * 2)
                act.activation(sg_f[:, u], acc((2 * u) % 3), ACT.Silu).then_inc(free["ffg"], 1)
            repeat(act, FT, ffg)
            if upto < 5: return
            act.wait_ge(free["ffd"], 3 + 8)
            norm_a(2, hn1)
            norm_b(2, hn1, 1, 0)
            act.sem_inc(free["rkv"], 3)

            def rk(i):
                for m in range(6):
                    t = i * 6 + m
                    u, w = m // 2, m % 2
                    tile_done(act, "rkv", t)
                    act.wait_ge(stored[m % 3], i * 32 + 16 * (m // 3 + 1))
                    act.activation(stage[:, m % 3], acc(m % 3), ACT.Copy).then_inc(free["rkv"], 1)
                    act.wait_ge(free["rkv"], t + (1 + 3))
                    act.dma_start(A["rkv_s"][bass.ds(i * 2 + w, 1), :, u, :].rearrange("a p n -> p (a n)"),
                                  stage[:, m % 3]).then_inc(stored[m % 3], 16)
            for s in stored:
                act.sem_inc(s, 16)
            with act.Fori(0, 4) as i:
                rk(i)
            act.sem_inc(free["lora"], 3)
            for t, fn in enumerate((ACT.Tanh, ACT.Copy, ACT.Sigmoid)):
                tile_done(act, "lora", t)
                act.activation(lhid[:, t], acc(t), fn).then_inc(free["lora"], 1)
            if upto < 6: return
            act.sem_inc(ract.sem, len(ract.names))
            with act.Fori(0, KT) as j:
                J = j + 1
                wide = lambda b: psf[:, b * 512:b * 512 + TOK]
                col = lambda t, k0: t[:, bass.ds(j + k0, 1)]
                rdve.wait(act, "yg", j)
                rpe.wait(act, "gate", J)
                ract.done(act.activation(T[2], wide(2), ACT.Copy), "gate")
                rpe.wait(act, "knorm", J)
                ract.done(act.activation(T[1], wide(0), ACT.Sqrt), "knorm")

                def th(d):
                    rpe.wait(act, f"w{d}", J)
                    if d:
                        rdve.wait(act, "ce0", J)
                        rdve.wait(act, "B10", J)
                    ract.done(act.activation(T[5], wide(4), ACT.Tanh, bias=col(w0h, d * KT), scale=0.5), f"thw{d}")
                    rpe.wait(act, f"a{d}", J)
                    ract.done(act.activation(T[8], wide(6), ACT.Tanh, bias=col(w0h, 2 * KT + d * KT), scale=0.5), f"tha{d}")
                th(0)
                for d in range(2):
                    if d:
                        th(1)
                    rdve.wait(act, f"ce{d}", J)
                    ract.done(act.activation(T[5], T[6], ACT.Exp), f"e1{d}")
                    ract.done(act.activation(T[6], T[6], ACT.Exp, scale=-1.0), f"e2{d}")
                    ract.done(act.activation(T[7], T[7], ACT.Exp), f"e3{d}")
                    ract.wait(act, f"e1{d}", J)
                    e1c = T[5].rearrange("p (c n) -> p c n", c=C64)
                    k = 63 if d == 0 else 0
                    ract.done(act.activation(pend[:, d].unsqueeze(2), e1c[:, :, k:k + 1], ACT.Copy), f"pend{d}")
                    if d == 0:
                        for g, (c0, c1) in enumerate(GR):
                            rpe.wait(act, f"V{g}", J)
                            ract.done(act.activation(Vbd[:, c0:c1].rearrange("p c n -> p (c n)"), PS[:, g, 0:(c1 - c0) * P], ACT.Copy), f"V{g}")
                    for nm, dst, b0 in (("Kt", Ktok[d], 0), ("Bt", Btok[d], 3)):
                        for g, (c0, c1) in enumerate(GR):
                            rpe.wait(act, f"{nm}{d}{g}", J)
                            ract.done(act.activation(dst[:, c0:c1].rearrange("p c n -> p (c n)"), PS[:, b0 + g, 0:(c1 - c0) * P], ACT.Copy),
                                      f"{nm}{d}{g}")
                for lv in LEVELS:
                    for d in range(2):
                        for g, (c0, c1) in enumerate(GR):
                            rpe.wait(act, f"X{lv}{d}{g}", J)
                            ract.done(act.activation(KX[d][:, c0:c1].rearrange("p c n -> p (c n)"),
                                                     PS[:, d * 3 + g, 0:(c1 - c0) * P], ACT.Copy), f"X{lv}{d}{g}")
                    if lv == 64:
                        for d in range(2):
                            for g, (c0, c1) in enumerate(GR):
                                rpe.wait(act, f"Z64{d}{g}", J)
                                ract.done(act.activation(XT[d][:, c0:c1].rearrange("p c n -> p (c n)"),
                                                         PS[:, d * 3 + g, 0:(c1 - c0) * P], ACT.Copy), f"Z64{d}{g}")
                for t in range(8):
                    mine = [i for i in chain_steps(t) if CHAINS[i][0]]
                    for i in mine:
                        rpe.wait(act, f"rhs{t}{i}", J)
                        ract.done(act.activation(RU[:, i], PS[:, i, 0:P], ACT.Copy), f"rhs{t}{i}")
                    for i in mine:
                        rpe.wait(act, f"U{t}{i}", J)
                        ract.done(act.activation(RU[:, i], PS[:, i, 0:P], ACT.Copy, scale=-1.0), f"U{t}{i}")
                    for i in mine:
                        c = CHAINS[i][1][t]
                        rpe.wait(act, f"S{t}{i}", J)
                        ract.done(act.activation(St[:, i], PS[:, 4 + i, 128:256], ACT.Copy, scale=pend[:, 1, c:c + 1]), f"S{t}{i}")
                rpe.wait(act, "var", J)
                ract.done(act.activation(T[5], wide(2), ACT.Sqrt, bias=cst("ln_eps")), "std")
                ract.next = 0
            if upto < 7: return
            act.wait_ge(free["rout"], 3 + 8)
            norm_a(3, hn2)
            norm_b(3, hn2, 1, 1)
            act.wait_ge(exp_in, 1)
            act.activation(e12, e12, ACT.Exp).then_inc(exp_done, 1)
            act.sem_inc(free["cb"], 3)
            for e in range(NE):
                act.wait_ge(cb_full, e + 1)
                act.activation(cb[:, e], acc(e % 3), ACT.Copy).then_inc(free["cb"], 1)
            with act.Fori(0, NE) as e:
                for f in range(ET):
                    tile_done(act, "moe", e * 30 + 2 * f)
                    act.activation(sg[:, f % RING], acc((2 * f) % 3), ACT.Silu).then_inc(free["moeg"], 1)
            act.wait_ge(free["moed"], 3 + 8 * NE)
            for kt in range(KT):
                act.activation(hn2[:, kt], x[:, kt], ACT.Square).then_inc(norm_sq, 1)
            act.wait_ge(norm_sum, 5)
            act.activation(rstd[:], stats, ACT.Sqrt, bias=cst("eps"), scale=1.0 / D).then_inc(norm_std, 1)

        @block.vector
        def _(dve):
            n_chain = [0]

            def link(ins):
                n_chain[0] += 1
                ins.then_inc(dve_chain, 1)
                dve.wait_ge(dve_chain, n_chain[0])

            dve.wait_ge(loaded, 64)
            link(dve.tensor_scalar(w0h[:], vcol("w0", 0, 4 * KT), 0.5, None, ALU.mult))
            link(dve.tensor_scalar(omka[:], vcol("k_a", 0, KT), -1.0, 1.0, ALU.mult, ALU.add))
            a0 = CONST["in_scale"][0]
            link(dve.tensor_tensor(bs_in[:], vcol("b_in", 0, IN_TILES), const[:, a0:a0 + IN_TILES], ALU.mult))
            tile_done(dve, "ada", 95)
            mf = mods[:].rearrange("p l k t s -> p (l k t) s")
            link(dve.tensor_tensor(mf, psf[:, 0:192].rearrange("p (n s) -> p n s", s=2),
                                   vcol("b_ada", 0, 96).unsqueeze(2).to_broadcast([P, 96, 2]), ALU.add))
            for la in range(2):
                for w in range(2):
                    g = vcol("gn1" if w == 0 else "gn2", la * KT, KT)
                    link(dve.tensor_scalar(gs[:, la, w], mods[:, la, 3 * w + 1], 1.0, None, ALU.add))
                    link(dve.tensor_tensor(gs[:, la, w], gs[:, la, w], g.unsqueeze(2).to_broadcast([P, KT, 2]), ALU.mult))
            dve.sem_inc(mods_ready, 1)

            def norm_v(n, buf):
                dve.wait_ge(norm_std, n + 1)
                dve.reciprocal(rstd[:], rstd[:]).then_inc(norm_rstd, 1)
                dve.wait_ge(norm_rstd, n + 1)
                for kt in range(KT):
                    dve.tensor_tensor(buf[:, kt], x[:, kt], rstd[:], ALU.mult).then_inc(norm_x, 1)

            def residual(name, a, t, layer, kind, n):
                tile_done(dve, name, n)
                for s, (lo, hi) in enumerate(HALVES):
                    xs = x[:, t, lo:hi] if isinstance(t, int) else x[:, bass.ds(t, 1), lo:hi].rearrange("p a n -> p (a n)")
                    if isinstance(t, int):
                        ga = mods[:, layer, kind, t, s:s + 1]
                    else:
                        ga = mods[:].rearrange("p l k t s -> p (l k t s)")[:, bass.ds(t * 2 + ((layer * NADA + kind) * KT * 2 + s), 1)]
                    i = dve.scalar_tensor_tensor(out=xs, in0=acc(a)[:, lo:hi], scalar=ga, in1=xs, op0=ALU.mult, op1=ALU.add)
                return i

            if upto < 2: return
            norm_v(0, hn)
            if upto < 3: return
            dve.wait_ge(free["in"], 3 + IN_TILES)
            R = slice(0, 64)
            Z0, Z1 = slice(0, 32), slice(32, 64)
            mact.wait(dve, "lnf")
            mdve.done(dve.tensor_scalar(gf[R], gf[R], 0.0, None, ALU.min), "minf")
            mdve.wait(dve, "minf")
            mdve.done(dve.tensor_tensor(gf[R], gf[R], tmp_row[R], ALU.subtract), "lf")
            mdve.wait(dve, "lf")
            mr = cst("mreset")
            mdve.done(dve.tensor_tensor_scan(b_row[Z0], mr[Z0, 0:TOK], gf[Z0], 0.0, ALU.mult, ALU.add), "b0")
            mdve.done(dve.tensor_tensor_scan(b_row[Z1][:, ::-1], mr[Z1, 1:TOK + 1][:, ::-1], gf[Z1][:, ::-1], 0.0, ALU.mult, ALU.add), "b1")
            mdve.wait(dve, "b1")
            mdve.done(dve.tensor_tensor(g_row[R], gi[R], b_row[R], ALU.subtract), "g")
            m0 = vcol("m0", 0)
            Ls, Cs = slice(0, LAT), slice(LAT, TOK)
            mdve.done(dve.tensor_tensor_scan(gm[Z0, Ls], gf[Z0, Ls], gi[Z0, Ls], m0[Z0], ALU.add, ALU.max), "m00")
            mdve.done(dve.tensor_tensor_scan(gm[Z1, Ls][:, ::-1], gf[Z1, Ls][:, ::-1], gi[Z1, Ls][:, ::-1], m0[Z1], ALU.add, ALU.max), "m01")
            mdve.done(dve.tensor_tensor_scan(gm[Z0, Cs], gf[Z0, Cs], gi[Z0, Cs], 0.0, ALU.add, ALU.max), "m10")
            mdve.done(dve.tensor_tensor_scan(gm[Z1, Cs][:, ::-1], gf[Z1, Cs][:, ::-1], gi[Z1, Cs][:, ::-1], 0.0, ALU.add, ALU.max), "m11")
            mdve.wait(dve, "m11")
            mdve.done(dve.tensor_tensor(negG[R], b_row[R], gm[R], ALU.subtract), "negG")
            mdve.wait(dve, "negG")
            mch = gm[:, 0:TOK].rearrange("p (c n) -> p c n", c=CH)
            gch = negG[:, 0:TOK].rearrange("p (c n) -> p c n", c=CH)
            mp = mprev.unsqueeze(2)
            mdve.done(dve.tensor_copy(mp[Z0, 1:4], mch[Z0, 0:3, P - 1:P]), "mprev0")
            mdve.done(dve.tensor_copy(mp[Z1, 0:3], mch[Z1, 1:4, 0:1]), "mprev1")
            mdve.done(dve.tensor_copy(mprev[Z0, 0:1], m0[Z0]), "mprev2")
            mdve.done(dve.tensor_copy(mprev[Z1, 3:4], m0[Z1]), "mprev3")
            mdve.done(dve.memset(mprev[R, 4:5], 0.0), "mprev4")
            mdve.done(dve.tensor_copy(gend.unsqueeze(2)[Z0], gch[Z0, :, P - 1:P]), "mprev5")
            mdve.done(dve.tensor_copy(gend.unsqueeze(2)[Z1], gch[Z1, :, 0:1]), "gend0")
            mdve.wait(dve, "gend0")
            mdve.done(dve.tensor_tensor(dec[R], mprev[R], gend[R], ALU.add), "gend1")
            mact.wait(dve, "dec")
            mdve.done(dve.tensor_tensor(decx[R], cst("ident")[R, 0:64].unsqueeze(1).to_broadcast([64, CH, 64]),
                                        dec[R].unsqueeze(2).to_broadcast([64, CH, 64]), ALU.mult), "decx")
            cw = colw.rearrange("p c k r -> p (c k r)")
            mpe.wait(dve, "cols0")
            mdve.done(dve.tensor_copy(cw[:, 0:512], PS[:, 6, :]), "cols0")
            mpe.wait(dve, "cols1")
            mdve.done(dve.tensor_copy(cw[:, 512:960], PS[:, 7, 0:448]), "cols1")
            mpe.wait(dve, "decb")
            pd = PS[:, 0, 0:CH * 64].rearrange("p (c r) -> p c r", c=CH)
            n = 0
            for half in range(2):
                for d in range(2):
                    hp = slice(64 * half, 64 * half + 64)
                    mdve.done(dve.tensor_copy(decp[hp, :, d, :], pd[hp, :, d * 32 + half:d * 32 + half + 7:2]), f"decp{n}")
                    n += 1
            seen = set()
            for n, (d, c) in enumerate(MGRP):
                seq = 0 if c < 4 else 1
                for g in range(2):
                    mpe.wait(dve, f"S{n}{g}")
                    mact.wait(dve, f"W{n}{g}")
                    wf = Wt[:, g].rearrange("p h n -> p (h n)")
                    mdve.done(dve.tensor_tensor(wf, wf, PS[:, 1, :], ALU.mult), f"P{n}{g}")
                    mpe.wait(dve, f"num{n}{g}")
                    if n or g:
                        mdve.wait(dve, f"h{n}0" if g else f"h{n-1}1")
                    for h in range(4):
                        o = slice((h % 2) * 129, (h % 2) * 129 + 129)
                        row = d * 32 + 2 * h + g
                        i = dve.tensor_scalar(comb[:, h, :], PS[:, 4 + h // 2, o], colw[:, c, 0, row:row + 1], None, ALU.mult)
                        if h == 3:
                            i.then_inc(dve_chain, 1)
                            n_chain[0] += 1
                    dve.wait_ge(dve_chain, n_chain[0])
                    for b in range(2):
                        i = dve.tensor_tensor(comb[:, 2 * b:2 * b + 2, :], comb[:, 2 * b:2 * b + 2, :],
                                              PS[:, 2 + b, 0:258].rearrange("p (h n) -> p h n", h=2), ALU.add)
                    mdve.done(i, f"comb{n}{g}")
                    mdve.wait(dve, f"comb{n}{g}")
                    em = colw[:, c, 2, d * 32 + g:d * 32 + AH:2]
                    dn = comb[:, :, DV:DV + 1]
                    mdve.done(dve.scalar_tensor_tensor(out=rden.unsqueeze(2), in0=dn, scalar=-1.0, in1=dn,
                                                       op0=ALU.mult, op1=ALU.max), f"absd{n}{g}")
                    mdve.wait(dve, f"absd{n}{g}")
                    mdve.done(dve.tensor_tensor(rden, rden, em, ALU.max), f"den{n}{g}")
                    mdve.wait(dve, f"den{n}{g}")
                    mdve.done(dve.reciprocal(rden, rden), f"rden{n}{g}")
                    mdve.wait(dve, f"rden{n}{g}")
                    for h in range(4):
                        o = hs_t[:, c, (2 * h + g) * DV:(2 * h + g + 1) * DV]
                        if (c, g) in seen:
                            i = dve.scalar_tensor_tensor(out=o, in0=comb[:, h, 0:DV], scalar=rden[:, h:h + 1], in1=o,
                                                         op0=ALU.mult, op1=ALU.add)
                        else:
                            i = dve.tensor_scalar(o, comb[:, h, 0:DV], rden[:, h:h + 1], None, ALU.mult)
                    seen.add((c, g))
                    mdve.done(i, f"h{n}{g}")
                mpe.wait(dve, f"C{n}")
                for pair in range(4):
                    s = Cst[:, d, seq, pair * 129:(pair + 1) * 129]
                    i = dve.scalar_tensor_tensor(out=s, in0=s, scalar=decp[:, c, d, pair:pair + 1],
                                                 in1=PS[:, 6 + pair // 2, (pair % 2) * 129:(pair % 2) * 129 + 129],
                                                 op0=ALU.mult, op1=ALU.add)
                mdve.done(i, f"C{n}")
            for c in range(CH):
                mpool.wait(dve, f"sq{c}")
                if c:
                    mdve.wait(dve, f"hn{c-1}")
                mdve.done(dve.tensor_reduce(ms, sqt, AX.X, ALU.add), f"ms{c}")
                mact.wait(dve, f"sd{c}")
                mdve.done(dve.reciprocal(rs, ms), f"rs{c}")
                mdve.wait(dve, f"rs{c}")
                hh = hs_t[:, c].rearrange("p (h n) -> p h n", h=AH)
                mdve.done(dve.tensor_tensor(hh, hh, rs.unsqueeze(2).to_broadcast([P, AH, DV]), ALU.mult), f"hn{c}")
            mact.wait(dve, "sigo")
            for h in range(AH):
                mpe.wait(dve, f"hT{h}")
                mdve.done(dve.scalar_tensor_tensor(out=o_[:, h], in0=acc(h % 3), scalar=vcol("g_head", h), in1=o_[:, h],
                                                   op0=ALU.mult, op1=ALU.mult), f"mo{h}")
            dve.sem_inc(free["mout"], 3)
            for t in range(8):
                residual("mout", t % 3, t, 0, 2, t).then_inc(free["mout"], 1)
            if upto < 4: return
            norm_v(1, hn_f)
            dve.sem_inc(free["ffu"], 2)

            def ffu(k, u):
                tile_done(dve, "ff", k * 2 + 1)
                dve.wait_ge(free["ffg"], k + 2)
                h = hid_f[:, k] if isinstance(k, int) else hid_f[:, bass.ds(k, 1)].rearrange("p a n -> p (a n)")
                dve.tensor_tensor(h, sg_f[:, u], acc((2 * u + 1) % 3), ALU.mult).then_inc(free["ffu"], 1)
            repeat(dve, FT, ffu)
            dve.sem_inc(free["ffd"], 3)
            repeat(dve, 8, lambda k, u: residual("ffd", u % 3, k, 0, 5, k).then_inc(free["ffd"], 1))
            if upto < 5: return
            norm_v(2, hn1)
            dve.wait_ge(norm_done, 48)

            def grid(a, k0):
                return a[:, k0:k0 + 2, 0:LAT].rearrange("p k (r w) -> p k r w", w=64)
            sub, neg = [], []
            h0, s0 = grid(hn1, 0), grid(xx, 0)
            sub.append((s0[:, :, :, 1:], h0[:, :, :, :-1], h0[:, :, :, 1:])); neg.append((s0[:, :, :, 0:1], h0[:, :, :, 0:1]))
            h0, s0 = grid(hn1, 2), grid(xx, 2)
            sub.append((s0[:, :, :, :-1], h0[:, :, :, 1:], h0[:, :, :, :-1])); neg.append((s0[:, :, :, 63:64], h0[:, :, :, 63:64]))
            sub.append((xx[:, 4:6, 64:LAT], hn1[:, 4:6, 0:LAT - 64], hn1[:, 4:6, 64:LAT])); neg.append((xx[:, 4:6, 0:64], hn1[:, 4:6, 0:64]))
            sub.append((xx[:, 6:8, 0:LAT - 64], hn1[:, 6:8, 64:LAT], hn1[:, 6:8, 0:LAT - 64]))
            neg.append((xx[:, 6:8, LAT - 64:LAT], hn1[:, 6:8, LAT - 64:LAT]))
            sub.append((xx[:, 0:4, LAT + 1:TOK], hn1[:, 0:4, LAT:TOK - 1], hn1[:, 0:4, LAT + 1:TOK]))
            neg.append((xx[:, 0:4, LAT:LAT + 1], hn1[:, 0:4, LAT:LAT + 1]))
            sub.append((xx[:, 4:8, LAT:TOK - 1], hn1[:, 4:8, LAT + 1:TOK], hn1[:, 4:8, LAT:TOK - 1]))
            neg.append((xx[:, 4:8, TOK - 1:TOK], hn1[:, 4:8, TOK - 1:TOK]))
            for o, a, b in sub:
                dve.tensor_tensor(o, a, b, ALU.subtract).then_inc(xx_ready, 1)
            for o, a in neg:
                dve.tensor_scalar(o, a, -1.0, None, ALU.mult).then_inc(xx_ready, 1)
            dve.wait_ge(xx_ready, 12)
            for s in range(6):
                if s == 3:
                    tile_done(dve, "rkv", 23)
                for kt in range(KT):
                    i = dve.scalar_tensor_tensor(out=xm[s % 3][:, kt], in0=xx[:, kt], scalar=vcol("mu", s * KT + kt),
                                                 in1=hn1[:, kt], op0=ALU.mult, op1=ALU.add)
                i.then_inc(xm_ready, 1)
            if upto < 6: return
            dve.wait_ge(zero_set, 6)
            tile_done(dve, "lora", 2)
            tile_done(dve, "rkv", 23)
            dve.sem_inc(rdve.sem, len(rdve.names))
            I2 = cst("ident2").unsqueeze(1)
            with dve.Fori(0, KT) as j:
                J = j + 1
                vc = lambda name, k0=0: vec[:, bass.ds(j + (VEC[name][0] + k0), 1)]
                wide = lambda b: psf[:, b * 512:b * 512 + TOK]
                ch = lambda a: a.rearrange("p (c n) -> p c n", c=C64)
                W = lambda name, lap=J: rdve.wait(dve, name, lap)
                dve.wait_ge(rkv_in[0], j * 48 + 48)
                rr, kr, vv = rkv[:, 0], rkv[:, 1], rkv[:, 2]
                rdve.done(dve.tensor_scalar(T[0], kr, vc("k_k"), None, ALU.mult), "kk0")
                W("kk0")
                rdve.done(dve.tensor_tensor(T[1], T[0], T[0], ALU.mult), "sq")
                for h in range(2):
                    hp = slice(64 * h, 64 * h + 64)
                    rdve.done(dve.tensor_copy(BY[1][hp, :, 64 * h:64 * h + 64], ch(vv)[hp]), f"vT{h}")
                dve.memset(St[:, 2:4], 0.0)
                ract.wait(dve, "knorm", J)
                rdve.done(dve.tensor_scalar(T[1], T[1], 1e-12, None, ALU.max), "kmax")
                W("kmax")
                rdve.done(dve.reciprocal(T[1], T[1]), "krec")
                W("krec")
                rdve.done(dve.tensor_tensor(T[0], T[0], T[1], ALU.mult), "kk")
                for d in range(2):
                    kd = T[3] if d == 0 else T[9]
                    ract.wait(dve, f"tha{d}", J)
                    rdve.done(dve.tensor_scalar(T[5], T[5], -DECAY / 2, -DECAY / 2, ALU.mult, ALU.add), f"lw{d}")
                    W(f"lw{d}")
                    rev = slice(None, None, -1) if d else slice(None)
                    rdve.done(dve.tensor_tensor_scan(T[6][:, rev], cst("reset")[:, d:d + TOK][:, rev], T[5][:, rev], 0.0,
                                                     ALU.mult, ALU.add), f"c{d}")
                    W(f"c{d}")
                    rdve.done(dve.tensor_tensor(T[7], T[6], T[5], ALU.subtract), f"ce{d}")
                    rdve.done(dve.tensor_scalar(T[8], T[8], 0.5, 0.5, ALU.mult, ALU.add), f"a{d}")
                    W(f"a{d}")
                    rdve.done(dve.tensor_scalar(kd, T[8], vc("k_a"), omka[:, bass.ds(j, 1)], ALU.mult, ALU.add), f"f{d}")
                    W(f"f{d}")
                    rdve.done(dve.tensor_tensor(kd, kd, kr, ALU.mult), f"kd{d}")
                    W("kk")
                    rdve.done(dve.tensor_tensor(T[8], T[8], T[0], ALU.mult), f"b{d}")
                    ract.wait(dve, f"e3{d}", J)
                    rdve.done(dve.tensor_tensor(QR[d][:, :, P:192], ch(rr), ch(T[5]), ALU.mult), f"R{d}")
                    W(f"b{d}")
                    if d:
                        rpe.wait(dve, "V2", J)
                    for nm, dst, a, b in (("Q", QR[d], T[0], T[7]), ("K", KX[d], kd, T[6]), ("B", BY[d], T[8], T[6])):
                        for h in range(2):
                            hp = slice(64 * h, 64 * h + 64)
                            rdve.done(dve.tensor_tensor(dst[hp, :, 64 * h:64 * h + 64], ch(a)[hp], ch(b)[hp], ALU.mult), f"{nm}{h}{d}")
                    mst = cst(f"strict{d}").unsqueeze(1).to_broadcast([P, 2, P])
                    minc = cst(f"incl{d}").unsqueeze(1).to_broadcast([P, 2, HD])
                    for nm, M, Ar, banks in (("GK", MkT[d], Ark[d], (6, 7, 0, 1, 2)), ("GB", LT[d], Arb[d], (3, 4, 5, 6, 7))):
                        for q in range(5):
                            rpe.wait(dve, f"{nm}{d}{q}", J)
                            src = PS[:, banks[q], 0:384].rearrange("p (c n) -> p c n", c=2)
                            rdve.done(dve.tensor_tensor(M[:, 2 * q:2 * q + 2], src[:, :, 0:P], mst, ALU.mult),
                                      f"MkT{d}{q}" if nm == "GK" else f"LT{d}{q}")
                            rdve.done(dve.tensor_tensor(Ar[:, 2 * q:2 * q + 2], src[:, :, P:192], minc, ALU.mult),
                                      f"Ark{d}{q}" if nm == "GK" else f"Arb{d}{q}")
                    W(f"LT{d}4")
                    all_i = cst("ident").unsqueeze(1).to_broadcast([P, C64, P])
                    rdve.done(dve.tensor_tensor(LT[d], LT[d], all_i, ALU.add), f"LTI{d}")
                    W(f"LTI{d}")
                    rdve.done(dve.scalar_tensor_tensor(out=XT[d], in0=LT[d], scalar=-1.0,
                                                       in1=cst("bd2").unsqueeze(1).to_broadcast([P, C64, P]),
                                                       op0=ALU.mult, op1=ALU.mult), f"XTa{d}")
                    W(f"XTa{d}")
                    rdve.done(dve.tensor_tensor(XT[d], XT[d], I2.to_broadcast([P, C64, P]), ALU.add), f"XT2{d}")
                rdve.done(dve.tensor_tensor(T[3], T[3], T[9], ALU.add), "kds")
                ract.wait(dve, "pend1", J)
                rdve.done(dve.tensor_scalar(T[5], rr, vc("r_k"), None, ALU.mult), "rk")
                W("rk")
                rdve.done(dve.tensor_tensor(T[5], T[5], T[3], ALU.mult), "rkk")
                rpe.wait(dve, "bonus", J)
                rdve.done(dve.tensor_tensor(T[4], wide(0), vv, ALU.mult), "y0")
                for lv in LEVELS:
                    for d in range(2):
                        for g, (c0, c1) in enumerate(GR):
                            rpe.wait(dve, f"Y{lv}{d}{g}", J)
                            src = PS[:, d * 3 + g, 0:(c1 - c0) * P].rearrange("p (c n) -> p c n", n=P)
                            rdve.done(dve.tensor_tensor(BY[d][:, c0:c1], I2.to_broadcast([P, c1 - c0, P]), src, ALU.subtract), f"Y{lv}{d}{g}")
                    if lv < 64:
                        for d in range(2):
                            for g, (c0, c1) in enumerate(GR):
                                rpe.wait(dve, f"Z{lv}{d}{g}", J)
                                src = PS[:, d * 3 + g, 0:(c1 - c0) * P].rearrange("p (c n) -> p c n", n=P)
                                rdve.done(dve.tensor_tensor(XT[d][:, c0:c1], src, cst(f"bd{lv}").unsqueeze(1).to_broadcast([P, c1 - c0, P]),
                                                            ALU.mult), f"Z{lv}{d}{g}")
                W("y0")
                for t in range(8):
                    mine = [i for i in chain_steps(t) if not CHAINS[i][0]]
                    for i in mine:
                        rpe.wait(dve, f"rhs{t}{i}", J)
                        rdve.done(dve.tensor_copy(RU[:, i], PS[:, i, 0:P]), f"rhs{t}{i}")
                    for i in mine:
                        rpe.wait(dve, f"U{t}{i}", J)
                        rdve.done(dve.tensor_scalar(RU[:, i], PS[:, i, 0:P], -1.0, None, ALU.mult), f"U{t}{i}")
                    for i in chain_steps(t):
                        d, cs = CHAINS[i]
                        c = cs[t]
                        rpe.wait(dve, f"S{t}{i}", J)
                        if d:
                            ract.wait(dve, f"S{t}{i}", J)
                        else:
                            rdve.done(dve.tensor_scalar(St[:, i], PS[:, 4 + i, 128:256], pend[:, 0, c:c + 1], None, ALU.mult), f"S{t}{i}")
                        ys = T[4][:, c * HD:(c + 1) * HD]
                        rdve.done(dve.tensor_tensor(ys, ys, PS[:, 4 + i, 0:HD], ALU.add), f"y{t}{i}")
                    W(f"y{t}{chain_steps(t)[-1]}")
                rpe.wait(dve, "mean", J)
                rdve.done(dve.tensor_tensor(T[1], T[4], wide(0), ALU.subtract), "yc")
                W("yc")
                rdve.done(dve.tensor_tensor(T[3], T[1], T[1], ALU.mult), "ysq")
                ract.wait(dve, "std", J)
                rdve.done(dve.reciprocal(T[5], T[5]), "rv")
                W("rv")
                rdve.done(dve.tensor_tensor(T[1], T[1], T[5], ALU.mult), "yn")
                W("yn")
                rdve.done(dve.tensor_scalar(T[1], T[1], vc("ln_g"), vc("ln_b"), ALU.mult, ALU.add), "yl")
                W("yl")
                rdve.done(dve.tensor_tensor(gk[:, bass.ds(j, 1)].rearrange("p a n -> p (a n)"), T[1], T[2], ALU.mult), "yg")
                W("yg")
                rdve.next = 0
            dve.sem_inc(free["rout"], 3)
            for t in range(8):
                residual("rout", t % 3, t, 1, 2, t).then_inc(free["rout"], 1)
            if upto < 7: return
            norm_v(3, hn2)
            br = vcol("b_router", 0, NE)
            cd = cst("code").unsqueeze(1).to_broadcast([P, CH, NE])
            dve.wait_ge(logits_full, 1)
            link(dve.tensor_tensor(lg, psf[:, 0:CH * NE].rearrange("p (c e) -> p c e", c=CH),
                                   br.unsqueeze(1).to_broadcast([P, CH, NE]), ALU.add))
            wide_ = lambda a: a.unsqueeze(2).to_broadcast([P, CH, NE])

            def top(src, mx, oh):
                link(dve.tensor_reduce(mx, src, AX.X, ALU.max))
                link(dve.tensor_tensor(eq, src, wide_(mx), ALU.is_equal))
                link(dve.tensor_tensor(eq, eq, cd, ALU.mult))
                link(dve.tensor_reduce(e12, eq, AX.X, ALU.max))
                link(dve.tensor_tensor(oh, cd, wide_(e12), ALU.is_equal))
            top(lg, mx1, oh1)
            link(dve.tensor_scalar(l2g, oh1, NEG, None, ALU.mult))
            link(dve.tensor_tensor(l2g, l2g, lg, ALU.add))
            top(l2g, mx2, oh2)
            link(dve.tensor_tensor(e12, mx2, mx1, ALU.subtract))
            dve.sem_inc(exp_in, 1)
            dve.wait_ge(exp_done, 1)
            link(dve.tensor_scalar(p1, e12, 1.0, None, ALU.add))
            link(dve.reciprocal(p1, p1))
            link(dve.tensor_tensor(p2, e12, p1, ALU.mult))
            link(dve.tensor_tensor(oh1, oh1, wide_(p1), ALU.mult))
            link(dve.tensor_tensor(oh2, oh2, wide_(p2), ALU.mult))
            dve.tensor_tensor(comb_w, oh1, oh2, ALU.add).then_inc(comb_ready, 1)
            dve.sem_inc(free["moed"], 3)
            with dve.Fori(0, NE) as e:
                for f in range(ET):
                    tile_done(dve, "moe", e * 30 + (2 * f + 1))
                    dve.wait_ge(free["moeg"], e * ET + (f + 1))
                    dve.tensor_tensor(hid[:, f], sg[:, f % RING], acc((2 * f + 1) % 3), ALU.mult).then_inc(free["moeu"], 1)
                    dve.wait_ge(free["moeu"], e * ET + (f + 1))
                    dve.tensor_tensor(hid[:, f], hid[:, f], cb[:, bass.ds(e, 1)].rearrange("p a n -> p (a n)"),
                                      ALU.mult).then_inc(hid_ready, 1)
                for o in range(8):
                    residual("moe", (2 * ET + o) % 3, o, 1, 5, e * 30 + (2 * ET + o)).then_inc(free["moed"], 1)
            dve.wait_ge(norm_std, 5)
            dve.reciprocal(rstd[:], rstd[:]).then_inc(norm_rstd, 1)
            dve.wait_ge(norm_rstd, 5)
            for kt in range(KT):
                dve.scalar_tensor_tensor(out=hn2[:, kt], in0=x[:, kt], scalar=vcol("gf", kt), in1=rstd[:],
                                         op0=ALU.mult, op1=ALU.mult).then_inc(y_ready, 1)
    return nc


def constants():
    c = np.zeros((P, N_CONST), np.float32)
    p, f = np.arange(P)[:, None], np.arange(P)[None, :]

    def put(name, v):
        a, w = CONST[name]
        c[:, a:a + w] = v
    eye = (p == f)
    put("ident", eye)
    put("ident2", 2 * eye)
    put("ones", 1)
    same = (p // HD == f // HD)
    put("headones", same)
    put("headmean", same / HD)
    put("neg0", np.where(p <= f, 0, NEG))
    put("neg1", np.where(p >= f, 0, NEG))
    put("strict0", p < f)
    put("strict1", p > f)
    put("incl0", (p % HD) <= f[:, :HD])
    put("incl1", (p % HD) >= f[:, :HD])
    for b in (2, 4, 8, 16, 32):
        put(f"bd{b}", p // b == f // b)
    t = np.arange(TOK + 1)[None, :]
    put("reset", t % HD != 0)
    put("mreset", t % P != 0)
    s = np.ones(IN_TILES)
    s[4:8] = DK ** -0.5
    put("in_scale", s)
    put("eps", EPS)
    put("ln_eps", LN_EPS)
    put("code", np.arange(NE, 0, -1))
    return c


def slab8(w):
    n = w.shape[1] // 256
    return w.reshape(KT, P, n, 256).transpose(2, 1, 0, 3).reshape(n, P, KT * 256)


def feat(v):
    return v.reshape(-1, P).T


def layout(i):
    a = {k: np.asarray(v) for k, v in i.items()}
    out = {}
    xs = np.concatenate([a["x_sample"][0], a["x_prompt"][0]])
    out["x"] = np.ascontiguousarray(xs.T.reshape(KT, P, TOK).transpose(1, 0, 2))
    win, bin_ = a["w_m_in"][0], a["b_m_in"][0]
    wi, bi = np.zeros((D, IN_TILES * P), np.float32), np.zeros(IN_TILES * P, np.float32)
    wi[:, :3072], bi[:3072] = win[:, :3072], bin_[:3072]
    for kind in range(2):
        for d in range(2):
            src = 3072 + kind * 16 + d * AH
            dst = (24 + kind) * P + d * 32
            wi[:, dst:dst + AH], bi[dst:dst + AH] = win[:, src:src + AH], bin_[src:src + AH]
    gu = a["w_ff_gu"][0].reshape(D, 2, FT, P).transpose(0, 2, 1, 3).reshape(D, 2 * DFF)
    rkv = a["w_rkv"][0].reshape(3, D, 4, 256).transpose(1, 2, 0, 3).reshape(D, 12 * 256)
    lo = np.zeros((D, 512), np.float32)
    lo[:, 0:64], lo[:, 64:128] = a["w_decay1"][0, 0], a["w_decay1"][0, 1]
    lo[:, 128:192], lo[:, 192:256] = a["w_iclr1"][0, 0], a["w_iclr1"][0, 1]
    lo[:, 256:384] = a["w_gate1"][0]
    eg = a["w_exp_gu"][0].reshape(NE, D, 2, ET, P).transpose(0, 1, 3, 2, 4).reshape(NE, D, 2 * ET * P)
    out["k8"] = np.concatenate([slab8(a["w_ada"][0]), slab8(a["w_ada"][1]), slab8(wi), slab8(a["w_m_out"][0]), slab8(gu),
                                slab8(rkv), slab8(lo), slab8(a["w_rwkv_out"][0])] + [slab8(eg[e]) for e in range(NE)])
    out["ffd"] = np.ascontiguousarray(a["w_ff_down"][0].reshape(FT, P, 8, P).transpose(2, 1, 0, 3).reshape(8, P, SLAB))
    out["exd"] = np.ascontiguousarray(a["w_exp_down"][0].reshape(NE, ET, P, 4, 256).transpose(0, 3, 2, 1, 4).reshape(NE * 4, P, SLAB))
    out["wrouter"] = np.ascontiguousarray(a["w_router"][0].reshape(KT, P, NE).transpose(1, 0, 2))
    l2 = np.stack([a["w_decay2"][0].reshape(P, D), a["w_iclr2"][0].reshape(P, D), a["w_gate2"][0]])
    out["l2"] = np.ascontiguousarray(l2.reshape(3, P, KT, P).transpose(2, 1, 0, 3))
    C0 = np.concatenate([a["state_mlstm_C"][0, 0], a["state_mlstm_n"][0, 0][..., None]], -1)
    out["C0"] = np.ascontiguousarray(C0.reshape(2, 4, 2, DK, DV + 1).transpose(2, 3, 0, 1, 4).reshape(P, 2, 4 * (DV + 1)))
    S = a["state_rwkv_S"][0, 0].reshape(2, KT, 2, HD, HD)
    S0 = np.zeros((KT, P, 2, P), np.float32)
    for h in range(2):
        S0[:, h * HD:(h + 1) * HD, :, h * HD:(h + 1) * HD] = S[:, :, h].transpose(1, 3, 0, 2)
    out["S0"] = S0
    v = np.zeros((P, N_VEC), np.float32)

    def put(name, val):
        at, w = VEC[name]
        v[:, at:at + w] = val
    put("cond", np.stack([feat(a["c"][0]), feat(a["c_ctx"])], -1).reshape(P, 2 * KT))
    for name, key in (("b_ada", "b_ada"), ("gn1", "g_norm1"), ("gn2", "g_norm2"), ("gf", "g_final"), ("g_head", "g_m_head"),
                      ("mu", "mu_rwkv"), ("w0", "w_decay0"), ("a0", "w_iclr0"), ("k_k", "k_k"), ("k_a", "k_a"),
                      ("r_k", "r_k"), ("ln_g", "g_ln_x"), ("ln_b", "b_ln_x")):
        put(name, feat(a[key]))
    put("b_in", feat(bi))
    put("b_router", a["b_router"][0][None, :])
    at = VEC["m0"][0]
    v[0:AH, at], v[32:32 + AH, at] = a["state_mlstm_m"][0, 0, 0], a["state_mlstm_m"][0, 0, 1]
    out["vec"] = v
    out["const"] = constants()
    return out


OUTS = {"y": (P, KT, TOK), "C_out": (P, 2, 4 * (DV + 1)), "m_out": (64, 1), "S_out": (KT, P, 2, P)}


def restore(r):
    y = r["y"].transpose(1, 0, 2).reshape(D, TOK).T
    C = r["C_out"].reshape(2, DK, 2, 4, DV + 1).transpose(2, 3, 0, 1, 4).reshape(2, AH, DK, DV + 1)
    m = r["m_out"][:, 0].reshape(2, 32)[:, :AH]
    S = np.zeros((2, KT, 2, HD, HD), np.float32)
    for h in range(2):
        S[:, :, h] = r["S_out"][:, h * HD:(h + 1) * HD, :, h * HD:(h + 1) * HD].transpose(2, 0, 3, 1)
    c = np.ascontiguousarray
    return (c(y[LAT:][None]), c(y[:LAT][None]), c(C[None, None, ..., :DV]), c(C[None, None, ..., DV]), c(m[None, None]),
            c(S.reshape(1, 1, 2, BH, HD, HD)))


def declare(nc, arrays):
    A = {n: nc.dram_tensor(f"in_{n}", a.shape, F32, kind="ExternalInput").ap() for n, a in arrays.items()}
    A.update({n: nc.dram_tensor(n, s, F32, kind="ExternalOutput").ap() for n, s in OUTS.items()})
    A["rkv_s"] = nc.dram_tensor("rkv_s", (KT, P, 3, TOK), F32, kind="Internal").ap()
    return A


def kernel(**inputs):
    import concourse.bacc as bacc
    from concourse.bass_utils import run_bass_kernel_spmd

    arrays = layout(inputs)
    nc = bacc.Bacc("TRN2", target_bir_lowering=False, num_devices=1)
    build(nc, declare(nc, arrays))
    r = run_bass_kernel_spmd(nc, [{f"in_{n}": v for n, v in arrays.items()}], core_ids=[0])
    return restore(r.results[0])
```

```python
from contextlib import ExitStack

import numpy as np

import concourse.bass as bass
from concourse import mybir

F32 = mybir.dt.float32
ALU = mybir.AluOpType
ACT = mybir.ActivationFunctionType
AX = mybir.AxisListType

P = 128
D = 1024
KT = D // P
LAT, CTX = 512, 128
TOK = LAT + CTX
HALVES = ((0, LAT), (LAT, TOK))
NADA = 6
EPS = 1e-6
AH, DK, DV = 8, 64, 128
CH = TOK // P
BH, HD = 16, 64
C64 = TOK // HD
DECAY = 0.606531
LN_EPS = 64e-5
DFF = 2816
FT = DFF // P
NE = 8
ET = DFF // 2 // P
IN_TILES = 26
CAP = 192
RING = 3
SLAB = 22 * P
NEG = -1e30

CONST = {}
_at = 0
for _name, _w in (("ident", 128), ("ident2", 128), ("ones", 128), ("headones", 128), ("headmean", 128),
                  ("neg0", 128), ("neg1", 128), ("strict0", 128), ("strict1", 128), ("incl0", 64), ("incl1", 64),
                  ("bd4", 128), ("bd8", 128), ("bd16", 128), ("bd32", 128),
                  ("reset", TOK + 1), ("mreset", TOK + 1), ("in_scale", IN_TILES), ("eps", 1), ("ln_eps", 1), ("kk_back", 1), ("nbd2", 128), ("code", NE)):
    CONST[_name] = (_at, _w)
    _at += _w
N_CONST = _at
VEC = {}
_at = 0
for _name, _w in (("cond", KT * 2), ("b_ada", 2 * NADA * KT), ("gn1", 2 * KT), ("gn2", 2 * KT), ("gf", KT),
                  ("b_in", IN_TILES), ("g_head", KT), ("mu", 6 * KT), ("w0", 2 * KT), ("a0", 2 * KT),
                  ("k_k", KT), ("k_a", KT), ("r_k", KT), ("ln_g", KT), ("ln_b", KT), ("b_router", NE), ("m0", 1)):
    VEC[_name] = (_at, _w)
    _at += _w
N_VEC = _at


class Steps:

    def __init__(self, sem, names):
        self.sem, self.names, self.at = sem, names, {n: k + 1 for k, n in enumerate(names)}
        assert len(self.at) == len(names)
        self.next = 0

    def done(self, ins, name):
        assert self.names[self.next] == name, (self.names[self.next], name)
        self.next += 1
        ins.then_inc(self.sem, 1)

    def wait(self, eng, name, lap=0):
        eng.wait_ge(self.sem, lap * len(self.names) + self.at[name])


def repeat(eng, count, body):
    laps = count // RING
    if laps > 1:
        with eng.Fori(0, laps) as i:
            for u in range(RING):
                body(i * RING + u, u)
    else:
        laps = 0
    for k in range(laps * RING, count):
        body(k, k % RING)


MGRP = [(0, 0), (1, 3), (0, 1), (1, 2), (0, 2), (1, 1), (0, 3), (1, 0), (0, 4), (1, 4)]
VK = [(c, kind) for c in range(CH) for kind in ("v0", "v1", "k")]


def mlstm_steps():
    pe, act, dve, pool = [], [], [], []
    pe += [f"T{c}{k}" for c, k in VK]
    act += [f"T{c}{k}" for c, k in VK]
    act += ["absf", "expf", "lnf", "em"] + [f"winter{c}" for c in range(CH)] + [f"ws{c}" for c in range(CH)] + ["dec"]
    dve += ["minf", "lf", "b0", "b1", "g", "m00", "m01", "m10", "m11", "negG"]
    dve += [f"mprev{k}" for k in range(6)] + [f"gend{k}" for k in range(2)] + ["decx"]
    pe += ["cols0", "cols1", "decb"]
    dve += ["cols0", "cols1"] + [f"decp{k}" for k in range(4)]
    for n, (d, c) in enumerate(MGRP):
        pool += [f"kw{n}"]
        for g in range(2):
            pe += [f"D{n}{g}", f"S{n}{g}"]
            act += [f"W{n}{g}"]
            dve += [f"P{n}{g}"]
            pe += [f"num{n}{g}"]
            dve += [f"comb{n}{g}", f"absd{n}{g}", f"den{n}{g}", f"rden{n}{g}", f"h{n}{g}"]
        pe += [f"C{n}"]
        dve += [f"C{n}"]
    act += ["sigo"]
    for c in range(CH):
        pool += [f"sq{c}"]
        dve += [f"ms{c}"]
        act += [f"sd{c}"]
        dve += [f"rs{c}", f"hn{c}"]
    for h in range(AH):
        pe += [f"hT{h}"]
        dve += [f"mo{h}"]
    return pe, act, dve, pool


LEVELS = (4, 8, 16, 32, 64)
GR = ((0, 4), (4, 8), (8, 10))
CHAINS = ((0, tuple(range(8))), (1, tuple(range(7, -1, -1))), (0, (8, 9)), (1, (9, 8)))


def chain_steps(t):
    return [i for i in range(4) if t < len(CHAINS[i][1])]


def rwkv_steps():
    pe, act, dve, pool = [], [], [], []
    dve += ["kk0", "sq", "vT0", "vT1"]
    pe += ["w0", "a0", "knorm", "gate", "V0", "V1", "V2", "w1", "a1"]
    act += ["thw0", "tha0", "knln", "knorm", "gate", "V0", "V1", "V2"]
    for d in range(2):
        dve += [f"lw{d}", f"c{d}", f"ce{d}"] + ["kmax"] * (d == 0) + [f"a{d}", f"f{d}", f"kd{d}"]
        act += [f"e1{d}", f"e2{d}", f"e3{d}", f"pend{d}"]
        if d == 0:
            dve += ["kk"]
            act += ["thw1", "tha1"]
        dve += [f"b{d}", f"R{d}"] + [f"{x}{h}{d}" for x in "QKB" for h in range(2)]
        pe += [f"Kt{d}{g}" for g in range(3)] + [f"Bt{d}{g}" for g in range(3)]
        act += [f"Kt{d}{g}" for g in range(3)] + [f"Bt{d}{g}" for g in range(3)]
        pe += [f"GK{d}{q}" for q in range(5)] + [f"GB{d}{q}" for q in range(5)]
    for d in range(2):
        for q in range(5):
            dve += [f"MkT{d}{q}", f"Ark{d}{q}"]
        for q in range(5):
            dve += [f"LT{d}{q}", f"Arb{d}{q}"]
    dve += ["XTa1", "XT21", "kds", "rk", "rkk"]
    pool += ["XTa0", "XT20", "LTI0", "Ark", "LTI1"]
    for d in range(2):
        pe += [f"MV{d}{g}" for g in range(3)] + [f"KV{d}{g}" for g in range(3)]
        act += [f"MV{d}{g}" for g in range(3)]
        dve += [f"KV{d}{g}" for g in range(3)]
    pe += ["bonus", "yV"]
    dve += ["yb", "y0"]
    for lv in LEVELS:
        for ph in ("X", "Y", "Z"):
            for d in range(2):
                for g in range(3):
                    pe += [f"{ph}{lv}{d}{g}"]
                    (act if ph == "X" or (ph == "Z" and lv == 64) else dve).append(f"{ph}{lv}{d}{g}")
    for t in range(8):
        mine = chain_steps(t)
        pe += [f"rhs{t}{i}" for i in mine] + [f"U{t}{i}" for i in mine] + [f"S{t}{i}" for i in mine] + [f"y{t}{i}" for i in mine]
        dve += [f"rhs{t}{i}" for i in mine] + [f"Sp{t}{i}" for i in mine] + [f"S{t}{i}" for i in mine] + [f"y{t}{i}" for i in mine]
        act += [f"U{t}{i}" for i in mine]
    pe += ["mean", "var"]
    dve += ["yc", "ysq", "yn", "yl", "yg"]
    act += ["varln", "std"]
    return pe, act, dve, pool


def build(nc, A, upto=99):
    with ExitStack() as ctx:
        def sb(name, shape, dtype=F32):
            return ctx.enter_context(nc.sbuf_tensor(name, shape, dtype))

        def sem(name):
            return ctx.enter_context(nc.semaphore(name))

        x = sb("x", [P, KT, TOK])
        ring = sb("ring", [P, RING, SLAB])
        const = sb("const", [P, N_CONST])
        vec = sb("vec", [P, N_VEC])
        wrouter = sb("wrouter", [P, KT, NE])
        scond = sb("scond", [P, KT, 2])
        mods = sb("mods", [P, 2, NADA, KT, 2])
        gs = sb("gs", [P, 2, 2, KT, 2])
        w0h = sb("w0h", [P, 2 * 2 * KT])
        omka = sb("omka", [P, KT])
        bs_in = sb("bs_in", [P, IN_TILES])
        rstd = sb("rstd", [P, TOK])
        NA = 34400
        arena = sb("arena", [P, NA])
        PS = ctx.enter_context(nc.psum_tensor("PS", [P, 8, 512], F32))
        psf = PS[:].rearrange("p b n -> p (b n)")

        def cst(name, rows=slice(0, P)):
            a, w = CONST[name]
            return const[rows, a:a + w]

        def vcol(name, k, n=1):
            a, _ = VEC[name]
            if isinstance(k, int):
                return vec[:, a + k:a + k + n]
            return vec[:, bass.ds(k + a, n)]

        class Region:
            def __init__(self):
                self.at = 0

            def __call__(self, *shape):
                n = int(np.prod(shape))
                v = arena[:, self.at:self.at + n]
                self.at += n
                assert self.at <= NA, self.at
                if len(shape) == 2:
                    v = v.rearrange("p (a b) -> p a b", a=shape[0])
                if len(shape) == 3:
                    v = v.rearrange("p (a b c) -> p a b c", a=shape[0], b=shape[1])
                if len(shape) == 4:
                    v = v.rearrange("p (a b c d) -> p a b c d", a=shape[0], b=shape[1], c=shape[2])
                return v

        def acc(k):
            return psf[:, k * 1024:k * 1024 + TOK]

        stats = psf[:, 3072:3072 + TOK]

        r = Region()
        hn = r(KT, TOK)
        z = r(IN_TILES, TOK)
        vaug = r(CH, AH, DV + 1)
        ktok = r(CH, AH * DK)
        colw = r(CH, 3, 64)
        mprev, gend, dec = r(CH), r(CH), r(CH)
        decx = r(CH, 64)
        decp = r(CH, 2, 4)
        winter_r, ws_r = r(TOK), r(TOK)
        smalls = r(64)
        g_row, negG = r(TOK), r(TOK)
        tmp_row, b_row = winter_r, ws_r
        hs_t = hn.rearrange("p a b -> p (a b)").rearrange("p (c f) -> p c f", c=CH)
        q_, k_ = z[:, 0:4], z[:, 4:8]
        v_, o_ = z[:, 8:16], z[:, 16:24]
        gi, gf = z[:, 24], z[:, 25]
        gm = gf
        vr = z[:, 8:16].rearrange("p a b -> p (a b)")
        Wt = vr[:, 0:1024].rearrange("p (a h n) -> p a h n", a=2, h=4)
        kw = vr[:, 1024:2048].rearrange("p (a n) -> p a n", a=2)
        comb = vr[:, 2048:2048 + 516].rearrange("p (h n) -> p h n", h=4)
        Cst = vr[:, 2564:2564 + 2064].rearrange("p (d s n) -> p d s n", d=2, s=2)
        rden = smalls[:, 0:4]
        ms, rs = smalls[:, 8:16], smalls[:, 16:24]
        sqt = vr[:, 0:1024].rearrange("p (h n) -> p h n", h=AH)

        r = Region()
        hn_f = r(KT, TOK)
        hid_f = r(FT, TOK)
        sg_f = r(RING, TOK)

        r = Region()
        QR = [r(C64, 192) for _ in range(2)]
        KX = [r(C64, P) for _ in range(2)]
        BY = [r(C64, P) for _ in range(2)]
        Ktok = [r(C64, P) for _ in range(2)]
        Btok = [r(C64, P) for _ in range(2)]
        MkT = [r(C64, P) for _ in range(2)]
        Ark = [r(C64, HD) for _ in range(2)]
        Arb = [r(C64, HD) for _ in range(2)]
        LT = [r(C64, P) for _ in range(2)]
        XT = [r(C64, P) for _ in range(2)]
        Vbd = r(C64, P)
        St = r(4, P)
        RU = r(4, P)
        pend = r(2, C64)
        split = r.at
        lhid = r(3, TOK)
        l2 = r(3, P)
        gk = r(KT, TOK)
        tr = ring[:].rearrange("p a b -> p (a b)")
        T = [tr[:, n * TOK:(n + 1) * TOK] for n in range(10)]
        Sp, St_odd = (T[n][:, 0:4 * P].rearrange("p (i n) -> p i n", i=4) for n in (6, 7))
        rkv = tr[:, 10 * TOK:13 * TOK].rearrange("p (s n) -> p s n", s=3)
        r = Region()
        hn1 = r(KT, TOK)
        xx = r(KT, TOK)
        xm = [r(KT, TOK) for _ in range(3)]
        stage = gk[:, 0:3]
        assert r.at <= split, (r.at, split)

        r = Region()
        hn2 = r(KT, TOK)
        lg = r(CH, NE)
        eq = r(CH, NE)
        oh1, oh2, l2g, comb_w = r(CH, NE), r(CH, NE), r(CH, NE), r(CH, NE)
        one_hot, row_of = r(CH, NE), r(CH, NE)
        mx1, mx2, e12, p1, p2 = r(CH), r(CH), r(CH), r(CH), r(CH)
        rows_f, over = r(2, CH), r(1)
        routed = r.at
        cb = r(NE, TOK)
        hid = r(ET, TOK)
        sg = r(RING, TOK)
        r.at = routed
        hnt = r(CH, D)
        out2 = r(CH, D)
        xg = r(2, D)
        yo = r(2, D)
        xe = r(KT, CAP)
        hide = r(ET, CAP)
        sge = r(4, CAP)
        rows_i = sb("rows_i", [P, 2 * CH + 1], mybir.dt.int32)

        loaded = sem("loaded")
        slab_ready = [sem(f"slab_ready{k}") for k in range(RING)]
        tiles_done = sem("tiles_done")
        cond_ready = sem("cond_ready")
        mods_ready = sem("mods_ready")
        dve_chain = sem("dve_chain")
        norm_sq, norm_sum, norm_std, norm_rstd = sem("norm_sq"), sem("norm_sum"), sem("norm_std"), sem("norm_rstd")
        norm_x, norm_done = sem("norm_x"), sem("norm_done")
        cb_full = sem("cb_full")
        free = {n: sem(f"{n}_free") for n in ("in", "mout", "ffg", "ffu", "ffd", "rkv", "lora", "rout", "cb",
                                              "moeg", "moeu", "moed")}
        state_loaded = sem("state_loaded")
        ones_set = sem("ones_set")
        zero_set = sem("zero_set")
        st_loaded = sem("st_loaded")
        mpe, mact, mdve, mpool = (Steps(sem(f"mlstm_{n}"), s) for n, s in zip(("pe", "act", "dve", "pool"), mlstm_steps()))
        rpe, ract, rdve, rpool = (Steps(sem(f"rwkv_{n}"), s) for n, s in zip(("pe", "act", "dve", "pool"), rwkv_steps()))
        out_done = sem("out_done")
        xx_ready, xm_ready = sem("xx_ready"), sem("xm_ready")
        staged = sem("staged")
        stored = [sem(f"stored{k}") for k in range(3)]
        l2_in, rkv_in, st_in = sem("l2_in"), sem("rkv_in"), sem("st_in")
        states_out = sem("states_out")
        logits_full, comb_ready = sem("logits_full"), sem("comb_ready")
        hid_ready = sem("hid_ready")
        exp_in, exp_done = sem("exp_in"), sem("exp_done")
        y_ready = sem("y_ready")
        zeroed = sem("zeroed")
        zero_stored = sem("zero_stored")
        hnt_t, hnt_ready = sem("hnt_t"), sem("hnt_ready")
        onehot_ready, counted, routes_ready = sem("onehot_ready"), sem("counted"), sem("routes_ready")
        scattered = sem("scattered")
        xg_in, xg_t = sem("xg_in"), sem("xg_t")
        xe_act, xe_dve = sem("xe_act"), sem("xe_dve")
        gate_done, pair_used = sem("gate_done"), sem("pair_used")
        yo_act, yo_dve, yo_stored = sem("yo_act"), sem("yo_dve"), sem("yo_stored")
        gathered = [sem(f"gathered{c}") for c in range(CH)]
        combine, outs_t, outs_used = sem("combine"), sem("outs_t"), sem("outs_used")
        x_done = sem("x_done")

        slab_n = {"sp": 0, "pe": 0}
        base, after = {}, []
        for name, slab_tiles in (("ada", [2] * 48), ("in", [2] * 13), ("mout", [2] * 4), ("ff", [2] * FT), ("ffd", [1] * 8),
                                 ("rkv", [2] * 12), ("lora", [2, 1]), ("rout", [2] * 4), ("moe", [2] * 15 * NE)):
            base[name] = after[-1] if after else 0
            for t in slab_tiles:
                after.append((after[-1] if after else 0) + t)

        def tile_done(eng, name, t):
            eng.wait_ge(tiles_done, t + (base[name] + 1))

        def stream(sp, dram, first, count, width):
            n0 = slab_n["sp"]
            laps = count // RING

            def load(k, slot):
                src = dram[k + first] if isinstance(k, int) else dram[bass.ds(k + first, 1)].rearrange("a p n -> p (a n)")
                sp.dma_start(ring[:, slot, 0:width], src).then_inc(slab_ready[slot], 16)

            need = lambda n: after[n - RING] if n >= RING else 0
            k = 0
            while k < count:
                rest = (count - k) // RING
                step = {need(n0 + k + RING * i + u) - need(n0 + k + RING * (i - 1) + u)
                        for i in range(1, rest) for u in range(RING)}
                if rest > 1 and len(step) == 1 and need(n0 + k) > 0:
                    grow = step.pop()
                    with sp.Fori(0, rest) as i:
                        for u in range(RING):
                            sp.wait_ge(tiles_done, i * grow + need(n0 + k + u))
                            load(i * RING + (k + u), (n0 + k + u) % RING)
                    k += rest * RING
                else:
                    if need(n0 + k):
                        sp.wait_ge(tiles_done, need(n0 + k))
                    load(k, (n0 + k) % RING)
                    k += 1
            slab_n["sp"] += count

        def slabs(pe, count, body):
            n0 = slab_n["pe"]

            def one(k, u):
                slot = (n0 + u) % RING
                lap = (k - u) // RING if isinstance(k, int) else None
                if lap is not None:
                    pe.wait_ge(slab_ready[slot], 16 * (lap + (n0 + u) // RING + 1))
                else:
                    pe.wait_ge(slab_ready[slot], wait_lap(k, u, (n0 + u) // RING))
                body(k, u, slot)
            repeat2(pe, count, one)
            slab_n["pe"] += count

        lap_reg = {}

        def wait_lap(k, u, off):
            return lap_reg["i"] * 16 + 16 * (off + 1)

        def repeat2(eng, count, body):
            laps = count // RING
            if laps > 1:
                with eng.Fori(0, laps) as i:
                    lap_reg["i"] = i
                    for u in range(RING):
                        body(i * RING + u, u)
            else:
                laps = 0
            for k in range(laps * RING, count):
                body(k, k % RING)

        def credit(eng, s, n):
            eng.sem_inc(s, n)

        def mm_tile(pe, a, w, src, kt_n, last_wait=None):
            for kt in range(kt_n):
                if last_wait and kt == kt_n - 1:
                    last_wait()
                for lo, hi in HALVES:
                    m = pe.matmul(acc(a)[:, lo:hi], w(kt), src(kt, lo, hi), start=kt == 0, stop=kt == kt_n - 1)
            return m

        block = ctx.enter_context(nc.Block())

        @block.sync
        def _(sp):
            sp.dma_start(vec[:], A["vec"]).then_inc(loaded, 16)
            sp.dma_start(const[:], A["const"]).then_inc(loaded, 16)
            sp.dma_start(x[:], A["x"]).then_inc(loaded, 16)
            sp.dma_start(wrouter[:], A["wrouter"]).then_inc(loaded, 16)
            k8 = A["k8"]
            W8 = KT * 256
            stream(sp, k8, 0, 48, W8)
            if upto < 2: return
            stream(sp, k8, 48, 13, W8)
            if upto < 3: return
            mact.wait(sp, f"T{CH-1}k")
            sp.dma_start(Cst[:, :, 0, :], A["C0"]).then_inc(state_loaded, 16)
            stream(sp, k8, 61, 4, W8)
            mdve.wait(sp, "m11")
            sp.dma_start(A["m_out"][0:32], gf[0:32, TOK - 1:TOK], allow_slow_non_contiguous=True).then_inc(out_done, 16)
            sp.dma_start(A["m_out"][32:64], gf[32:64, LAT:LAT + 1], allow_slow_non_contiguous=True).then_inc(out_done, 16)
            mdve.wait(sp, "C9")
            sp.dma_start(A["C_out"], Cst[:, :, 1, :]).then_inc(out_done, 16)
            sp.wait_ge(out_done, 48)
            credit(sp, states_out, 1)
            if upto < 4: return
            stream(sp, k8, 65, 22, W8)
            stream(sp, A["ffd"], 0, 8, SLAB)
            if upto < 5: return
            stream(sp, k8, 87, 12, W8)
            stream(sp, k8, 99, 2, W8)
            if upto < 6: return
            for s in stored:
                sp.wait_ge(s, 16 * 9)
            sp.sem_inc(st_loaded, 16)
            tile_done(sp, "lora", 2)

            def l2_load(j):
                sp.dma_start(l2, A["l2"][bass.ds(j, 1)].rearrange("a p s n -> p (a s) n")).then_inc(l2_in, 16)

            def rkv_load(j):
                sp.dma_start(rkv, A["rkv_s"][bass.ds(j, 1)].rearrange("a p s n -> p (a s) n")).then_inc(rkv_in, 16)

            def st_load(j):
                sp.dma_start(St[:, 0:2], A["S0"][bass.ds(j, 1)].rearrange("a p s n -> p (a s) n")).then_inc(st_in, 16)

            def tile_io(j, last):
                J = j + 1
                if not last:
                    rpe.wait(sp, "a1", J)
                    l2_load(J)
                    rdve.wait(sp, "y0", J)
                    rkv_load(J)
                rdve.wait(sp, "S13", J)
                sp.dma_start(A["S_out"][bass.ds(j, 1)].rearrange("a p s n -> p (a s) n"), St[:, 2:4]).then_inc(st_loaded, 16)
                if not last:
                    rdve.wait(sp, "S71", J)
                    st_load(J)
            l2_load(0)
            rkv_load(0)
            st_load(0)
            with sp.Fori(0, KT - 1) as j:
                tile_io(j, False)
            tile_io(KT - 1, True)
            sp.wait_ge(st_loaded, 16 * (KT + 1))
            ract.wait(sp, "std", KT)
            rdve.wait(sp, "yg", KT)
            stream(sp, k8, 101, 4, W8)
            if upto < 7: return
            with sp.Fori(0, NE) as e:
                n0 = slab_n["sp"]
                per = 15
                for k in range(per):
                    slot = (n0 + k) % RING
                    sp.wait_ge(tiles_done, e * 30 + after[n0 + k - RING])
                    if k < ET:
                        src = k8[bass.ds(e * ET + (105 + k), 1)].rearrange("a p n -> p (a n)")
                        w = W8
                    else:
                        src = A["exd"][bass.ds(e * 4 + (k - ET), 1)].rearrange("a p n -> p (a n)")
                        w = SLAB
                    sp.dma_start(ring[:, slot, 0:w], src).then_inc(slab_ready[slot], 16)
            for kt in range(KT):
                sp.wait_ge(y_ready, kt + 1)
                sp.dma_start(A["y"][:, kt], hn2[:, kt]).then_inc(out_done, 16)
            sp.wait_ge(out_done, 48 + 16 * KT)

        @block.gpsimd
        def _(pool):
            zeros = arena[:, NA - 3 * D:NA]
            pool.memset(zeros, 0.0).then_inc(zeroed, 1)
            pool.wait_ge(zeroed, 1)
            for q in range(NE * CAP // (3 * P)):
                pool.dma_start(A["rows"].rearrange("(q p a) n -> q p (a n)", p=P, a=3)[q], zeros).then_inc(zero_stored, 16)
            if upto < 3: return
            pool.wait_ge(free["in"], 3 + IN_TILES)
            pool.wait_ge(zero_stored, 16 * 4)
            pool.sem_inc(zeroed, 1)
            pool.memset(vaug[:, :, :, DV:DV + 1], 1.0).then_inc(ones_set, 1)
            mact.wait(pool, f"T{CH-1}k")
            pool.wait_ge(ones_set, 1)
            pool.memset(Cst[:, :, 1, :], 0.0).then_inc(ones_set, 1)
            pool.wait_ge(ones_set, 2)
            mdve.wait(pool, "cols1")
            for n, (d, c) in enumerate(MGRP):
                if n >= 2:
                    mpe.wait(pool, f"C{n-2}")
                if n >= 1:
                    mpool.wait(pool, f"kw{n-1}")
                mpool.done(pool.tensor_tensor(
                    kw[:, n % 2].rearrange("p (h k) -> p h k", h=AH), ktok[:, c].rearrange("p (h k) -> p h k", h=AH),
                    colw[:, c, 1, d * 32:d * 32 + AH].unsqueeze(2).to_broadcast([P, AH, DK]), ALU.mult), f"kw{n}")
            for c in range(CH):
                mdve.wait(pool, "h91")
                mpool.wait(pool, f"kw9" if c == 0 else f"sq{c-1}")
                if c:
                    mdve.wait(pool, f"ms{c-1}")
                mpool.done(pool.tensor_tensor(sqt.rearrange("p h n -> p (h n)"), hs_t[:, c], hs_t[:, c], ALU.mult), f"sq{c}")
            if upto < 6: return
            pool.wait_ge(free["lora"], 3 + 3)
            n = 0
            for buf in (QR[0], QR[1], KX[0], KX[1], BY[0], BY[1]):
                if n:
                    pool.wait_ge(zero_set, n)
                pool.memset(buf, 0.0).then_inc(zero_set, 1)
                n += 1
            pool.sem_inc(rpool.sem, len(rpool.names))
            all_i = cst("ident").unsqueeze(1).to_broadcast([P, C64, P])
            with pool.Fori(0, KT) as j:
                J = j + 1
                rdve.wait(pool, "LT04", J)
                rpool.done(pool.tensor_tensor(XT[0], LT[0], cst("nbd2").unsqueeze(1).to_broadcast([P, C64, P]), ALU.mult), "XTa0")
                rpool.wait(pool, "XTa0", J)
                rpool.done(pool.tensor_tensor(XT[0], XT[0], all_i, ALU.add), "XT20")
                rpool.wait(pool, "XT20", J)
                rpool.done(pool.tensor_tensor(LT[0], LT[0], all_i, ALU.add), "LTI0")
                rdve.wait(pool, "Ark14", J)
                rpool.wait(pool, "LTI0", J)
                rpool.done(pool.tensor_tensor(Ark[0], Ark[0], Ark[1], ALU.add), "Ark")
                rdve.wait(pool, "XTa1", J)
                rpool.wait(pool, "Ark", J)
                rpool.done(pool.tensor_tensor(LT[1], LT[1], all_i, ALU.add), "LTI1")
                rpool.next = 0
            if upto < 7: return
            pool.wait_ge(routes_ready, 1)
            dense = pool.value_load(rows_i[0:1, 2 * CH:2 * CH + 1], min_val=0, max_val=1)
            with pool.If(1 - dense):
                def rows(k, c):
                    return bass.IndirectOffsetOnAxis(ap=rows_i[:, k * CH + c:k * CH + c + 1].bitcast(mybir.dt.uint32), axis=0)
                pool.wait_ge(hnt_ready, 2 * CH)
                for c in range(CH):
                    for k in range(2):
                        pool.indirect_dma_start(A["rows"], rows(k, c), hnt[:, c], None, bounds_check=NE * CAP - 1).then_inc(scattered, 16)
                pool.wait_ge(yo_stored, 32 * (NE + 1))
                for c in range(CH):
                    for k in range(2):
                        pool.indirect_dma_start((hnt, out2)[k][:, c], None, A["rows"], rows(k, c),
                                                bounds_check=NE * CAP - 1).then_inc(gathered[c], 16)

        @block.tensor
        def _(pe):
            pe.wait_ge(cond_ready, 1)

            def ada(k, u, slot):
                w = ring[:, slot, 0:KT * 256].rearrange("p (kt n) -> p kt n", kt=KT)
                for t in range(2):
                    out = psf[:, 4 * k + 2 * t:4 * k + 2 * t + 2] if isinstance(k, int) else psf[:, bass.ds(k * 4 + 2 * t, 2)]
                    for kt in range(KT):
                        m = pe.matmul(out, w[:, kt, t * P:(t + 1) * P], scond[:, kt, :], start=kt == 0, stop=kt == KT - 1)
                    m.then_inc(tiles_done, 1)
            slabs(pe, 48, ada)

            def norm(n):
                for kt in range(KT):
                    pe.wait_ge(norm_sq, 8 * n + kt + 1)
                    for lo, hi in HALVES:
                        m = pe.matmul(stats[:, lo:hi], cst("ones"), sq_buf[n][:, kt, lo:hi], start=kt == 0, stop=kt == KT - 1)
                m.then_inc(norm_sum, 1)

            def dense8(count, src, name, credits=3):
                def one(k, u, slot):
                    w = ring[:, slot, 0:KT * 256].rearrange("p (kt n) -> p kt n", kt=KT)
                    for t in range(2):
                        pe.wait_ge(free[name], k * 2 + (t + 1))
                        m = mm_tile(pe, (2 * u + t) % 3, lambda kt: w[:, kt, t * P:(t + 1) * P],
                                    lambda kt, lo, hi: src[:, kt, lo:hi], KT)
                        m.then_inc(tiles_done, 1)
                slabs(pe, count, one)

            sq_buf = [hn, hn_f, hn1, hn2, hn2]
            if upto < 2: return
            norm(0)
            pe.wait_ge(norm_done, 16)
            dense8(13, hn, "in")
            if upto < 3: return
            pe.wait_ge(free["in"], 3 + IN_TILES)
            for n, (c, kind) in enumerate(VK):
                if n >= 6:
                    mact.wait(pe, "T%d%s" % VK[n - 6])
                src = {"v0": v_[:, 0:4], "v1": v_[:, 4:8], "k": k_}[kind]
                for t in range(4):
                    m = pe.transpose(PS[:, n % 6, t * P:(t + 1) * P], src[:, t, c * P:(c + 1) * P], cst("ident"))
                mpe.done(m, f"T{c}{kind}")
            mact.wait(pe, "dec")
            for n in range(15):
                c, kind = n // 3, n % 3
                src = (winter_r, ws_r, gi)[kind]
                m = pe.transpose(PS[:, 6 + n // 8, (n % 8) * 64:(n % 8) * 64 + 64], src[0:64, c * P:(c + 1) * P],
                                 cst("ident", slice(0, 64))[:, 0:64])
                if n in (7, 14):
                    mpe.done(m, f"cols{n // 8}")
            mdve.wait(pe, "decx")
            mact.wait(pe, "T%d%s" % VK[-1])
            mpe.done(pe.matmul(PS[:, 0, 0:CH * 64], cst("ones", slice(0, 64)), decx[0:64].rearrange("p c r -> p (c r)"),
                               start=True, stop=True), "decb")
            mdve.wait(pe, "decp3")
            pe.wait_ge(state_loaded, 16)
            pe.wait_ge(ones_set, 2)
            for n, (d, c) in enumerate(MGRP):
                seq = 0 if c < 4 else 1
                tok = slice(c * P, (c + 1) * P)
                for g in range(2):
                    prev = (n, 0) if g else (n - 1, 1)
                    if n or g:
                        mact.wait(pe, f"W{prev[0]}{prev[1]}")
                    for h in range(4):
                        row = d * 32 + 2 * h + g
                        pick = cst("ident", slice(0, 64))[:, row:row + 1].to_broadcast([64, P])
                        o = PS[:, 0, h * P:(h + 1) * P]
                        pe.matmul(o, pick, negG[0:64, tok], start=True, stop=False)
                        pe.matmul(o, g_row[0:64, tok], pick, start=False, stop=False)
                        m = pe.matmul(o, cst("ident"), cst(f"neg{d}"), start=False, stop=True)
                    mpe.done(m, f"D{n}{g}")
                    if n or g:
                        mdve.wait(pe, f"P{prev[0]}{prev[1]}")
                    for h in range(4):
                        hh = 2 * h + g
                        pr = slice(64 * g, 64 * g + 64)
                        m = pe.matmul(PS[:, 1, h * P:(h + 1) * P], k_[pr, hh // 2, tok], q_[pr, hh // 2, tok],
                                      start=True, stop=True)
                    mpe.done(m, f"S{n}{g}")
                    if n or g:
                        mdve.wait(pe, f"comb{prev[0]}{prev[1]}")
                    if n >= 2 and not g:
                        mdve.wait(pe, f"C{n-2}")
                    mdve.wait(pe, f"P{n}{g}")
                    for h in range(4):
                        hh = 2 * h + g
                        pr = slice(64 * g, 64 * g + 64)
                        pe.matmul(PS[:, 4 + h // 2, (h % 2) * 129:(h % 2) * 129 + 129], q_[pr, hh // 2, tok],
                                  Cst[pr, d, seq, (hh // 2) * 129:(hh // 2) * 129 + 129], start=True, stop=True)
                        m = pe.matmul(PS[:, 2 + h // 2, (h % 2) * 129:(h % 2) * 129 + 129], Wt[:, g, h, :],
                                      vaug[:, c, hh, :], start=True, stop=True)
                    mpe.done(m, f"num{n}{g}")
                mpool.wait(pe, f"kw{n}")
                if n:
                    mdve.wait(pe, f"C{n-1}")
                for hh in range(AH):
                    p0 = 64 * (hh % 2)
                    pair = hh // 2
                    m = pe.matmul(PS[p0:p0 + 64, 6 + pair // 2, (pair % 2) * 129:(pair % 2) * 129 + 129],
                                  kw[:, n % 2, hh * DK:(hh + 1) * DK], vaug[:, c, hh, :], start=True, stop=True)
                mpe.done(m, f"C{n}")
            for h in range(AH):
                if h >= 3:
                    mdve.wait(pe, f"mo{h-3}")
                for c in range(CH):
                    mdve.wait(pe, f"hn{c}")
                    m = pe.transpose(acc(h % 3)[:, c * P:(c + 1) * P], hs_t[:, c, h * DV:(h + 1) * DV], cst("ident"))
                mpe.done(m, f"hT{h}")
            mdve.wait(pe, "mo7")
            dense8(4, o_, "mout")
            if upto < 4: return
            norm(1)
            pe.wait_ge(norm_done, 32)

            def ff(k, u, slot):
                w = ring[:, slot, 0:KT * 256].rearrange("p (kt n) -> p kt n", kt=KT)
                for t in range(2):
                    pe.wait_ge(free["ffu"] if t == 0 else free["ffg"], k + 1)
                    m = mm_tile(pe, (2 * u + t) % 3, lambda kt: w[:, kt, t * P:(t + 1) * P],
                                lambda kt, lo, hi: hn_f[:, kt, lo:hi], KT)
                    m.then_inc(tiles_done, 1)
            slabs(pe, FT, ff)
            pe.wait_ge(free["ffu"], 2 + FT)

            def ffd(k, u, slot):
                w = ring[:, slot, :].rearrange("p (kt n) -> p kt n", kt=FT)
                pe.wait_ge(free["ffd"], k + 1)
                m = mm_tile(pe, u % 3, lambda kt: w[:, kt, :], lambda kt, lo, hi: hid_f[:, kt, lo:hi], FT)
                m.then_inc(tiles_done, 1)
            slabs(pe, 8, ffd)
            if upto < 5: return
            norm(2)

            pe.wait_ge(xm_ready, 3)

            def rkvp(k, u, slot):
                w = ring[:, slot, 0:KT * 256].rearrange("p (kt n) -> p kt n", kt=KT)
                for t in range(2):
                    pe.wait_ge(free["rkv"], k * 2 + (t + 1))
                    m = mm_tile(pe, (2 * u + t) % 3, lambda kt: w[:, kt, t * P:(t + 1) * P],
                                lambda kt, lo, hi: xm[u][:, kt, lo:hi], KT)
                    m.then_inc(tiles_done, 1)
            slabs(pe, 12, rkvp)
            pe.wait_ge(xm_ready, 6)

            def lora(k, u, slot):
                w = ring[:, slot, 0:KT * 256].rearrange("p (kt n) -> p kt n", kt=KT)
                for t in range(2):
                    if 2 * k + t > 2:
                        break
                    pe.wait_ge(free["lora"], 2 * k + t + 1)
                    m = mm_tile(pe, 2 * k + t, lambda kt: w[:, kt, t * P:(t + 1) * P],
                                lambda kt, lo, hi: xm[2 * k + t][:, kt, lo:hi], KT)
                    m.then_inc(tiles_done, 1)
            slabs(pe, 2, lora)
            if upto < 6: return
            pe.wait_ge(free["lora"], 3 + 3)
            pe.wait_ge(zero_set, 6)
            pe.sem_inc(rpe.sem, len(rpe.names))
            with pe.Fori(0, KT) as j:
                J = j + 1
                wide = lambda b: psf[:, b * 512:b * 512 + TOK]

                def two(b, lhsT, rhs):
                    for lo, hi in HALVES:
                        m = pe.matmul(wide(b)[:, lo:hi], lhsT, rhs[:, lo:hi], start=True, stop=True)
                    return m

                def lora2(d):
                    dd = slice(64 * d, 64 * d + 64)
                    rpe.done(two(4, l2[dd, 0], lhid[dd, 0]), f"w{d}")
                    rpe.done(two(6, l2[dd, 1], lhid[dd, 1]), f"a{d}")
                pe.wait_ge(l2_in, j * 16 + 16)
                rdve.wait(pe, "y71", j)
                lora2(0)
                rdve.wait(pe, "sq", J)
                rpe.done(two(0, cst("headones"), T[1]), "knorm")
                ract.wait(pe, "varln", j)
                rpe.done(two(2, l2[:, 2], lhid[:, 2]), "gate")

                def tr(src, b0, label, before):
                    for g, (c0, c1) in enumerate(GR):
                        before(g)
                        for c in range(c0, c1):
                            m = pe.transpose(PS[:, b0 + g, (c - c0) * P:(c - c0 + 1) * P], src[:, c], cst("ident"))
                        rpe.done(m, f"{label}{g}")
                rdve.wait(pe, "vT1", J)
                rdve.wait(pe, "kmax", J)
                tr(BY[1], 0, "V", lambda g: ract.wait(pe, "gate", J) if g == 2 else None)
                ract.wait(pe, "tha0", J)
                lora2(1)
                for d in range(2):
                    rdve.wait(pe, f"K1{d}", J)
                    tr(KX[d], 0, f"Kt{d}", lambda g: rdve.wait(pe, "Ark04", J) if d else ract.wait(pe, f"V{g}", J))
                    rdve.wait(pe, f"B1{d}", J)
                    if d == 0:
                        ract.wait(pe, "tha1", J)
                    tr(BY[d], 3, f"Bt{d}", lambda g: rdve.wait(pe, f"Arb0{g}", J) if d else None)
                    for nm, src, banks in (("GK", KX[d], (6, 7, 0, 1, 2)), ("GB", BY[d], (3, 4, 5, 6, 7))):
                        for q in range(5):
                            b = banks[q]
                            if nm == "GK" and b >= 6 and d:
                                rdve.wait(pe, f"Arb0{b-3}", J)
                            if nm == "GK" and b < 3:
                                ract.wait(pe, f"Kt{d}{b}", J)
                            if nm == "GB" and b < 6:
                                ract.wait(pe, f"Bt{d}{b-3}", J)
                            if nm == "GB" and b >= 6:
                                rdve.wait(pe, f"Ark{d}{b-6}", J)
                            for i in range(2):
                                c = 2 * q + i
                                m = pe.matmul(PS[:, b, i * 192:(i + 1) * 192], src[:, c], QR[d][:, c, :], start=True, stop=True)
                            rpe.done(m, f"{nm}{d}{q}")
                for d in range(2):
                    for nm, b0, src in (("MV", 0, MkT[d]), ("KV", 3, Ktok[d])):
                        for g, (c0, c1) in enumerate(GR):
                            if d:
                                (ract if nm == "MV" else rdve).wait(pe, f"{nm}0{g}", J)
                            else:
                                rdve.wait(pe, f"Ark1{g+2}" if nm == "MV" else f"Arb1{g}", J)
                            for c in range(c0, c1):
                                m = pe.matmul(PS[:, b0 + g, (c - c0) * P:(c - c0 + 1) * P], src[:, c], Vbd[:, c], start=True, stop=True)
                            rpe.done(m, f"{nm}{d}{g}")
                rdve.wait(pe, "rkk", J)
                rdve.wait(pe, "Arb14", J)
                rpe.done(two(6, cst("headones"), T[5]), "bonus")
                ract.wait(pe, "MV10", J)
                ract.wait(pe, "MV11", J)
                rpool.wait(pe, "Ark", J)
                for c in range(C64):
                    m = pe.matmul(wide(0)[:, c * HD:(c + 1) * HD], Vbd[:, c], Ark[0][:, c], start=True, stop=True)
                rpe.done(m, "yV")
                for n, lv in enumerate(LEVELS):
                    for ph in ("X", "Y", "Z"):
                        for d in range(2):
                            for g, (c0, c1) in enumerate(GR):
                                b = d * 3 + g
                                if ph == "X":
                                    if n == 0:
                                        (rdve if d else rpool).wait(pe, f"XT2{d}", J)
                                        rdve.wait(pe, "y0", J)
                                        if d == 0 and g == 2:
                                            ract.wait(pe, "MV12", J)
                                        if d:
                                            rdve.wait(pe, f"KV1{g}", J)
                                    else:
                                        rdve.wait(pe, f"Z{LEVELS[n-1]}{d}{g}", J)
                                elif ph == "Y":
                                    ract.wait(pe, f"X{lv}{d}{g}", J)
                                    if n == 0:
                                        rpool.wait(pe, f"LTI{d}", J)
                                else:
                                    rdve.wait(pe, f"Y{lv}{d}{g}", J)
                                for c in range(c0, c1):
                                    o = PS[:, b, (c - c0) * P:(c - c0 + 1) * P]
                                    if ph == "X":
                                        m = pe.transpose(o, XT[d][:, c], cst("ident"))
                                    elif ph == "Y":
                                        m = pe.matmul(o, LT[d][:, c], KX[d][:, c], start=True, stop=True)
                                    else:
                                        m = pe.matmul(o, BY[d][:, c], XT[d][:, c], start=True, stop=True)
                                rpe.done(m, f"{ph}{lv}{d}{g}")
                for d in range(2):
                    for g in range(3):
                        ract.wait(pe, f"Z64{d}{g}", J)
                pe.wait_ge(st_in, j * 16 + 16)
                now = lambda t: St_odd if t % 2 else St
                ybank = lambda t, i: i if t < 2 else 2 + i
                for t in range(8):
                    mine = chain_steps(t)
                    for i in mine:
                        d, cs = CHAINS[i]
                        if t:
                            rdve.wait(pe, f"S{t-1}{i}", J)
                            if t < 3:
                                rdve.wait(pe, f"y{t-1}{i}", J)
                        rpe.done(pe.matmul(PS[:, i, 0:P], QR[d][:, cs[t], 0:P], now(t)[:, i], start=True, stop=True), f"rhs{t}{i}")
                    for i in mine:
                        d, cs = CHAINS[i]
                        rdve.wait(pe, f"rhs{t}{i}", J)
                        rpe.done(pe.matmul(PS[:, i, 0:P], XT[d][:, cs[t]], RU[:, i], start=True, stop=True), f"U{t}{i}")
                    for i in mine:
                        d, cs = CHAINS[i]
                        ract.wait(pe, f"U{t}{i}", J)
                        rpe.done(pe.matmul(PS[:, 4 + i, 0:P], Btok[d][:, cs[t]], RU[:, i], start=True, stop=True), f"S{t}{i}")
                    for i in mine:
                        d, cs = CHAINS[i]
                        c = cs[t]
                        if t > 2:
                            rdve.wait(pe, f"y{t-1}{i}", J)
                        if t == 2:
                            rdve.wait(pe, f"y{t-1}{i+2}", J)
                        for h in range(2):
                            hs = slice(64 * h, 64 * h + 64)
                            yo = PS[hs, ybank(t, i), 128:128 + HD]
                            pe.matmul(yo, now(t)[:, i, hs], QR[d][:, c, P:192], start=True, stop=False)
                            m = pe.matmul(yo, RU[:, i, hs], Arb[d][:, c], start=False, stop=True)
                        rpe.done(m, f"y{t}{i}")
                rdve.wait(pe, "y71", J)
                rpe.done(two(0, cst("headmean"), T[4]), "mean")
                rdve.wait(pe, "ysq", J)
                rpe.done(two(2, cst("headmean"), T[3]), "var")
                rpe.next = 0
            rdve.wait(pe, "yg", KT)
            dense8(4, gk, "rout")
            if upto < 7: return
            norm(3)
            pe.wait_ge(norm_done, 64)
            pe.wait_ge(free["rout"], 3 + 8)
            for c in range(CH):
                for kt in range(KT):
                    m = pe.matmul(psf[:, c * NE:(c + 1) * NE], hn2[:, kt, c * P:(c + 1) * P], wrouter[:, kt, :],
                                  start=kt == 0, stop=kt == KT - 1)
            m.then_inc(logits_full, 1)
            for n in range(2 * CH):
                if n >= 5:
                    pe.wait_ge(hnt_ready, n - 4)
                c, half = n // 2, n % 2
                for t in range(4):
                    m = pe.transpose(PS[:, 3 + n % 5, t * P:(t + 1) * P], hn2[:, half * 4 + t, c * P:(c + 1) * P], cst("ident"))
                m.then_inc(hnt_t, 1)
            pe.wait_ge(onehot_ready, 1)
            oh = one_hot.rearrange("p c e -> p (c e)")
            pe.matmul(PS[:, 1, 0:CH * NE], cst("strict0"), oh, start=True, stop=False)
            for back in range(1, CH):
                pe.matmul(PS[:, 1, back * NE:CH * NE], cst("ones"), oh[:, 0:(CH - back) * NE], start=False, stop=back == CH - 1)
            for c in range(CH):
                m = pe.matmul(PS[:, 2, 0:NE], cst("ones"), one_hot[:, c], start=c == 0, stop=c == CH - 1)
            m.then_inc(counted, 1)
            n0 = slab_n["pe"]
            pe.wait_ge(routes_ready, 1)
            dense = pe.value_load(rows_i[0:1, 2 * CH:2 * CH + 1], min_val=0, max_val=1)
            with pe.If(dense):
                pe.wait_ge(hnt_ready, 2 * CH)
                pe.wait_ge(comb_ready, 1)
                for e in range(NE):
                    pe.wait_ge(free["cb"], e + 1)
                    for c in range(CH):
                        m = pe.matmul(acc(e % 3)[:, c * P:(c + 1) * P], comb_w[:, c, e:e + 1].to_broadcast([P, P]), cst("ident"),
                                      start=True, stop=True)
                    m.then_inc(cb_full, 1)
                pe.wait_ge(free["cb"], 3 + NE)
                with pe.Fori(0, NE) as e:
                    for k in range(15):
                        slot = (n0 + k) % RING
                        pe.wait_ge(slab_ready[slot], e * 80 + 16 * ((n0 + k) // RING + 1))
                        if k < ET:
                            w = ring[:, slot, 0:KT * 256].rearrange("p (kt n) -> p kt n", kt=KT)
                        else:
                            w = ring[:, slot, :].rearrange("p (kt n) -> p kt n", kt=ET)
                        for t in range(2):
                            tile = 2 * k + t
                            a = tile % 3
                            if k < ET:
                                if tile < 3:
                                    pe.wait_ge(free["moed"], e * 8 + (1 + tile))
                                elif tile % 2 == 0:
                                    pe.wait_ge(free["moeu"], e * ET + (tile - 4) // 2 + 1)
                                else:
                                    pe.wait_ge(free["moeg"], e * ET + (tile - 3) // 2 + 1)
                                m = mm_tile(pe, a, lambda kt: w[:, kt, t * P:(t + 1) * P], lambda kt, lo, hi: hn2[:, kt, lo:hi], KT)
                            else:
                                o = tile - 2 * ET
                                last = None
                                if o == 1:
                                    pe.wait_ge(free["moeg"], e * ET + ET)
                                elif o < 3:
                                    pe.wait_ge(free["moeu"], e * ET + (tile - 4) // 2 + 1)
                                if o == 0:
                                    pe.wait_ge(hid_ready, e * ET + ET - 1)
                                if o >= 3:
                                    pe.wait_ge(free["moed"], e * 8 + (o + 1))
                                if o == 0:
                                    last = lambda: pe.wait_ge(hid_ready, e * ET + ET)
                                m = mm_tile(pe, a, lambda kt: w[:, kt, t * P:(t + 1) * P], lambda kt, lo, hi: hid[:, kt, lo:hi], ET, last)
                            m.then_inc(tiles_done, 1)
            with pe.Else():
                with pe.Fori(0, NE) as e:
                    pe.wait_ge(xg_in, e * 32 + 32)
                    for i in range(4):
                        if i == 2:
                            pe.wait_ge(yo_dve, e * 4 + 2)
                        for t in range(2):
                            b0 = t * 256
                            kts = slice((2 * i + t) * P, (2 * i + t + 1) * P)
                            pe.transpose(PS[:, (1, 2, 6, 7)[i], b0:b0 + P], xg[:, 0, kts], cst("ident"))
                            m = pe.transpose(PS[:, (1, 2, 6, 7)[i], b0 + P:b0 + CAP], xg[0:CAP - P, 1, kts],
                                             cst("ident", slice(0, CAP - P))[:, 0:CAP - P])
                        m.then_inc(xg_t, 1)
                    for k in range(15):
                        slot = (n0 + k) % RING
                        pe.wait_ge(slab_ready[slot], e * 80 + 16 * ((n0 + k) // RING + 1))
                        if k < ET:
                            w = ring[:, slot, 0:KT * 256].rearrange("p (kt n) -> p kt n", kt=KT)
                            pe.wait_ge(pair_used, e * ET + (max(k - 3, 0) + 1))
                            for t in range(2):
                                for kt in range(KT):
                                    if k == 0 and t == 0 and kt % 2 == 0:
                                        pe.wait_ge(xe_dve if kt % 4 else xe_act, e * 2 + (kt // 4 + 1))
                                    m = pe.matmul(PS[:, k % 4, t * CAP:(t + 1) * CAP], w[:, kt, t * P:(t + 1) * P], xe[:, kt],
                                                  start=kt == 0, stop=kt == KT - 1)
                                m.then_inc(tiles_done, 1)
                        else:
                            w = ring[:, slot, :].rearrange("p (kt n) -> p kt n", kt=ET)
                            o = k - ET
                            pe.wait_ge(yo_act, e * 4 + (o + 1))
                            pe.wait_ge(yo_dve, e * 4 + (o + 1))
                            for rows in range(2):
                                n = (P, CAP - P)[rows]
                                for f in range(ET):
                                    if o == 0 and rows == 0 and f in (0, ET - 1):
                                        pe.wait_ge(pair_used, e * ET + (f and ET or ET - 1) + 1)
                                    m = pe.matmul(PS[0:n, 4 + 2 * rows + o % 2, 0:256], hide[:, f, rows * P:rows * P + n],
                                                  w[:, f, :], start=f == 0, stop=f == ET - 1)
                                m.then_inc(tiles_done, 1)
                for kt in range(KT):
                    if kt >= 3:
                        pe.wait_ge(outs_used, kt - 2)
                    for c in range(CH):
                        if kt == 0:
                            pe.wait_ge(combine, 2 * c + 2)
                        m = pe.transpose(acc(kt % 3)[:, c * P:(c + 1) * P], hnt[:, c, kt * P:(kt + 1) * P], cst("ident"))
                    m.then_inc(outs_t, 1)
            norm(4)

        @block.scalar
        def _(act):
            act.wait_ge(loaded, 64)
            act.activation(scond[:].rearrange("p a b -> p (a b)"), vcol("cond", 0, 2 * KT), ACT.Silu).then_inc(cond_ready, 1)

            def norm_a(n, buf):
                for kt in range(KT):
                    act.activation(buf[:, kt], x[:, kt], ACT.Square).then_inc(norm_sq, 1)
                act.wait_ge(norm_sum, n + 1)
                act.activation(rstd[:], stats, ACT.Sqrt, bias=cst("eps"), scale=1.0 / D).then_inc(norm_std, 1)

            def norm_b(n, buf, layer, which):
                for kt in range(KT):
                    act.wait_ge(norm_x, 8 * n + kt + 1)
                    for s, (lo, hi) in enumerate(HALVES):
                        act.activation(buf[:, kt, lo:hi], buf[:, kt, lo:hi], ACT.Identity,
                                       bias=mods[:, layer, 3 * which, kt, s:s + 1],
                                       scale=gs[:, layer, which, kt, s:s + 1]).then_inc(norm_done, 1)

            if upto < 2: return
            norm_a(0, hn)
            act.wait_ge(mods_ready, 1)
            norm_b(0, hn, 0, 0)
            act.sem_inc(free["in"], 3)

            def one(k, u):
                for t in range(2):
                    n = 2 * k + t if isinstance(k, int) else k * 2 + t
                    tile_done(act, "in", n)
                    zz = z[:, n] if isinstance(n, int) else z[:, bass.ds(n, 1)].rearrange("p a n -> p (a n)")
                    a0 = CONST["in_scale"][0]
                    sc = const[:, a0 + n:a0 + n + 1] if isinstance(n, int) else const[:, bass.ds(n + a0, 1)]
                    act.activation(zz, acc((2 * u + t) % 3), ACT.Identity, bias=b_in_col(n), scale=sc).then_inc(free["in"], 1)

            def b_in_col(n):
                return bs_in[:, n:n + 1] if isinstance(n, int) else bs_in[:, bass.ds(n, 1)]
            repeat(act, 13, one)
            if upto < 3: return
            act.wait_ge(free["in"], 3 + IN_TILES)
            act.wait_ge(zeroed, 2)
            for n, (c, kind) in enumerate(VK):
                mpe.wait(act, f"T{c}{kind}")
                dst = ktok[:, c] if kind == "k" else vaug[:, c, 4 * int(kind[1]):4 * int(kind[1]) + 4, 0:DV]
                src = PS[:, n % 6, :] if kind == "k" else PS[:, n % 6, :].rearrange("p (h n) -> p h n", h=4)
                mact.done(act.activation(dst, src, ACT.Copy), f"T{c}{kind}")
            R = slice(0, 64)
            mact.done(act.activation(tmp_row[R], gf[R], ACT.Abs), "absf")
            mact.wait(act, "absf")
            mact.done(act.activation(tmp_row[R], tmp_row[R], ACT.Exp, scale=-1.0), "expf")
            mact.wait(act, "expf")
            mact.done(act.activation(tmp_row[R], tmp_row[R], ACT.Ln, bias=1.0), "lnf")
            mdve.wait(act, "m11")
            mdve.wait(act, "g")
            mact.done(act.activation(gi[R], gf[R], ACT.Exp, scale=-1.0), "em")
            mdve.wait(act, "gend1")
            for c in range(CH):
                mact.done(act.activation(winter_r[R, c * P:(c + 1) * P], negG[R, c * P:(c + 1) * P], ACT.Exp,
                                         bias=mprev[R, c:c + 1]), f"winter{c}")
            for c in range(CH):
                mact.done(act.activation(ws_r[R, c * P:(c + 1) * P], g_row[R, c * P:(c + 1) * P], ACT.Exp,
                                         bias=gend[R, c:c + 1]), f"ws{c}")
            mact.done(act.activation(dec[R], dec[R], ACT.Exp), "dec")
            for n, (d, c) in enumerate(MGRP):
                for g in range(2):
                    mpe.wait(act, f"D{n}{g}")
                    if n:
                        mpe.wait(act, f"num{n-1}{g}")
                    mact.done(act.activation(Wt[:, g].rearrange("p h n -> p (h n)"), PS[:, 0, :], ACT.Exp), f"W{n}{g}")
            mact.done(act.activation(o_.rearrange("p a n -> p (a n)"), o_.rearrange("p a n -> p (a n)"), ACT.Sigmoid), "sigo")
            for c in range(CH):
                mdve.wait(act, f"ms{c}")
                mact.done(act.activation(ms, ms, ACT.Sqrt, bias=cst("eps"), scale=1.0 / DV), f"sd{c}")
            if upto < 4: return
            act.wait_ge(free["mout"], 3 + 8)
            act.wait_ge(states_out, 1)
            norm_a(1, hn_f)
            norm_b(1, hn_f, 0, 1)
            act.sem_inc(free["ffg"], 1)

            def ffg(k, u):
                tile_done(act, "ff", k * 2)
                act.activation(sg_f[:, u], acc((2 * u) % 3), ACT.Silu).then_inc(free["ffg"], 1)
            repeat(act, FT, ffg)
            if upto < 5: return
            act.wait_ge(free["ffd"], 3 + 8)
            norm_a(2, hn1)
            norm_b(2, hn1, 1, 0)
            act.sem_inc(free["rkv"], 3)

            def rk(i):
                for m in range(6):
                    t = i * 6 + m
                    u, w = m // 2, m % 2
                    tile_done(act, "rkv", t)
                    act.wait_ge(stored[m % 3], i * 32 + 16 * (m // 3 + 1))
                    act.activation(stage[:, m % 3], acc(m % 3), ACT.Copy).then_inc(free["rkv"], 1)
                    act.wait_ge(free["rkv"], t + (1 + 3))
                    act.dma_start(A["rkv_s"][bass.ds(i * 2 + w, 1), :, u, :].rearrange("a p n -> p (a n)"),
                                  stage[:, m % 3]).then_inc(stored[m % 3], 16)
            for s in stored:
                act.sem_inc(s, 16)
            with act.Fori(0, 4) as i:
                rk(i)
            act.sem_inc(free["lora"], 3)
            for t, fn in enumerate((ACT.Tanh, ACT.Copy, ACT.Sigmoid)):
                tile_done(act, "lora", t)
                act.activation(lhid[:, t], acc(t), fn).then_inc(free["lora"], 1)
            if upto < 6: return
            act.sem_inc(ract.sem, len(ract.names))
            with act.Fori(0, KT) as j:
                J = j + 1
                wide = lambda b: psf[:, b * 512:b * 512 + TOK]
                col = lambda t, k0: t[:, bass.ds(j + k0, 1)]
                rpe.wait(act, "w0", J)
                rdve.wait(act, "yb", j)
                ract.done(act.activation(T[5], wide(4), ACT.Tanh, bias=col(w0h, 0), scale=0.5), "thw0")
                rpe.wait(act, "a0", J)
                ract.done(act.activation(T[8], wide(6), ACT.Tanh, bias=col(w0h, 2 * KT), scale=0.5), "tha0")
                rdve.wait(act, "kmax", J)
                ract.done(act.activation(T[1], T[1], ACT.Ln, scale=2.0 ** 32), "knln")
                ract.wait(act, "knln", J)
                ract.done(act.activation(T[1], T[1], ACT.Exp, bias=cst("kk_back"), scale=-0.5), "knorm")
                rpe.wait(act, "gate", J)
                rdve.wait(act, "yg", j)
                ract.done(act.activation(T[2], wide(2), ACT.Copy), "gate")
                for g, (c0, c1) in enumerate(GR):
                    rpe.wait(act, f"V{g}", J)
                    ract.done(act.activation(Vbd[:, c0:c1].rearrange("p c n -> p (c n)"), PS[:, g, 0:(c1 - c0) * P], ACT.Copy), f"V{g}")

                def tokens(d):
                    for nm, dst, b0 in (("Kt", Ktok[d], 0), ("Bt", Btok[d], 3)):
                        for g, (c0, c1) in enumerate(GR):
                            rpe.wait(act, f"{nm}{d}{g}", J)
                            ract.done(act.activation(dst[:, c0:c1].rearrange("p c n -> p (c n)"), PS[:, b0 + g, 0:(c1 - c0) * P], ACT.Copy),
                                      f"{nm}{d}{g}")
                for d in range(2):
                    rdve.wait(act, f"ce{d}", J)
                    ract.done(act.activation(T[5], T[6], ACT.Exp), f"e1{d}")
                    ract.done(act.activation(T[6], T[6], ACT.Exp, scale=-1.0), f"e2{d}")
                    ract.done(act.activation(T[7], T[7], ACT.Exp), f"e3{d}")
                    ract.wait(act, f"e1{d}", J)
                    e1c = T[5].rearrange("p (c n) -> p c n", c=C64)
                    k = 63 if d == 0 else 0
                    ract.done(act.activation(pend[:, d].unsqueeze(2), e1c[:, :, k:k + 1], ACT.Copy), f"pend{d}")
                    if d == 0:
                        rpe.wait(act, "w1", J)
                        rdve.wait(act, "B10", J)
                        ract.wait(act, "pend0", J)
                        ract.done(act.activation(T[5], wide(4), ACT.Tanh, bias=col(w0h, KT), scale=0.5), "thw1")
                        rpe.wait(act, "a1", J)
                        ract.done(act.activation(T[8], wide(6), ACT.Tanh, bias=col(w0h, 3 * KT), scale=0.5), "tha1")
                    tokens(d)
                for d in range(2):
                    for g, (c0, c1) in enumerate(GR):
                        rpe.wait(act, f"MV{d}{g}", J)
                        ract.done(act.activation(MkT[d][:, c0:c1].rearrange("p c n -> p (c n)"), PS[:, g, 0:(c1 - c0) * P], ACT.Copy), f"MV{d}{g}")
                for lv in LEVELS:
                    for d in range(2):
                        for g, (c0, c1) in enumerate(GR):
                            rpe.wait(act, f"X{lv}{d}{g}", J)
                            ract.done(act.activation(KX[d][:, c0:c1].rearrange("p c n -> p (c n)"),
                                                     PS[:, d * 3 + g, 0:(c1 - c0) * P], ACT.Copy), f"X{lv}{d}{g}")
                    if lv == 64:
                        for d in range(2):
                            for g, (c0, c1) in enumerate(GR):
                                rpe.wait(act, f"Z64{d}{g}", J)
                                ract.done(act.activation(XT[d][:, c0:c1].rearrange("p c n -> p (c n)"),
                                                         PS[:, d * 3 + g, 0:(c1 - c0) * P], ACT.Copy), f"Z64{d}{g}")
                for t in range(8):
                    for i in chain_steps(t):
                        rpe.wait(act, f"U{t}{i}", J)
                        ract.done(act.activation(RU[:, i], PS[:, i, 0:P], ACT.Copy, scale=-1.0), f"U{t}{i}")
                rpe.wait(act, "var", J)
                ract.done(act.activation(T[3], wide(2), ACT.Ln, bias=cst("ln_eps")), "varln")
                ract.wait(act, "varln", J)
                ract.done(act.activation(T[3], T[3], ACT.Exp, scale=-0.5), "std")
                ract.next = 0
            if upto < 7: return
            act.wait_ge(free["rout"], 3 + 8)
            norm_a(3, hn2)
            norm_b(3, hn2, 1, 1)
            for n in range(2 * CH):
                act.wait_ge(hnt_t, n + 1)
                act.activation(hnt[:, n // 2, (n % 2) * 512:(n % 2) * 512 + 512], PS[:, 3 + n % 5, :], ACT.Copy).then_inc(hnt_ready, 1)
            act.wait_ge(exp_in, 1)
            act.activation(e12, e12, ACT.Exp).then_inc(exp_done, 1)
            act.wait_ge(routes_ready, 1)
            dense = act.value_load(rows_i[0:1, 2 * CH:2 * CH + 1], min_val=0, max_val=1)
            with act.If(dense):
                act.sem_inc(free["cb"], 3)
                for e in range(NE):
                    act.wait_ge(cb_full, e + 1)
                    act.activation(cb[:, e], acc(e % 3), ACT.Copy).then_inc(free["cb"], 1)
                with act.Fori(0, NE) as e:
                    for f in range(ET):
                        tile_done(act, "moe", e * 30 + 2 * f)
                        act.activation(sg[:, f % RING], acc((2 * f) % 3), ACT.Silu).then_inc(free["moeg"], 1)
            with act.Else():
                def rows_of(e, lo, hi):
                    if isinstance(e, int):
                        return A["rows"][e * CAP + lo:e * CAP + hi]
                    return A["rows"][bass.ds(e * CAP + lo, hi - lo)]

                def fetch(e):
                    act.dma_start(xg[:, 0], rows_of(e, 0, P)).then_inc(xg_in, 16)
                    act.dma_start(xg[0:CAP - P, 1], rows_of(e, P, CAP)).then_inc(xg_in, 16)

                credit(act, yo_act, 2)
                credit(act, yo_stored, 32)
                act.wait_ge(scattered, 16 * 2 * CH)
                fetch(0)

                def expert(e, last):
                    for i in (0, 2):
                        act.wait_ge(xg_t, e * 4 + (i + 1))
                        src = PS[:, (1, 2, 6, 7)[i], :].rearrange("p (t n) -> p t n", t=2)[:, :, 0:CAP]
                        act.activation(xe[:, 2 * i:2 * i + 2], src, ACT.Copy).then_inc(xe_act, 1)
                    if not last:
                        act.wait_ge(xg_t, e * 4 + 4)
                        fetch(e + 1)
                    for f in range(ET):
                        tile_done(act, "moe", e * 30 + (2 * f + 1))
                        act.activation(sge[:, f % 4], PS[:, f % 4, 0:CAP], ACT.Silu).then_inc(gate_done, 1)
                    for o in range(4):
                        tile_done(act, "moe", e * 30 + (2 * ET + 2 * o))
                        if o == 0:
                            act.wait_ge(yo_stored, e * 32 + 32)
                        act.activation(yo[:, 0, o * 256:(o + 1) * 256], PS[:, 4 + o % 2, 0:256], ACT.Copy).then_inc(yo_act, 1)
                    act.wait_ge(yo_act, e * 4 + 6)
                    act.dma_start(rows_of(e, 0, P), yo[:, 0]).then_inc(yo_stored, 16)
                    act.wait_ge(yo_dve, e * 4 + 6)
                    act.dma_start(rows_of(e, P, CAP), yo[0:CAP - P, 1]).then_inc(yo_stored, 16)
                with act.Fori(0, NE - 1) as e:
                    expert(e, False)
                expert(NE - 1, True)
            for kt in range(KT):
                act.wait_ge(x_done, kt + 1)
                act.activation(hn2[:, kt], x[:, kt], ACT.Square).then_inc(norm_sq, 1)
            act.wait_ge(norm_sum, 5)
            act.activation(rstd[:], stats, ACT.Sqrt, bias=cst("eps"), scale=1.0 / D).then_inc(norm_std, 1)

        @block.vector
        def _(dve):
            n_chain = [0]

            def link(ins):
                n_chain[0] += 1
                ins.then_inc(dve_chain, 1)
                dve.wait_ge(dve_chain, n_chain[0])

            dve.wait_ge(loaded, 64)
            link(dve.tensor_scalar(w0h[:], vcol("w0", 0, 4 * KT), 0.5, None, ALU.mult))
            link(dve.tensor_scalar(omka[:], vcol("k_a", 0, KT), -1.0, 1.0, ALU.mult, ALU.add))
            a0 = CONST["in_scale"][0]
            link(dve.tensor_tensor(bs_in[:], vcol("b_in", 0, IN_TILES), const[:, a0:a0 + IN_TILES], ALU.mult))
            tile_done(dve, "ada", 95)
            mf = mods[:].rearrange("p l k t s -> p (l k t) s")
            link(dve.tensor_tensor(mf, psf[:, 0:192].rearrange("p (n s) -> p n s", s=2),
                                   vcol("b_ada", 0, 96).unsqueeze(2).to_broadcast([P, 96, 2]), ALU.add))
            for la in range(2):
                for w in range(2):
                    g = vcol("gn1" if w == 0 else "gn2", la * KT, KT)
                    link(dve.tensor_scalar(gs[:, la, w], mods[:, la, 3 * w + 1], 1.0, None, ALU.add))
                    link(dve.tensor_tensor(gs[:, la, w], gs[:, la, w], g.unsqueeze(2).to_broadcast([P, KT, 2]), ALU.mult))
            dve.sem_inc(mods_ready, 1)

            def norm_v(n, buf):
                dve.wait_ge(norm_std, n + 1)
                dve.reciprocal(rstd[:], rstd[:]).then_inc(norm_rstd, 1)
                dve.wait_ge(norm_rstd, n + 1)
                for kt in range(KT):
                    dve.tensor_tensor(buf[:, kt], x[:, kt], rstd[:], ALU.mult).then_inc(norm_x, 1)

            def residual(name, a, t, layer, kind, n):
                tile_done(dve, name, n)
                return gated_add(a, t, layer, kind)

            def gated_add(a, t, layer, kind):
                for s, (lo, hi) in enumerate(HALVES):
                    xs = x[:, t, lo:hi] if isinstance(t, int) else x[:, bass.ds(t, 1), lo:hi].rearrange("p a n -> p (a n)")
                    if isinstance(t, int):
                        ga = mods[:, layer, kind, t, s:s + 1]
                    else:
                        ga = mods[:].rearrange("p l k t s -> p (l k t s)")[:, bass.ds(t * 2 + ((layer * NADA + kind) * KT * 2 + s), 1)]
                    i = dve.scalar_tensor_tensor(out=xs, in0=acc(a)[:, lo:hi], scalar=ga, in1=xs, op0=ALU.mult, op1=ALU.add)
                return i

            if upto < 2: return
            norm_v(0, hn)
            if upto < 3: return
            dve.wait_ge(zeroed, 2)
            dve.wait_ge(free["in"], 3 + IN_TILES)
            R = slice(0, 64)
            Z0, Z1 = slice(0, 32), slice(32, 64)
            mact.wait(dve, "lnf")
            mdve.done(dve.tensor_scalar(gf[R], gf[R], 0.0, None, ALU.min), "minf")
            mdve.wait(dve, "minf")
            mdve.done(dve.tensor_tensor(gf[R], gf[R], tmp_row[R], ALU.subtract), "lf")
            mdve.wait(dve, "lf")
            mr = cst("mreset")
            mdve.done(dve.tensor_tensor_scan(b_row[Z0], mr[Z0, 0:TOK], gf[Z0], 0.0, ALU.mult, ALU.add), "b0")
            mdve.done(dve.tensor_tensor_scan(b_row[Z1][:, ::-1], mr[Z1, 1:TOK + 1][:, ::-1], gf[Z1][:, ::-1], 0.0, ALU.mult, ALU.add), "b1")
            mdve.wait(dve, "b1")
            mdve.done(dve.tensor_tensor(g_row[R], gi[R], b_row[R], ALU.subtract), "g")
            m0 = vcol("m0", 0)
            Ls, Cs = slice(0, LAT), slice(LAT, TOK)
            mdve.done(dve.tensor_tensor_scan(gm[Z0, Ls], gf[Z0, Ls], gi[Z0, Ls], m0[Z0], ALU.add, ALU.max), "m00")
            mdve.done(dve.tensor_tensor_scan(gm[Z1, Ls][:, ::-1], gf[Z1, Ls][:, ::-1], gi[Z1, Ls][:, ::-1], m0[Z1], ALU.add, ALU.max), "m01")
            mdve.done(dve.tensor_tensor_scan(gm[Z0, Cs], gf[Z0, Cs], gi[Z0, Cs], 0.0, ALU.add, ALU.max), "m10")
            mdve.done(dve.tensor_tensor_scan(gm[Z1, Cs][:, ::-1], gf[Z1, Cs][:, ::-1], gi[Z1, Cs][:, ::-1], 0.0, ALU.add, ALU.max), "m11")
            mdve.wait(dve, "m11")
            mdve.done(dve.tensor_tensor(negG[R], b_row[R], gm[R], ALU.subtract), "negG")
            mdve.wait(dve, "negG")
            mch = gm[:, 0:TOK].rearrange("p (c n) -> p c n", c=CH)
            gch = negG[:, 0:TOK].rearrange("p (c n) -> p c n", c=CH)
            mp = mprev.unsqueeze(2)
            mdve.done(dve.tensor_copy(mp[Z0, 1:4], mch[Z0, 0:3, P - 1:P]), "mprev0")
            mdve.done(dve.tensor_copy(mp[Z1, 0:3], mch[Z1, 1:4, 0:1]), "mprev1")
            mdve.done(dve.tensor_copy(mprev[Z0, 0:1], m0[Z0]), "mprev2")
            mdve.done(dve.tensor_copy(mprev[Z1, 3:4], m0[Z1]), "mprev3")
            mdve.done(dve.memset(mprev[R, 4:5], 0.0), "mprev4")
            mdve.done(dve.tensor_copy(gend.unsqueeze(2)[Z0], gch[Z0, :, P - 1:P]), "mprev5")
            mdve.done(dve.tensor_copy(gend.unsqueeze(2)[Z1], gch[Z1, :, 0:1]), "gend0")
            mdve.wait(dve, "gend0")
            mdve.done(dve.tensor_tensor(dec[R], mprev[R], gend[R], ALU.add), "gend1")
            mact.wait(dve, "dec")
            mdve.done(dve.tensor_tensor(decx[R], cst("ident")[R, 0:64].unsqueeze(1).to_broadcast([64, CH, 64]),
                                        dec[R].unsqueeze(2).to_broadcast([64, CH, 64]), ALU.mult), "decx")
            cw = colw.rearrange("p c k r -> p (c k r)")
            mpe.wait(dve, "cols0")
            mdve.done(dve.tensor_copy(cw[:, 0:512], PS[:, 6, :]), "cols0")
            mpe.wait(dve, "cols1")
            mdve.done(dve.tensor_copy(cw[:, 512:960], PS[:, 7, 0:448]), "cols1")
            mpe.wait(dve, "decb")
            pd = PS[:, 0, 0:CH * 64].rearrange("p (c r) -> p c r", c=CH)
            n = 0
            for half in range(2):
                for d in range(2):
                    hp = slice(64 * half, 64 * half + 64)
                    mdve.done(dve.tensor_copy(decp[hp, :, d, :], pd[hp, :, d * 32 + half:d * 32 + half + 7:2]), f"decp{n}")
                    n += 1
            seen = set()
            for n, (d, c) in enumerate(MGRP):
                seq = 0 if c < 4 else 1
                for g in range(2):
                    mpe.wait(dve, f"S{n}{g}")
                    mact.wait(dve, f"W{n}{g}")
                    wf = Wt[:, g].rearrange("p h n -> p (h n)")
                    mdve.done(dve.tensor_tensor(wf, wf, PS[:, 1, :], ALU.mult), f"P{n}{g}")
                    mpe.wait(dve, f"num{n}{g}")
                    if n or g:
                        mdve.wait(dve, f"h{n}0" if g else f"h{n-1}1")
                    for h in range(4):
                        o = slice((h % 2) * 129, (h % 2) * 129 + 129)
                        row = d * 32 + 2 * h + g
                        i = dve.tensor_scalar(comb[:, h, :], PS[:, 4 + h // 2, o], colw[:, c, 0, row:row + 1], None, ALU.mult)
                        if h == 3:
                            i.then_inc(dve_chain, 1)
                            n_chain[0] += 1
                    dve.wait_ge(dve_chain, n_chain[0])
                    for b in range(2):
                        i = dve.tensor_tensor(comb[:, 2 * b:2 * b + 2, :], comb[:, 2 * b:2 * b + 2, :],
                                              PS[:, 2 + b, 0:258].rearrange("p (h n) -> p h n", h=2), ALU.add)
                    mdve.done(i, f"comb{n}{g}")
                    mdve.wait(dve, f"comb{n}{g}")
                    em = colw[:, c, 2, d * 32 + g:d * 32 + AH:2]
                    dn = comb[:, :, DV:DV + 1]
                    mdve.done(dve.scalar_tensor_tensor(out=rden.unsqueeze(2), in0=dn, scalar=-1.0, in1=dn,
                                                       op0=ALU.mult, op1=ALU.max), f"absd{n}{g}")
                    mdve.wait(dve, f"absd{n}{g}")
                    mdve.done(dve.tensor_tensor(rden, rden, em, ALU.max), f"den{n}{g}")
                    mdve.wait(dve, f"den{n}{g}")
                    mdve.done(dve.reciprocal(rden, rden), f"rden{n}{g}")
                    mdve.wait(dve, f"rden{n}{g}")
                    for h in range(4):
                        o = hs_t[:, c, (2 * h + g) * DV:(2 * h + g + 1) * DV]
                        if (c, g) in seen:
                            i = dve.scalar_tensor_tensor(out=o, in0=comb[:, h, 0:DV], scalar=rden[:, h:h + 1], in1=o,
                                                         op0=ALU.mult, op1=ALU.add)
                        else:
                            i = dve.tensor_scalar(o, comb[:, h, 0:DV], rden[:, h:h + 1], None, ALU.mult)
                    seen.add((c, g))
                    mdve.done(i, f"h{n}{g}")
                mpe.wait(dve, f"C{n}")
                for pair in range(4):
                    s = Cst[:, d, seq, pair * 129:(pair + 1) * 129]
                    i = dve.scalar_tensor_tensor(out=s, in0=s, scalar=decp[:, c, d, pair:pair + 1],
                                                 in1=PS[:, 6 + pair // 2, (pair % 2) * 129:(pair % 2) * 129 + 129],
                                                 op0=ALU.mult, op1=ALU.add)
                mdve.done(i, f"C{n}")
            for c in range(CH):
                mpool.wait(dve, f"sq{c}")
                if c:
                    mdve.wait(dve, f"hn{c-1}")
                mdve.done(dve.tensor_reduce(ms, sqt, AX.X, ALU.add), f"ms{c}")
                mact.wait(dve, f"sd{c}")
                mdve.done(dve.reciprocal(rs, ms), f"rs{c}")
                mdve.wait(dve, f"rs{c}")
                hh = hs_t[:, c].rearrange("p (h n) -> p h n", h=AH)
                mdve.done(dve.tensor_tensor(hh, hh, rs.unsqueeze(2).to_broadcast([P, AH, DV]), ALU.mult), f"hn{c}")
            mact.wait(dve, "sigo")
            for h in range(AH):
                mpe.wait(dve, f"hT{h}")
                mdve.done(dve.scalar_tensor_tensor(out=o_[:, h], in0=acc(h % 3), scalar=vcol("g_head", h), in1=o_[:, h],
                                                   op0=ALU.mult, op1=ALU.mult), f"mo{h}")
            dve.sem_inc(free["mout"], 3)
            for t in range(8):
                residual("mout", t % 3, t, 0, 2, t).then_inc(free["mout"], 1)
            if upto < 4: return
            norm_v(1, hn_f)
            dve.sem_inc(free["ffu"], 2)

            def ffu(k, u):
                tile_done(dve, "ff", k * 2 + 1)
                dve.wait_ge(free["ffg"], k + 2)
                h = hid_f[:, k] if isinstance(k, int) else hid_f[:, bass.ds(k, 1)].rearrange("p a n -> p (a n)")
                dve.tensor_tensor(h, sg_f[:, u], acc((2 * u + 1) % 3), ALU.mult).then_inc(free["ffu"], 1)
            repeat(dve, FT, ffu)
            dve.sem_inc(free["ffd"], 3)
            repeat(dve, 8, lambda k, u: residual("ffd", u % 3, k, 0, 5, k).then_inc(free["ffd"], 1))
            if upto < 5: return
            norm_v(2, hn1)
            dve.wait_ge(norm_done, 48)

            def grid(a, k0):
                return a[:, k0:k0 + 2, 0:LAT].rearrange("p k (r w) -> p k r w", w=64)
            sub, neg = [], []
            h0, s0 = grid(hn1, 0), grid(xx, 0)
            sub.append((s0[:, :, :, 1:], h0[:, :, :, :-1], h0[:, :, :, 1:])); neg.append((s0[:, :, :, 0:1], h0[:, :, :, 0:1]))
            h0, s0 = grid(hn1, 2), grid(xx, 2)
            sub.append((s0[:, :, :, :-1], h0[:, :, :, 1:], h0[:, :, :, :-1])); neg.append((s0[:, :, :, 63:64], h0[:, :, :, 63:64]))
            sub.append((xx[:, 4:6, 64:LAT], hn1[:, 4:6, 0:LAT - 64], hn1[:, 4:6, 64:LAT])); neg.append((xx[:, 4:6, 0:64], hn1[:, 4:6, 0:64]))
            sub.append((xx[:, 6:8, 0:LAT - 64], hn1[:, 6:8, 64:LAT], hn1[:, 6:8, 0:LAT - 64]))
            neg.append((xx[:, 6:8, LAT - 64:LAT], hn1[:, 6:8, LAT - 64:LAT]))
            sub.append((xx[:, 0:4, LAT + 1:TOK], hn1[:, 0:4, LAT:TOK - 1], hn1[:, 0:4, LAT + 1:TOK]))
            neg.append((xx[:, 0:4, LAT:LAT + 1], hn1[:, 0:4, LAT:LAT + 1]))
            sub.append((xx[:, 4:8, LAT:TOK - 1], hn1[:, 4:8, LAT + 1:TOK], hn1[:, 4:8, LAT:TOK - 1]))
            neg.append((xx[:, 4:8, TOK - 1:TOK], hn1[:, 4:8, TOK - 1:TOK]))
            for o, a, b in sub:
                dve.tensor_tensor(o, a, b, ALU.subtract).then_inc(xx_ready, 1)
            for o, a in neg:
                dve.tensor_scalar(o, a, -1.0, None, ALU.mult).then_inc(xx_ready, 1)
            dve.wait_ge(xx_ready, 12)
            for s in range(6):
                if s == 3:
                    tile_done(dve, "rkv", 23)
                for kt in range(KT):
                    i = dve.scalar_tensor_tensor(out=xm[s % 3][:, kt], in0=xx[:, kt], scalar=vcol("mu", s * KT + kt),
                                                 in1=hn1[:, kt], op0=ALU.mult, op1=ALU.add)
                i.then_inc(xm_ready, 1)
            if upto < 6: return
            dve.wait_ge(zero_set, 6)
            tile_done(dve, "lora", 2)
            tile_done(dve, "rkv", 23)
            dve.sem_inc(rdve.sem, len(rdve.names))
            I2 = cst("ident2").unsqueeze(1)
            with dve.Fori(0, KT) as j:
                J = j + 1
                vc = lambda name, k0=0: vec[:, bass.ds(j + (VEC[name][0] + k0), 1)]
                wide = lambda b: psf[:, b * 512:b * 512 + TOK]
                ch = lambda a: a.rearrange("p (c n) -> p c n", c=C64)
                W = lambda name, lap=J: rdve.wait(dve, name, lap)
                dve.wait_ge(rkv_in, j * 16 + 16)
                rr, kr, vv = rkv[:, 0], rkv[:, 1], rkv[:, 2]
                rdve.done(dve.tensor_scalar(T[0], kr, vc("k_k"), None, ALU.mult), "kk0")
                W("kk0")
                rdve.done(dve.tensor_tensor(T[1], T[0], T[0], ALU.mult), "sq")
                for h in range(2):
                    hp = slice(64 * h, 64 * h + 64)
                    rdve.done(dve.tensor_copy(BY[1][hp, :, 64 * h:64 * h + 64], ch(vv)[hp]), f"vT{h}")
                for d in range(2):
                    kd = T[3] if d == 0 else T[9]
                    ract.wait(dve, f"tha{d}", J)
                    rdve.done(dve.tensor_scalar(T[5], T[5], -DECAY / 2, -DECAY / 2, ALU.mult, ALU.add), f"lw{d}")
                    W(f"lw{d}")
                    rev = slice(None, None, -1) if d else slice(None)
                    rdve.done(dve.tensor_tensor_scan(T[6][:, rev], cst("reset")[:, d:d + TOK][:, rev], T[5][:, rev], 0.0,
                                                     ALU.mult, ALU.add), f"c{d}")
                    W(f"c{d}")
                    rdve.done(dve.tensor_tensor(T[7], T[6], T[5], ALU.subtract), f"ce{d}")
                    if d == 0:
                        rpe.wait(dve, "knorm", J)
                        rdve.done(dve.tensor_scalar(T[1], wide(0), 1e-24, None, ALU.max), "kmax")
                    rdve.done(dve.tensor_scalar(T[8], T[8], 0.5, 0.5, ALU.mult, ALU.add), f"a{d}")
                    W(f"a{d}")
                    rdve.done(dve.tensor_scalar(kd, T[8], vc("k_a"), omka[:, bass.ds(j, 1)], ALU.mult, ALU.add), f"f{d}")
                    W(f"f{d}")
                    rdve.done(dve.tensor_tensor(kd, kd, kr, ALU.mult), f"kd{d}")
                    if d == 0:
                        ract.wait(dve, "knorm", J)
                        rdve.done(dve.tensor_tensor(T[0], T[0], T[1], ALU.mult), "kk")
                    W("kk")
                    rdve.done(dve.tensor_tensor(T[8], T[8], T[0], ALU.mult), f"b{d}")
                    ract.wait(dve, f"e3{d}", J)
                    rdve.done(dve.tensor_tensor(QR[d][:, :, P:192], ch(rr), ch(T[5]), ALU.mult), f"R{d}")
                    W(f"b{d}")
                    if d:
                        rpe.wait(dve, "V2", J)
                    for nm, dst, a, b in (("Q", QR[d], T[0], T[7]), ("K", KX[d], kd, T[6]), ("B", BY[d], T[8], T[6])):
                        for h in range(2):
                            hp = slice(64 * h, 64 * h + 64)
                            rdve.done(dve.tensor_tensor(dst[hp, :, 64 * h:64 * h + 64], ch(a)[hp], ch(b)[hp], ALU.mult), f"{nm}{h}{d}")
                dve.wait_ge(st_loaded, j * 16 + 16)
                dve.memset(St[:, 2:4], 0.0)
                for d in range(2):
                    mst = cst(f"strict{d}").unsqueeze(1).to_broadcast([P, 2, P])
                    minc = cst(f"incl{d}").unsqueeze(1).to_broadcast([P, 2, HD])
                    for nm, M, Ar, banks in (("GK", MkT[d], Ark[d], (6, 7, 0, 1, 2)), ("GB", LT[d], Arb[d], (3, 4, 5, 6, 7))):
                        for q in range(5):
                            rpe.wait(dve, f"{nm}{d}{q}", J)
                            src = PS[:, banks[q], 0:384].rearrange("p (c n) -> p c n", c=2)
                            rdve.done(dve.tensor_tensor(M[:, 2 * q:2 * q + 2], src[:, :, 0:P], mst, ALU.mult),
                                      f"MkT{d}{q}" if nm == "GK" else f"LT{d}{q}")
                            rdve.done(dve.tensor_tensor(Ar[:, 2 * q:2 * q + 2], src[:, :, P:192], minc, ALU.mult),
                                      f"Ark{d}{q}" if nm == "GK" else f"Arb{d}{q}")
                W("LT14")
                rdve.done(dve.tensor_tensor(XT[1], LT[1], cst("nbd2").unsqueeze(1).to_broadcast([P, C64, P]), ALU.mult), "XTa1")
                W("XTa1")
                rdve.done(dve.tensor_tensor(XT[1], XT[1], cst("ident").unsqueeze(1).to_broadcast([P, C64, P]), ALU.add), "XT21")
                rdve.done(dve.tensor_tensor(T[3], T[3], T[9], ALU.add), "kds")
                ract.wait(dve, "pend1", J)
                rdve.done(dve.tensor_scalar(T[5], rr, vc("r_k"), None, ALU.mult), "rk")
                W("rk")
                rdve.done(dve.tensor_tensor(T[5], T[5], T[3], ALU.mult), "rkk")
                for d in range(2):
                    for g, (c0, c1) in enumerate(GR):
                        rpe.wait(dve, f"KV{d}{g}", J)
                        src = PS[:, 3 + g, 0:(c1 - c0) * P].rearrange("p (c n) -> p c n", n=P)
                        rdve.done(dve.tensor_tensor(Ktok[d][:, c0:c1], src, pend[:, d, c0:c1].unsqueeze(2).to_broadcast([P, c1 - c0, P]),
                                                    ALU.mult), f"KV{d}{g}")
                rpe.wait(dve, "bonus", J)
                rdve.done(dve.tensor_tensor(T[4], wide(6), vv, ALU.mult), "yb")
                W("yb")
                rpe.wait(dve, "yV", J)
                rdve.done(dve.tensor_tensor(T[4], T[4], wide(0), ALU.add), "y0")
                for lv in LEVELS:
                    for d in range(2):
                        for g, (c0, c1) in enumerate(GR):
                            rpe.wait(dve, f"Y{lv}{d}{g}", J)
                            src = PS[:, d * 3 + g, 0:(c1 - c0) * P].rearrange("p (c n) -> p c n", n=P)
                            rdve.done(dve.tensor_tensor(BY[d][:, c0:c1], I2.to_broadcast([P, c1 - c0, P]), src, ALU.subtract), f"Y{lv}{d}{g}")
                    if lv < 64:
                        for d in range(2):
                            for g, (c0, c1) in enumerate(GR):
                                rpe.wait(dve, f"Z{lv}{d}{g}", J)
                                src = PS[:, d * 3 + g, 0:(c1 - c0) * P].rearrange("p (c n) -> p c n", n=P)
                                rdve.done(dve.tensor_tensor(XT[d][:, c0:c1], src, cst(f"bd{lv}").unsqueeze(1).to_broadcast([P, c1 - c0, P]),
                                                            ALU.mult), f"Z{lv}{d}{g}")
                W("y0")
                for t in range(8):
                    mine = chain_steps(t)
                    for i in mine:
                        d, cs = CHAINS[i]
                        rpe.wait(dve, f"rhs{t}{i}", J)
                        rdve.done(dve.tensor_tensor(RU[:, i], PS[:, i, 0:P], MkT[d][:, cs[t]], ALU.add), f"rhs{t}{i}")
                    for i in mine:
                        d, cs = CHAINS[i]
                        rdve.done(dve.scalar_tensor_tensor(out=Sp[:, i], in0=(St, St_odd)[t % 2][:, i], scalar=pend[:, d, cs[t]:cs[t] + 1],
                                                           in1=Ktok[d][:, cs[t]], op0=ALU.mult, op1=ALU.add), f"Sp{t}{i}")
                    for i in mine:
                        d, cs = CHAINS[i]
                        W(f"Sp{t}{i}")
                        rpe.wait(dve, f"S{t}{i}", J)
                        rdve.done(dve.scalar_tensor_tensor(out=(St_odd, St)[t % 2][:, i], in0=PS[:, 4 + i, 0:P], scalar=pend[:, d, cs[t]:cs[t] + 1],
                                                           in1=Sp[:, i], op0=ALU.mult, op1=ALU.add), f"S{t}{i}")
                    for i in mine:
                        c = CHAINS[i][1][t]
                        ys = T[4][:, c * HD:(c + 1) * HD]
                        rpe.wait(dve, f"y{t}{i}", J)
                        rdve.done(dve.tensor_tensor(ys, ys, PS[:, i if t < 2 else 2 + i, 128:128 + HD], ALU.add), f"y{t}{i}")
                    W(f"y{t}{chain_steps(t)[-1]}")
                rpe.wait(dve, "mean", J)
                rdve.done(dve.tensor_tensor(T[1], T[4], wide(0), ALU.subtract), "yc")
                W("yc")
                rdve.done(dve.tensor_tensor(T[3], T[1], T[1], ALU.mult), "ysq")
                ract.wait(dve, "std", J)
                rdve.done(dve.tensor_tensor(T[1], T[1], T[3], ALU.mult), "yn")
                W("yn")
                rdve.done(dve.tensor_scalar(T[1], T[1], vc("ln_g"), vc("ln_b"), ALU.mult, ALU.add), "yl")
                W("yl")
                rdve.done(dve.tensor_tensor(gk[:, bass.ds(j, 1)].rearrange("p a n -> p (a n)"), T[1], T[2], ALU.mult), "yg")
                W("yg")
                rdve.next = 0
            dve.sem_inc(free["rout"], 3)
            for t in range(8):
                residual("rout", t % 3, t, 1, 2, t).then_inc(free["rout"], 1)
            if upto < 7: return
            norm_v(3, hn2)
            br = vcol("b_router", 0, NE)
            cd = cst("code").unsqueeze(1).to_broadcast([P, CH, NE])
            dve.wait_ge(logits_full, 1)
            link(dve.tensor_tensor(lg, psf[:, 0:CH * NE].rearrange("p (c e) -> p c e", c=CH),
                                   br.unsqueeze(1).to_broadcast([P, CH, NE]), ALU.add))
            wide_ = lambda a: a.unsqueeze(2).to_broadcast([P, CH, NE])

            def top(src, mx, oh):
                link(dve.tensor_reduce(mx, src, AX.X, ALU.max))
                link(dve.tensor_tensor(eq, src, wide_(mx), ALU.is_equal))
                link(dve.tensor_tensor(eq, eq, cd, ALU.mult))
                link(dve.tensor_reduce(e12, eq, AX.X, ALU.max))
                link(dve.tensor_tensor(oh, cd, wide_(e12), ALU.is_equal))
            top(lg, mx1, oh1)
            link(dve.tensor_scalar(l2g, oh1, NEG, None, ALU.mult))
            link(dve.tensor_tensor(l2g, l2g, lg, ALU.add))
            top(l2g, mx2, oh2)
            link(dve.tensor_tensor(one_hot, oh1, oh2, ALU.add))
            dve.sem_inc(onehot_ready, 1)
            link(dve.tensor_tensor(e12, mx2, mx1, ALU.subtract))
            dve.sem_inc(exp_in, 1)
            link(dve.tensor_scalar(eq, cd, float(-CAP), float(NE * CAP), ALU.mult, ALU.add))
            dve.wait_ge(counted, 1)
            link(dve.tensor_tensor(row_of, PS[:, 1, 0:CH * NE].rearrange("p (c e) -> p c e", c=CH), eq, ALU.add))
            for k, oh in enumerate((oh1, oh2)):
                link(dve.tensor_tensor(eq, oh, row_of, ALU.mult))
                link(dve.tensor_reduce(rows_f[:, k], eq, AX.X, ALU.add))
            link(dve.tensor_reduce(over, PS[:, 2, 0:NE], AX.X, ALU.max))
            link(dve.tensor_scalar(over, over, float(CAP), None, ALU.is_gt))
            link(dve.tensor_copy(rows_i[:, 0:2 * CH], rows_f.rearrange("p k c -> p (k c)")))
            link(dve.tensor_copy(rows_i[:, 2 * CH:2 * CH + 1], over))
            dve.sem_inc(routes_ready, 1)
            dve.wait_ge(exp_done, 1)
            link(dve.tensor_scalar(p1, e12, 1.0, None, ALU.add))
            link(dve.reciprocal(p1, p1))
            link(dve.tensor_tensor(p2, e12, p1, ALU.mult))
            dve.wait_ge(routes_ready, 1)
            dense = dve.value_load(rows_i[0:1, 2 * CH:2 * CH + 1], min_val=0, max_val=1)
            with dve.If(dense):
                link(dve.tensor_tensor(oh1, oh1, wide_(p1), ALU.mult))
                link(dve.tensor_tensor(oh2, oh2, wide_(p2), ALU.mult))
                dve.tensor_tensor(comb_w, oh1, oh2, ALU.add).then_inc(comb_ready, 1)
                dve.sem_inc(free["moed"], 3)
                with dve.Fori(0, NE) as e:
                    for f in range(ET):
                        tile_done(dve, "moe", e * 30 + (2 * f + 1))
                        dve.wait_ge(free["moeg"], e * ET + (f + 1))
                        dve.tensor_tensor(hid[:, f], sg[:, f % RING], acc((2 * f + 1) % 3), ALU.mult).then_inc(free["moeu"], 1)
                        dve.wait_ge(free["moeu"], e * ET + (f + 1))
                        dve.tensor_tensor(hid[:, f], hid[:, f], cb[:, bass.ds(e, 1)].rearrange("p a n -> p (a n)"),
                                          ALU.mult).then_inc(hid_ready, 1)
                    for o in range(8):
                        residual("moe", (2 * ET + o) % 3, o, 1, 5, e * 30 + (2 * ET + o)).then_inc(free["moed"], 1)
                dve.wait_ge(free["moed"], 3 + 8 * NE)
                dve.sem_inc(x_done, KT)
            with dve.Else():
                dve.sem_inc(pair_used, 1)
                credit(dve, yo_dve, 2)
                with dve.Fori(0, NE) as e:
                    for i in (1, 3):
                        dve.wait_ge(xg_t, e * 4 + (i + 1))
                        src = PS[:, (1, 2, 6, 7)[i], :].rearrange("p (t n) -> p t n", t=2)[:, :, 0:CAP]
                        dve.tensor_copy(xe[:, 2 * i:2 * i + 2], src).then_inc(xe_dve, 1)
                    for f in range(ET):
                        tile_done(dve, "moe", e * 30 + (2 * f + 1))
                        dve.wait_ge(gate_done, e * ET + (f + 1))
                        dve.tensor_tensor(hide[:, f], sge[:, f % 4], PS[:, f % 4, CAP:2 * CAP], ALU.mult).then_inc(pair_used, 1)
                    for o in range(4):
                        tile_done(dve, "moe", e * 30 + (2 * ET + 2 * o + 1))
                        if o == 0:
                            dve.wait_ge(yo_stored, e * 32 + 32)
                        dve.tensor_copy(yo[0:CAP - P, 1, o * 256:(o + 1) * 256], PS[0:CAP - P, 6 + o % 2, 0:256]).then_inc(yo_dve, 1)
                for c in range(CH):
                    dve.wait_ge(gathered[c], 32)
                    dve.tensor_scalar(hnt[:, c], hnt[:, c], p1[:, c:c + 1], None, ALU.mult).then_inc(combine, 1)
                    dve.wait_ge(combine, 2 * c + 1)
                    dve.scalar_tensor_tensor(out=hnt[:, c], in0=out2[:, c], scalar=p2[:, c:c + 1], in1=hnt[:, c],
                                             op0=ALU.mult, op1=ALU.add).then_inc(combine, 1)
                for kt in range(KT):
                    dve.wait_ge(outs_t, kt + 1)
                    gated_add(kt % 3, kt, 1, 5).then_inc(outs_used, 1)
                    dve.wait_ge(outs_used, kt + 1)
                    dve.sem_inc(x_done, 1)
            dve.wait_ge(norm_std, 5)
            dve.reciprocal(rstd[:], rstd[:]).then_inc(norm_rstd, 1)
            dve.wait_ge(norm_rstd, 5)
            for kt in range(KT):
                dve.scalar_tensor_tensor(out=hn2[:, kt], in0=x[:, kt], scalar=vcol("gf", kt), in1=rstd[:],
                                         op0=ALU.mult, op1=ALU.mult).then_inc(y_ready, 1)
    return nc


def constants():
    c = np.zeros((P, N_CONST), np.float32)
    p, f = np.arange(P)[:, None], np.arange(P)[None, :]

    def put(name, v):
        a, w = CONST[name]
        c[:, a:a + w] = v
    eye = (p == f)
    put("ident", eye)
    put("ident2", 2 * eye)
    put("ones", 1)
    same = (p // HD == f // HD)
    put("headones", same)
    put("headmean", same / HD)
    put("neg0", np.where(p <= f, 0, NEG))
    put("neg1", np.where(p >= f, 0, NEG))
    put("strict0", p < f)
    put("strict1", p > f)
    put("incl0", (p % HD) <= f[:, :HD])
    put("incl1", (p % HD) >= f[:, :HD])
    put("kk_back", 16 * np.log(2))
    put("nbd2", -1.0 * (p // 2 == f // 2))
    for b in (4, 8, 16, 32):
        put(f"bd{b}", p // b == f // b)
    t = np.arange(TOK + 1)[None, :]
    put("reset", t % HD != 0)
    put("mreset", t % P != 0)
    s = np.ones(IN_TILES)
    s[4:8] = DK ** -0.5
    put("in_scale", s)
    put("eps", EPS)
    put("ln_eps", LN_EPS)
    put("code", np.arange(NE, 0, -1))
    return c


def slab8(w):
    n = w.shape[1] // 256
    return w.reshape(KT, P, n, 256).transpose(2, 1, 0, 3).reshape(n, P, KT * 256)


def feat(v):
    return v.reshape(-1, P).T


def layout(i):
    a = {k: np.asarray(v) for k, v in i.items()}
    out = {}
    xs = np.concatenate([a["x_sample"][0], a["x_prompt"][0]])
    out["x"] = np.ascontiguousarray(xs.T.reshape(KT, P, TOK).transpose(1, 0, 2))
    win, bin_ = a["w_m_in"][0], a["b_m_in"][0]
    wi, bi = np.zeros((D, IN_TILES * P), np.float32), np.zeros(IN_TILES * P, np.float32)
    wi[:, :3072], bi[:3072] = win[:, :3072], bin_[:3072]
    for kind in range(2):
        for d in range(2):
            src = 3072 + kind * 16 + d * AH
            dst = (24 + kind) * P + d * 32
            wi[:, dst:dst + AH], bi[dst:dst + AH] = win[:, src:src + AH], bin_[src:src + AH]
    gu = a["w_ff_gu"][0].reshape(D, 2, FT, P).transpose(0, 2, 1, 3).reshape(D, 2 * DFF)
    rkv = a["w_rkv"][0].reshape(3, D, 4, 256).transpose(1, 2, 0, 3).reshape(D, 12 * 256)
    lo = np.zeros((D, 512), np.float32)
    lo[:, 0:64], lo[:, 64:128] = a["w_decay1"][0, 0], a["w_decay1"][0, 1]
    lo[:, 128:192], lo[:, 192:256] = a["w_iclr1"][0, 0], a["w_iclr1"][0, 1]
    lo[:, 256:384] = a["w_gate1"][0]
    eg = a["w_exp_gu"][0].reshape(NE, D, 2, ET, P).transpose(0, 1, 3, 2, 4).reshape(NE, D, 2 * ET * P)
    out["k8"] = np.concatenate([slab8(a["w_ada"][0]), slab8(a["w_ada"][1]), slab8(wi), slab8(a["w_m_out"][0]), slab8(gu),
                                slab8(rkv), slab8(lo), slab8(a["w_rwkv_out"][0])] + [slab8(eg[e]) for e in range(NE)])
    out["ffd"] = np.ascontiguousarray(a["w_ff_down"][0].reshape(FT, P, 8, P).transpose(2, 1, 0, 3).reshape(8, P, SLAB))
    out["exd"] = np.ascontiguousarray(a["w_exp_down"][0].reshape(NE, ET, P, 4, 256).transpose(0, 3, 2, 1, 4).reshape(NE * 4, P, SLAB))
    out["wrouter"] = np.ascontiguousarray(a["w_router"][0].reshape(KT, P, NE).transpose(1, 0, 2))
    l2 = np.stack([a["w_decay2"][0].reshape(P, D), a["w_iclr2"][0].reshape(P, D), a["w_gate2"][0]])
    out["l2"] = np.ascontiguousarray(l2.reshape(3, P, KT, P).transpose(2, 1, 0, 3))
    C0 = np.concatenate([a["state_mlstm_C"][0, 0], a["state_mlstm_n"][0, 0][..., None]], -1)
    out["C0"] = np.ascontiguousarray(C0.reshape(2, 4, 2, DK, DV + 1).transpose(2, 3, 0, 1, 4).reshape(P, 2, 4 * (DV + 1)))
    S = a["state_rwkv_S"][0, 0].reshape(2, KT, 2, HD, HD)
    S0 = np.zeros((KT, P, 2, P), np.float32)
    for h in range(2):
        S0[:, h * HD:(h + 1) * HD, :, h * HD:(h + 1) * HD] = S[:, :, h].transpose(1, 3, 0, 2)
    out["S0"] = S0
    v = np.zeros((P, N_VEC), np.float32)

    def put(name, val):
        at, w = VEC[name]
        v[:, at:at + w] = val
    put("cond", np.stack([feat(a["c"][0]), feat(a["c_ctx"])], -1).reshape(P, 2 * KT))
    for name, key in (("b_ada", "b_ada"), ("gn1", "g_norm1"), ("gn2", "g_norm2"), ("gf", "g_final"), ("g_head", "g_m_head"),
                      ("mu", "mu_rwkv"), ("w0", "w_decay0"), ("a0", "w_iclr0"), ("k_k", "k_k"), ("k_a", "k_a"),
                      ("r_k", "r_k"), ("ln_g", "g_ln_x"), ("ln_b", "b_ln_x")):
        put(name, feat(a[key]))
    put("b_in", feat(bi))
    put("b_router", a["b_router"][0][None, :])
    at = VEC["m0"][0]
    v[0:AH, at], v[32:32 + AH, at] = a["state_mlstm_m"][0, 0, 0], a["state_mlstm_m"][0, 0, 1]
    out["vec"] = v
    out["const"] = constants()
    return out


OUTS = {"y": (P, KT, TOK), "C_out": (P, 2, 4 * (DV + 1)), "m_out": (64, 1), "S_out": (KT, P, 2, P)}


def restore(r):
    y = r["y"].transpose(1, 0, 2).reshape(D, TOK).T
    C = r["C_out"].reshape(2, DK, 2, 4, DV + 1).transpose(2, 3, 0, 1, 4).reshape(2, AH, DK, DV + 1)
    m = r["m_out"][:, 0].reshape(2, 32)[:, :AH]
    S = np.zeros((2, KT, 2, HD, HD), np.float32)
    for h in range(2):
        S[:, :, h] = r["S_out"][:, h * HD:(h + 1) * HD, :, h * HD:(h + 1) * HD].transpose(2, 0, 3, 1)
    c = np.ascontiguousarray
    return (c(y[LAT:][None]), c(y[:LAT][None]), c(C[None, None, ..., :DV]), c(C[None, None, ..., DV]), c(m[None, None]),
            c(S.reshape(1, 1, 2, BH, HD, HD)))


def declare(nc, arrays):
    A = {n: nc.dram_tensor(f"in_{n}", a.shape, F32, kind="ExternalInput").ap() for n, a in arrays.items()}
    A.update({n: nc.dram_tensor(n, s, F32, kind="ExternalOutput").ap() for n, s in OUTS.items()})
    A["rows"] = nc.dram_tensor("expert_rows", (NE * CAP, D), F32, kind="Internal").ap()
    A["rkv_s"] = nc.dram_tensor("rkv_s", (KT, P, 3, TOK), F32, kind="Internal").ap()
    return A


def kernel(**inputs):
    import concourse.bacc as bacc
    from concourse.bass_utils import run_bass_kernel_spmd

    arrays = layout(inputs)
    nc = bacc.Bacc("TRN2", target_bir_lowering=False, num_devices=1)
    build(nc, declare(nc, arrays))
    r = run_bass_kernel_spmd(nc, [{f"in_{n}": v for n, v in arrays.items()}], core_ids=[0])
    return restore(r.results[0])
```

```python
from contextlib import ExitStack

import numpy as np

import concourse.bass as bass
from concourse import mybir

F32 = mybir.dt.float32
ALU = mybir.AluOpType
ACT = mybir.ActivationFunctionType
AX = mybir.AxisListType

P = 128
D = 1024
KT = D // P
LAT, CTX = 512, 128
TOK = LAT + CTX
HALVES = ((0, LAT), (LAT, TOK))
NADA = 6
EPS = 1e-6
AH, DK, DV = 8, 64, 128
CH = TOK // P
BH, HD = 16, 64
C64 = TOK // HD
DECAY = 0.606531
LN_EPS = 64e-5
DFF = 2816
FT = DFF // P
NE = 8
ET = DFF // 2 // P
IN_TILES = 26
CAP = 192
RING = 3
ADA_SLOTS = 4
SLAB = 22 * P
NEG = -1e30

CONST = {}
_at = 0
for _name, _w in (("ident", 128), ("ident2", 128), ("ones", 128), ("headones", 128), ("headmean", 128),
                  ("neg0", 128), ("neg1", 128), ("strict0", 128), ("strict1", 128), ("incl0", 64), ("incl1", 64),
                  ("bd4", 128), ("bd8", 128), ("bd16", 128), ("bd32", 128),
                  ("reset", TOK + 1), ("mreset", TOK + 1), ("in_scale", IN_TILES), ("eps", 1), ("ln_eps", 1), ("kk_back", 1), ("nbd2", 128), ("code", NE)):
    CONST[_name] = (_at, _w)
    _at += _w
N_CONST = _at
VEC = {}
_at = 0
for _name, _w in (("cond", KT * 2), ("b_ada", 2 * NADA * KT), ("gn1", 2 * KT), ("gn2", 2 * KT), ("gf", KT),
                  ("b_in", IN_TILES), ("g_head", KT), ("mu", 6 * KT), ("w0", 2 * KT), ("a0", 2 * KT),
                  ("k_k", KT), ("k_a", KT), ("r_k", KT), ("ln_g", KT), ("ln_b", KT), ("b_router", NE), ("m0", 1)):
    VEC[_name] = (_at, _w)
    _at += _w
N_VEC = _at


class Steps:

    def __init__(self, sem, names):
        self.sem, self.names, self.at = sem, names, {n: k + 1 for k, n in enumerate(names)}
        assert len(self.at) == len(names)
        self.next = 0

    def done(self, ins, name):
        assert self.names[self.next] == name, (self.names[self.next], name)
        self.next += 1
        ins.then_inc(self.sem, 1)

    def wait(self, eng, name, lap=0):
        eng.wait_ge(self.sem, lap * len(self.names) + self.at[name])


def repeat(eng, count, body):
    laps = count // RING if count >= 2 * RING else 0
    if laps:
        with eng.Fori(0, laps) as i:
            for u in range(RING):
                body(i * RING + u, u, i)
    for k in range(laps * RING, count):
        body(k, k % RING, k // RING)


MGRP = [(0, 0), (1, 3), (0, 1), (1, 2), (0, 2), (1, 1), (0, 3), (1, 0), (0, 4), (1, 4)]
VK = [(c, kind) for c in range(CH) for kind in ("v0", "v1", "k")]


def mlstm_steps():
    pe, act, dve, pool = [], [], [], []
    pe += [f"T{c}{k}" for c, k in VK]
    act += [f"T{c}{k}" for c, k in VK]
    act += ["absf", "expf", "lnf", "em"] + [f"winter{c}" for c in range(CH)] + [f"ws{c}" for c in range(CH)] + ["dec"]
    dve += ["minf", "lf", "b0", "b1", "g", "m00", "m01", "m10", "m11", "negG"]
    dve += [f"mprev{k}" for k in range(6)] + [f"gend{k}" for k in range(2)] + ["decx"]
    pe += ["cols0", "cols1", "decb"]
    dve += ["cols0", "cols1"] + [f"decp{k}" for k in range(4)]
    for n, (d, c) in enumerate(MGRP):
        pool += [f"kw{n}"]
        for g in range(2):
            pe += [f"D{n}{g}", f"S{n}{g}"]
            act += [f"W{n}{g}"]
            dve += [f"P{n}{g}"]
            pe += [f"num{n}{g}"]
            dve += [f"comb{n}{g}", f"absd{n}{g}", f"den{n}{g}", f"rden{n}{g}", f"h{n}{g}"]
        pe += [f"C{n}"]
        dve += [f"C{n}"]
    act += ["sigo"] + [f"sq{c}" for c in range(CH)] + ["sd"]
    dve += [f"ms{c}" for c in range(CH)] + ["rs", "hn0", "hn2", "hn4"]
    pool += ["hn1", "hn3"]
    for h in range(AH):
        pe += [f"hT{h}"]
        dve += [f"mo{h}"]
    return pe, act, dve, pool


LEVELS = (4, 8, 16, 32, 64)
GR = ((0, 4), (4, 8), (8, 10))
CHAINS = ((0, tuple(range(8))), (1, tuple(range(7, -1, -1))), (0, (8, 9)), (1, (9, 8)))


def chain_steps(t):
    return [i for i in range(4) if t < len(CHAINS[i][1])]


RWKV_HEAD = (("w0", "a0", "knorm"), ("sq", "thw0", "tha0"), ("kk0", "vT0", "vT1", "lw0", "c0", "ce0", "kmax"))


def rwkv_steps():
    pe, act, dve, pool = [], [], [], []
    pe += ["gate", "V0", "V1", "V2", "w1", "a1"]
    act += ["knln", "knorm", "gate", "V0", "V1", "V2"]
    for d in range(2):
        dve += ["lw1", "c1", "ce1"] if d else []
        dve += [f"a{d}", f"f{d}", f"kd{d}"]
        act += [f"e1{d}", f"e2{d}", f"e3{d}", f"pend{d}"]
        if d == 0:
            dve += ["kk"]
            act += ["thw1", "tha1"]
        dve += [f"b{d}", f"R{d}"] + [f"{x}{h}{d}" for x in "QKB" for h in range(2)]
        pe += [f"Kt{d}{g}" for g in range(3)] + [f"Bt{d}{g}" for g in range(3)]
        act += [f"Kt{d}{g}" for g in range(3)] + [f"Bt{d}{g}" for g in range(3)]
        pe += [f"GK{d}{q}" for q in range(5)] + [f"GB{d}{q}" for q in range(5)]
    for d in range(2):
        for q in range(5):
            dve += [f"MkT{d}{q}", f"Ark{d}{q}"]
        for q in range(5):
            dve += [f"LT{d}{q}", f"Arb{d}{q}"]
    dve += ["XTa1", "XT21", "kds", "rk", "rkk"]
    pool += ["XTa0", "XT20", "LTI0", "Ark", "LTI1"]
    for d in range(2):
        pe += [f"MV{d}{g}" for g in range(3)] + [f"KV{d}{g}" for g in range(3)]
        act += [f"MV{d}{g}" for g in range(3)]
        dve += [f"KV{d}{g}" for g in range(3)]
    pe += ["bonus", "yV"]
    dve += ["yb", "y0"]
    for lv in LEVELS:
        for ph in ("X", "Y", "Z"):
            for d in range(2):
                for g in range(3):
                    pe += [f"{ph}{lv}{d}{g}"]
                    (act if ph == "X" or (ph == "Z" and lv == 64) else dve).append(f"{ph}{lv}{d}{g}")
    for t in range(8):
        mine = chain_steps(t)
        pe += [f"rhs{t}{i}" for i in mine] + [f"U{t}{i}" for i in mine] + [f"S{t}{i}" for i in mine] + [f"y{t}{i}" for i in mine]
        dve += [f"rhs{t}{i}" for i in mine] + [f"Sp{t}{i}" for i in mine] + [f"S{t}{i}" for i in mine] + [f"y{t}{i}" for i in mine]
        act += [f"U{t}{i}" for i in mine]
    pe += ["mean", "var"]
    dve += ["yc", "yn", "yl", "yg"]
    act += ["ysq", "varln", "std"]
    return pe, act, dve, pool


def build(nc, A):
    with ExitStack() as ctx:
        def sb(name, shape, dtype=F32):
            return ctx.enter_context(nc.sbuf_tensor(name, shape, dtype))

        def sem(name):
            return ctx.enter_context(nc.semaphore(name))

        x = sb("x", [P, KT, TOK])
        ring = sb("ring", [P, RING, SLAB])
        const = sb("const", [P, N_CONST])
        vec = sb("vec", [P, N_VEC])
        wrouter = sb("wrouter", [P, KT, NE])
        scond = sb("scond", [P, KT, 32])
        mods = sb("mods", [P, 2, NADA, KT, 2])
        gs = sb("gs", [P, 2, 2, KT, 2])
        w0h = sb("w0h", [P, 2 * 2 * KT])
        omka = sb("omka", [P, KT])
        bs_in = sb("bs_in", [P, IN_TILES])
        rstd = sb("rstd", [P, TOK])
        NA = 34400
        arena = sb("arena", [P, NA])
        PS = ctx.enter_context(nc.psum_tensor("PS", [P, 8, 512], F32))
        psf = PS[:].rearrange("p b n -> p (b n)")

        def cst(name, rows=slice(0, P)):
            a, w = CONST[name]
            return const[rows, a:a + w]

        def vcol(name, k, n=1):
            a, _ = VEC[name]
            if isinstance(k, int):
                return vec[:, a + k:a + k + n]
            return vec[:, bass.ds(k + a, n)]

        class Region:
            def __init__(self):
                self.at = 0

            def __call__(self, *shape):
                n = int(np.prod(shape))
                v = arena[:, self.at:self.at + n]
                self.at += n
                assert self.at <= NA, self.at
                if len(shape) == 2:
                    v = v.rearrange("p (a b) -> p a b", a=shape[0])
                if len(shape) == 3:
                    v = v.rearrange("p (a b c) -> p a b c", a=shape[0], b=shape[1])
                if len(shape) == 4:
                    v = v.rearrange("p (a b c d) -> p a b c d", a=shape[0], b=shape[1], c=shape[2])
                return v

        def acc(k):
            return psf[:, k * 1024:k * 1024 + TOK]

        stats = psf[:, 3072:3072 + TOK]

        r = Region()
        hn = r(KT, TOK)
        z = r(IN_TILES, TOK)
        vaug_at = r.at
        vaug = r(CH, AH, DV + 1)
        ktok = r(CH, AH * DK)
        colw = r(CH, 3, 64)
        mprev, gend, dec = r(CH), r(CH), r(CH)
        decx = r(CH, 64)
        decp = r(CH, 2, 4)
        winter_r, ws_r = r(TOK), r(TOK)
        smalls = r(64)
        g_row, negG = r(TOK), r(TOK)
        tmp_row, b_row = winter_r, ws_r
        hs_t = hn.rearrange("p a b -> p (a b)").rearrange("p (c f) -> p c f", c=CH)
        q_, k_ = z[:, 0:4], z[:, 4:8]
        v_, o_ = z[:, 8:16], z[:, 16:24]
        gi, gf = z[:, 24], z[:, 25]
        gm = gf
        vr = z[:, 8:16].rearrange("p a b -> p (a b)")
        Wt = vr[:, 0:1024].rearrange("p (a h n) -> p a h n", a=2, h=4)
        kw = vr[:, 1024:2048].rearrange("p (a n) -> p a n", a=2)
        comb = vr[:, 2048:2048 + 516].rearrange("p (h n) -> p h n", h=4)
        Cst = vr[:, 2564:2564 + 2064].rearrange("p (d s n) -> p d s n", d=2, s=2)
        rden = smalls[:, 0:4]
        ms = smalls[:, 8:8 + CH * AH].rearrange("p (c h) -> p c h", c=CH)
        sqt = [vr[:, a * 1024:a * 1024 + 1024].rearrange("p (h n) -> p h n", h=AH) for a in range(2)]

        ada_region = arena[:, vaug_at:NA - 3 * D]
        ada_slab = [ada_region[:, k * KT * 256:(k + 1) * KT * 256].rearrange("p (kt n) -> p kt n", kt=KT) for k in range(ADA_SLOTS)]
        ada_rows = ada_region[:, ADA_SLOTS * KT * 256:][:, 0:3 * 256].rearrange("p (g n) -> p g n", g=3)

        r = Region()
        hn_f = r(KT, TOK)
        hid_f = r(FT, TOK)
        sg_f = r(RING, TOK)

        r = Region()
        QR = [r(C64, 192) for _ in range(2)]
        KX = [r(C64, P) for _ in range(2)]
        BY = [r(C64, P) for _ in range(2)]
        Ktok = [r(C64, P) for _ in range(2)]
        Btok = [r(C64, P) for _ in range(2)]
        MkT = [r(C64, P) for _ in range(2)]
        Ark = [r(C64, HD) for _ in range(2)]
        Arb = [r(C64, HD) for _ in range(2)]
        LT = [r(C64, P) for _ in range(2)]
        XT = [r(C64, P) for _ in range(2)]
        Vbd = r(C64, P)
        St = r(4, P)
        RU = r(4, P)
        pend = r(2, C64)
        split = r.at
        lhid = r(3, TOK)
        l2 = r(3, P)
        gk = r(KT, TOK)
        tr = ring[:].rearrange("p a b -> p (a b)")
        T = [tr[:, n * TOK:(n + 1) * TOK] for n in range(10)]
        Sp, St_odd = (T[n][:, 0:4 * P].rearrange("p (i n) -> p i n", i=4) for n in (6, 7))
        rkv = tr[:, 10 * TOK:13 * TOK].rearrange("p (s n) -> p s n", s=3)
        r = Region()
        hn1 = r(KT, TOK)
        xx = r(KT, TOK)
        xm = [r(KT, TOK) for _ in range(3)]
        stage = gk[:, 0:3]
        assert r.at <= split, (r.at, split)

        r = Region()
        hn2 = r(KT, TOK)
        lg = r(CH, NE)
        eq = r(CH, NE)
        oh1, oh2, l2g, comb_w = r(CH, NE), r(CH, NE), r(CH, NE), r(CH, NE)
        one_hot, row_of = r(CH, NE), r(CH, NE)
        mx1, mx2, e12, p1, p2 = r(CH), r(CH), r(CH), r(CH), r(CH)
        rows_f, over = r(2, CH), r(1)
        logit_rows = r(TOK)
        routed = r.at
        cb = r(NE, TOK)
        hid = r(ET, TOK)
        sg = r(RING, TOK)
        r.at = routed
        hnt = r(CH, D)
        out2 = r(CH, D)
        xg = r(2, D)
        yo = r(2, D)
        xe = r(KT, CAP)
        hide = r(ET, CAP)
        yf = r(KT, CAP)
        sge = r(4, CAP)
        rows_i = sb("rows_i", [P, 2 * CH + 1], mybir.dt.int32)

        loaded = sem("loaded")
        slab_ready = [sem(f"slab_ready{k}") for k in range(RING)]
        tiles_done = sem("tiles_done")
        cond_ready = sem("cond_ready")
        cond_zero = sem("cond_zero")
        ada_slab_ready = [sem(f"ada_slab_ready{k}") for k in range(ADA_SLOTS)]
        ada_used, ada_copied, ada_t, ada_done = sem("ada_used"), sem("ada_copied"), sem("ada_t"), sem("ada_done")
        norm_add, norm_ln = sem("norm_add"), sem("norm_ln")
        mods_ready = sem("mods_ready")
        dve_chain = sem("dve_chain")
        norm_sq, norm_sum, norm_std = sem("norm_sq"), sem("norm_sum"), sem("norm_std")
        norm_x, norm_done = sem("norm_x"), sem("norm_done")
        cb_full = sem("cb_full")
        free = {n: sem(f"{n}_free") for n in ("in", "mout", "ffg", "ffu", "ffd", "rkv", "lora", "rout", "cb",
                                              "moeg", "moeu", "moed")}
        state_loaded = sem("state_loaded")
        ones_set = sem("ones_set")
        zero_set = sem("zero_set")
        st_loaded = sem("st_loaded")
        mpe, mact, mdve, mpool = (Steps(sem(f"mlstm_{n}"), s) for n, s in zip(("pe", "act", "dve", "pool"), mlstm_steps()))
        rpe, ract, rdve, rpool = (Steps(sem(f"rwkv_{n}"), s) for n, s in zip(("pe", "act", "dve", "pool"), rwkv_steps()))
        hpe, hact, hdve = (Steps(sem(f"rwkv_head_{n}"), s) for n, s in zip(("pe", "act", "dve"), RWKV_HEAD))
        out_done = sem("out_done")
        xx_ready, xm_ready = sem("xx_ready"), sem("xm_ready")
        stored = [sem(f"stored{k}") for k in range(3)]
        l2_in, rkv_in, st_in = sem("l2_in"), sem("rkv_in"), sem("st_in")
        states_out = sem("states_out")
        logits_rows, logits_copied, logits_full, comb_ready = sem("logits_rows"), sem("logits_copied"), sem("logits_full"), sem("comb_ready")
        hid_ready = sem("hid_ready")
        exp_in, exp_done = sem("exp_in"), sem("exp_done")
        y_ready = sem("y_ready")
        zeroed = sem("zeroed")
        zero_stored = sem("zero_stored")
        hnt_t, hnt_ready = sem("hnt_t"), sem("hnt_ready")
        onehot_ready, counted, routes_ready = sem("onehot_ready"), sem("counted"), sem("routes_ready")
        scattered = sem("scattered")
        xg_in, xg_t = sem("xg_in"), sem("xg_t")
        xe_act, xe_dve = sem("xe_act"), sem("xe_dve")
        gate_done, pair_used = sem("gate_done"), sem("pair_used")
        yf_act, yf_dve = sem("yf_act"), sem("yf_dve")
        yo_t = sem("yo_t")
        yo_act, yo_dve, yo_stored = sem("yo_act"), sem("yo_dve"), sem("yo_stored")
        gathered = [sem(f"gathered{c}") for c in range(CH)]
        combine, outs_t, outs_used = sem("combine"), sem("outs_t"), sem("outs_used")
        x_done = sem("x_done")

        slab_n = {"sp": 0, "pe": 0}
        base, after = {}, []
        for name, slab_tiles in (("ada", [2] * 48), ("in", [2] * 13), ("mout", [2] * 4), ("ff", [2] * FT), ("ffd", [1] * 8),
                                 ("rkv", [2] * 12), ("lora", [2, 1]), ("rout", [2] * 4), ("moe", [2] * 15 * NE)):
            base[name] = after[-1] if after else 0
            for t in slab_tiles:
                after.append((after[-1] if after else 0) + t)

        def tile_done(eng, name, t):
            eng.wait_ge(tiles_done, t + (base[name] + 1))

        def stream(sp, dram, first, count, width):
            n0 = slab_n["sp"]

            def load(k, slot):
                src = dram[k + first] if isinstance(k, int) else dram[bass.ds(k + first, 1)].rearrange("a p n -> p (a n)")
                sp.dma_start(ring[:, slot, 0:width], src).then_inc(slab_ready[slot], 16)

            need = lambda n: after[n - RING] if n >= RING else 0
            k = 0
            while k < count:
                rest = (count - k) // RING
                step = {need(n0 + k + RING * i + u) - need(n0 + k + RING * (i - 1) + u)
                        for i in range(1, rest) for u in range(RING)}
                if rest > 1 and len(step) == 1 and need(n0 + k) > 0:
                    grow = step.pop()
                    with sp.Fori(0, rest) as i:
                        for u in range(RING):
                            sp.wait_ge(tiles_done, i * grow + need(n0 + k + u))
                            load(i * RING + (k + u), (n0 + k + u) % RING)
                    k += rest * RING
                else:
                    if need(n0 + k):
                        sp.wait_ge(tiles_done, need(n0 + k))
                    load(k, (n0 + k) % RING)
                    k += 1
            slab_n["sp"] += count

        def slabs(pe, count, body):
            n0 = slab_n["pe"]

            def one(k, u, lap):
                slot = (n0 + u) % RING
                pe.wait_ge(slab_ready[slot], lap * 16 + 16 * ((n0 + u) // RING + 1))
                body(k, u, slot)
            repeat(pe, count, one)
            slab_n["pe"] += count

        def credit(eng, s, n):
            eng.sem_inc(s, n)

        def mm_tile(pe, a, w, src, kt_n, last_wait=None, each=None):
            for kt in range(kt_n):
                if each:
                    each(kt)
                if last_wait and kt == kt_n - 1:
                    last_wait()
                for lo, hi in HALVES:
                    m = pe.matmul(acc(a)[:, lo:hi], w(kt), src(kt, lo, hi), start=kt == 0, stop=kt == kt_n - 1)
            return m

        block = ctx.enter_context(nc.Block())

        @block.sync
        def _(sp):
            sp.dma_start(vec[:], A["vec"]).then_inc(loaded, 16)
            sp.dma_start(const[:], A["const"]).then_inc(loaded, 16)
            sp.dma_start(x[:], A["x"]).then_inc(loaded, 16)
            sp.dma_start(wrouter[:], A["wrouter"]).then_inc(loaded, 16)
            k8 = A["k8"]
            W8 = KT * 256
            def ada_load(k, slot):
                src = k8[k] if isinstance(k, int) else k8[bass.ds(k, 1)].rearrange("a p n -> p (a n)")
                if not isinstance(k, int) or k >= ADA_SLOTS:
                    sp.wait_ge(ada_used, k - (ADA_SLOTS - 1))
                sp.dma_start(ada_slab[slot].rearrange("p kt n -> p (kt n)"), src).then_inc(ada_slab_ready[slot], 16)

            def in_load(k, slot):
                src = k8[48 + k] if isinstance(k, int) else k8[bass.ds(k + 48, 1)].rearrange("a p n -> p (a n)")
                if not isinstance(k, int) or k >= RING:
                    tile_done(sp, "in", k * 2 - 2 * RING + 1)
                sp.dma_start(ring[:, slot, 0:W8], src).then_inc(slab_ready[slot], 16)
            for s in slab_ready:
                sp.sem_inc(s, 16 * 48 // RING)
            for k in range(12):
                ada_load(k, k % ADA_SLOTS)
            for u in range(RING):
                in_load(u, u)
            for q in range(4):
                ada_load(12 + q, q)
            with sp.Fori(0, 3) as lap:
                for u in range(RING):
                    in_load(lap * 3 + (3 + u), u)
                    if u < 2:
                        for q in range(4):
                            ada_load(lap * 8 + (16 + 4 * u + q), q)
            in_load(12, 0)
            for k in range(40, 48):
                ada_load(k, k % ADA_SLOTS)
            slab_n["sp"] += 48 + 13
            mact.wait(sp, f"T{CH-1}k")
            sp.dma_start(Cst[:, :, 0, :], A["C0"]).then_inc(state_loaded, 16)
            stream(sp, k8, 61, 4, W8)
            mdve.wait(sp, "m11")
            sp.dma_start(A["m_out"][0:32], gf[0:32, TOK - 1:TOK], allow_slow_non_contiguous=True).then_inc(out_done, 16)
            sp.dma_start(A["m_out"][32:64], gf[32:64, LAT:LAT + 1], allow_slow_non_contiguous=True).then_inc(out_done, 16)
            mdve.wait(sp, "C9")
            sp.dma_start(A["C_out"], Cst[:, :, 1, :]).then_inc(out_done, 16)
            sp.wait_ge(out_done, 48)
            credit(sp, states_out, 1)
            stream(sp, k8, 65, 22, W8)
            stream(sp, A["ffd"], 0, 8, SLAB)
            stream(sp, k8, 87, 12, W8)
            stream(sp, k8, 99, 2, W8)
            for s in stored:
                sp.wait_ge(s, 16 * 9)
            sp.sem_inc(st_loaded, 16)
            tile_done(sp, "lora", 2)

            def l2_load(j):
                sp.dma_start(l2, A["l2"][bass.ds(j, 1)].rearrange("a p s n -> p (a s) n")).then_inc(l2_in, 16)

            def rkv_load(j):
                sp.dma_start(rkv, A["rkv_s"][bass.ds(j, 1)].rearrange("a p s n -> p (a s) n")).then_inc(rkv_in, 16)

            def st_load(j):
                sp.dma_start(St[:, 0:2], A["S0"][bass.ds(j, 1)].rearrange("a p s n -> p (a s) n")).then_inc(st_in, 16)

            def tile_io(j, last):
                J = j + 1
                nxt = j if last else j + 1
                rpe.wait(sp, "a1", J)
                l2_load(nxt)
                rdve.wait(sp, "y0", J)
                rkv_load(nxt)
                rdve.wait(sp, "S13", J)
                sp.dma_start(A["S_out"][bass.ds(j, 1)].rearrange("a p s n -> p (a s) n"), St[:, 2:4]).then_inc(st_loaded, 16)
                if not last:
                    rdve.wait(sp, "S71", J)
                    st_load(J)
            l2_load(0)
            rkv_load(0)
            st_load(0)
            with sp.Fori(0, KT - 1) as j:
                tile_io(j, False)
            tile_io(KT - 1, True)
            sp.wait_ge(st_loaded, 16 * (KT + 1))
            hdve.wait(sp, "kmax", KT)
            hpe.wait(sp, "knorm", KT)
            hact.wait(sp, "tha0", KT)
            ract.wait(sp, "std", KT)
            rdve.wait(sp, "yg", KT)
            stream(sp, k8, 101, 4, W8)
            with sp.Fori(0, NE) as e:
                n0 = slab_n["sp"]
                per = 15
                for k in range(per):
                    slot = (n0 + k) % RING
                    sp.wait_ge(tiles_done, e * 30 + after[n0 + k - RING])
                    if k < ET:
                        src = k8[bass.ds(e * ET + (105 + k), 1)].rearrange("a p n -> p (a n)")
                        w = W8
                    else:
                        src = A["exd"][bass.ds(e * 4 + (k - ET), 1)].rearrange("a p n -> p (a n)")
                        w = SLAB
                    sp.dma_start(ring[:, slot, 0:w], src).then_inc(slab_ready[slot], 16)
            for kt in range(KT):
                sp.wait_ge(y_ready, kt + 1)
                sp.dma_start(A["y"][:, kt], hn2[:, kt]).then_inc(out_done, 16)
            sp.wait_ge(out_done, 48 + 16 * KT)

        @block.gpsimd
        def _(pool):
            zeros = arena[:, NA - 3 * D:NA]
            pool.wait_ge(mods_ready, 1)
            pool.memset(zeros, 0.0).then_inc(zeroed, 1)
            pool.wait_ge(zeroed, 1)
            for q in range(NE * CAP // (3 * P)):
                pool.dma_start(A["rows"].rearrange("(q p a) n -> q p (a n)", p=P, a=3)[q], zeros).then_inc(zero_stored, 16)
            pool.wait_ge(free["in"], 3 + IN_TILES)
            pool.wait_ge(ada_done, 12)
            pool.wait_ge(zero_stored, 16 * 4)
            pool.sem_inc(zeroed, 1)
            pool.memset(vaug[:, :, :, DV:DV + 1], 1.0).then_inc(ones_set, 1)
            mact.wait(pool, f"T{CH-1}k")
            pool.wait_ge(ones_set, 1)
            pool.memset(Cst[:, :, 1, :], 0.0).then_inc(ones_set, 1)
            pool.wait_ge(ones_set, 2)
            mdve.wait(pool, "cols1")
            for n, (d, c) in enumerate(MGRP):
                if n >= 2:
                    mpe.wait(pool, f"C{n-2}")
                if n >= 1:
                    mpool.wait(pool, f"kw{n-1}")
                mpool.done(pool.tensor_tensor(
                    kw[:, n % 2].rearrange("p (h k) -> p h k", h=AH), ktok[:, c].rearrange("p (h k) -> p h k", h=AH),
                    colw[:, c, 1, d * 32:d * 32 + AH].unsqueeze(2).to_broadcast([P, AH, DK]), ALU.mult), f"kw{n}")
            for c in (1, 3):
                mdve.wait(pool, "rs")
                mpool.wait(pool, "kw9" if c == 1 else "hn1")
                hh = hs_t[:, c].rearrange("p (h n) -> p h n", h=AH)
                mpool.done(pool.tensor_tensor(hh, hh, ms[:, c].unsqueeze(2).to_broadcast([P, AH, DV]), ALU.mult), f"hn{c}")
            pool.wait_ge(free["lora"], 3 + 3)
            n = 0
            for buf in (BY[1], KX[0], BY[0], QR[0], KX[1], QR[1]):
                if n:
                    pool.wait_ge(zero_set, n)
                pool.memset(buf, 0.0).then_inc(zero_set, 1)
                n += 1
            pool.sem_inc(rpool.sem, len(rpool.names))
            all_i = cst("ident").unsqueeze(1).to_broadcast([P, C64, P])
            with pool.Fori(0, KT) as j:
                J = j + 1
                rdve.wait(pool, "LT04", J)
                rpool.done(pool.tensor_tensor(XT[0], LT[0], cst("nbd2").unsqueeze(1).to_broadcast([P, C64, P]), ALU.mult), "XTa0")
                rpool.wait(pool, "XTa0", J)
                rpool.done(pool.tensor_tensor(XT[0], XT[0], all_i, ALU.add), "XT20")
                rpool.wait(pool, "XT20", J)
                rpool.done(pool.tensor_tensor(LT[0], LT[0], all_i, ALU.add), "LTI0")
                rdve.wait(pool, "Ark14", J)
                rpool.wait(pool, "LTI0", J)
                rpool.done(pool.tensor_tensor(Ark[0], Ark[0], Ark[1], ALU.add), "Ark")
                rdve.wait(pool, "XTa1", J)
                rpool.wait(pool, "Ark", J)
                rpool.done(pool.tensor_tensor(LT[1], LT[1], all_i, ALU.add), "LTI1")
                rpool.next = 0
            pool.wait_ge(routes_ready, 1)
            dense = pool.value_load(rows_i[0:1, 2 * CH:2 * CH + 1], min_val=0, max_val=1)
            with pool.If(1 - dense):
                def rows(k, c):
                    return bass.IndirectOffsetOnAxis(ap=rows_i[:, k * CH + c:k * CH + c + 1].bitcast(mybir.dt.uint32), axis=0)
                for c in range(CH):
                    pool.wait_ge(hnt_ready, 2 * c + 2)
                    for k in range(2):
                        pool.indirect_dma_start(A["rows"], rows(k, c), hnt[:, c], None, bounds_check=NE * CAP - 1).then_inc(scattered, 16)
                pool.wait_ge(yo_stored, 32 * (NE + 1))
                for c in range(CH):
                    for k in range(2):
                        pool.indirect_dma_start((hnt, out2)[k][:, c], None, A["rows"], rows(k, c),
                                                bounds_check=NE * CAP - 1).then_inc(gathered[c], 16)

        @block.tensor
        def _(pe):
            sq_buf = [hn, hn_f, hn1, hn2, hn2]

            def norm(n):
                pe.wait_ge(norm_add, 7 * n + 7)
                for lo, hi in HALVES:
                    m = pe.matmul(stats[:, lo:hi], cst("ones"), sq_buf[n][:, 0, lo:hi], start=True, stop=True)
                m.then_inc(norm_sum, 1)

            norm(0)
            pe.wait_ge(cond_ready, 1)
            pe.sem_inc(tiles_done, 96)

            def ada_group(group, bank):
                for q in range(4):
                    pe.wait_ge(ada_slab_ready[q], group * 16 + 16)
                    for kt in range(KT):
                        m = pe.matmul(PS[32 * q:32 * q + 32, bank, 0:256], scond[:, kt, :], ada_slab[q][:, kt, :], start=kt == 0, stop=kt == KT - 1)
                    m.then_inc(ada_used, 1)

            def ada_columns(group, row, bank):
                pe.wait_ge(ada_copied, group + 1)
                for h in range(2):
                    m = pe.transpose(PS[:, bank, h * P:(h + 1) * P], ada_rows[:, row, h * P:(h + 1) * P], cst("ident"))
                m.then_inc(ada_t, 1)
            for g in range(3):
                ada_group(g, g)
                if g:
                    ada_columns(g - 1, g - 1, 3 + g - 1)
            ada_columns(2, 2, 5)

            def norm_tile(n, first):
                return (lambda kt: pe.wait_ge(norm_done, 16 * n + 2 * kt + 2)) if first else None

            def dense8(count, src, name, n=None):
                def one(k, u, slot):
                    w = ring[:, slot, 0:KT * 256].rearrange("p (kt n) -> p kt n", kt=KT)
                    for t in range(2):
                        pe.wait_ge(free[name], k * 2 + (t + 1))
                        m = mm_tile(pe, (2 * u + t) % 3, lambda kt: w[:, kt, t * P:(t + 1) * P],
                                    lambda kt, lo, hi: src[:, kt, lo:hi], KT, each=norm_tile(n, n is not None and u == t == 0))
                        m.then_inc(tiles_done, 1)
                slabs(pe, count, one)


            def in_slab(k, u, lap):
                w = ring[:, u, 0:KT * 256].rearrange("p (kt n) -> p kt n", kt=KT)
                pe.wait_ge(slab_ready[u], lap * 16 + 16 * (48 // RING + 1))
                for t in range(2):
                    pe.wait_ge(free["in"], k * 2 + (t + 1))
                    m = mm_tile(pe, (2 * u + t) % 3, lambda kt: w[:, kt, t * P:(t + 1) * P],
                                lambda kt, lo, hi: hn[:, kt, lo:hi], KT, each=norm_tile(0, u == t == 0))
                    m.then_inc(tiles_done, 1)

            def late_group(group):
                pe.wait_ge(ada_copied, group)
                ada_group(group, 6)

            def late_columns(group, row):
                pe.wait_ge(ada_done, group)
                ada_columns(group, row, 7)
            with pe.Fori(0, 4) as lap:
                for u in range(3):
                    in_slab(lap * 3 + u, u, lap)
                    if u:
                        late_columns(lap * 2 + (2 + u), 0 if u == 1 else 1)
                    if u < 2:
                        late_group(lap * 2 + (3 + u))
            in_slab(12, 0, 4)
            late_group(11)
            late_columns(11, 0)
            slab_n["pe"] += 48 + 13
            pe.wait_ge(free["in"], 3 + IN_TILES)
            for n, (c, kind) in enumerate(VK):
                if n >= 6:
                    mact.wait(pe, "T%d%s" % VK[n - 6])
                src = {"v0": v_[:, 0:4], "v1": v_[:, 4:8], "k": k_}[kind]
                for t in range(4):
                    m = pe.transpose(PS[:, n % 6, t * P:(t + 1) * P], src[:, t, c * P:(c + 1) * P], cst("ident"))
                mpe.done(m, f"T{c}{kind}")
            mact.wait(pe, "dec")
            for n in range(15):
                c, kind = n // 3, n % 3
                src = (winter_r, ws_r, gi)[kind]
                m = pe.transpose(PS[:, 6 + n // 8, (n % 8) * 64:(n % 8) * 64 + 64], src[0:64, c * P:(c + 1) * P],
                                 cst("ident", slice(0, 64))[:, 0:64])
                if n in (7, 14):
                    mpe.done(m, f"cols{n // 8}")
            mdve.wait(pe, "decx")
            mact.wait(pe, "T%d%s" % VK[-1])
            mpe.done(pe.matmul(PS[:, 0, 0:CH * 64], cst("ones", slice(0, 64)), decx[0:64].rearrange("p c r -> p (c r)"),
                               start=True, stop=True), "decb")
            mdve.wait(pe, "decp3")
            pe.wait_ge(state_loaded, 16)
            pe.wait_ge(ones_set, 2)
            for n, (d, c) in enumerate(MGRP):
                seq = 0 if c < 4 else 1
                tok = slice(c * P, (c + 1) * P)
                for g in range(2):
                    prev = (n, 0) if g else (n - 1, 1)
                    if n or g:
                        mact.wait(pe, f"W{prev[0]}{prev[1]}")
                    for h in range(4):
                        row = d * 32 + 2 * h + g
                        pick = cst("ident", slice(0, 64))[:, row:row + 1].to_broadcast([64, P])
                        o = PS[:, 0, h * P:(h + 1) * P]
                        pe.matmul(o, pick, negG[0:64, tok], start=True, stop=False)
                        pe.matmul(o, g_row[0:64, tok], pick, start=False, stop=False)
                        m = pe.matmul(o, cst("ident"), cst(f"neg{d}"), start=False, stop=True)
                    mpe.done(m, f"D{n}{g}")
                    if n or g:
                        mdve.wait(pe, f"P{prev[0]}{prev[1]}")
                    for h in range(4):
                        hh = 2 * h + g
                        pr = slice(64 * g, 64 * g + 64)
                        m = pe.matmul(PS[:, 1, h * P:(h + 1) * P], k_[pr, hh // 2, tok], q_[pr, hh // 2, tok],
                                      start=True, stop=True)
                    mpe.done(m, f"S{n}{g}")
                    if n or g:
                        mdve.wait(pe, f"comb{prev[0]}{prev[1]}")
                    if n >= 2 and not g:
                        mdve.wait(pe, f"C{n-2}")
                    mdve.wait(pe, f"P{n}{g}")
                    for h in range(4):
                        hh = 2 * h + g
                        pr = slice(64 * g, 64 * g + 64)
                        pe.matmul(PS[:, 4 + h // 2, (h % 2) * 129:(h % 2) * 129 + 129], q_[pr, hh // 2, tok],
                                  Cst[pr, d, seq, (hh // 2) * 129:(hh // 2) * 129 + 129], start=True, stop=True)
                        m = pe.matmul(PS[:, 2 + h // 2, (h % 2) * 129:(h % 2) * 129 + 129], Wt[:, g, h, :],
                                      vaug[:, c, hh, :], start=True, stop=True)
                    mpe.done(m, f"num{n}{g}")
                mpool.wait(pe, f"kw{n}")
                if n:
                    mdve.wait(pe, f"C{n-1}")
                for hh in range(AH):
                    p0 = 64 * (hh % 2)
                    pair = hh // 2
                    m = pe.matmul(PS[p0:p0 + 64, 6 + pair // 2, (pair % 2) * 129:(pair % 2) * 129 + 129],
                                  kw[:, n % 2, hh * DK:(hh + 1) * DK], vaug[:, c, hh, :], start=True, stop=True)
                mpe.done(m, f"C{n}")
            for h in range(AH):
                if h >= 3:
                    mdve.wait(pe, f"mo{h-3}")
                for c in range(CH):
                    (mpool if c in (1, 3) else mdve).wait(pe, f"hn{c}")
                    m = pe.transpose(acc(h % 3)[:, c * P:(c + 1) * P], hs_t[:, c, h * DV:(h + 1) * DV], cst("ident"))
                mpe.done(m, f"hT{h}")
            mdve.wait(pe, "mo7")
            dense8(4, o_, "mout")
            norm(1)

            def ff(k, u, slot):
                w = ring[:, slot, 0:KT * 256].rearrange("p (kt n) -> p kt n", kt=KT)
                for t in range(2):
                    pe.wait_ge(free["ffu"] if t == 0 else free["ffg"], k + 1)
                    m = mm_tile(pe, (2 * u + t) % 3, lambda kt: w[:, kt, t * P:(t + 1) * P],
                                lambda kt, lo, hi: hn_f[:, kt, lo:hi], KT, each=norm_tile(1, u == t == 0))
                    m.then_inc(tiles_done, 1)
            slabs(pe, FT, ff)
            pe.wait_ge(free["ffu"], 2 + FT)

            def ffd(k, u, slot):
                w = ring[:, slot, :].rearrange("p (kt n) -> p kt n", kt=FT)
                pe.wait_ge(free["ffd"], k + 1)
                m = mm_tile(pe, u % 3, lambda kt: w[:, kt, :], lambda kt, lo, hi: hid_f[:, kt, lo:hi], FT)
                m.then_inc(tiles_done, 1)
            slabs(pe, 8, ffd)
            norm(2)


            def rkvp(k, u, slot):
                w = ring[:, slot, 0:KT * 256].rearrange("p (kt n) -> p kt n", kt=KT)
                for t in range(2):
                    pe.wait_ge(free["rkv"], k * 2 + (t + 1))
                    m = mm_tile(pe, (2 * u + t) % 3, lambda kt: w[:, kt, t * P:(t + 1) * P],
                                lambda kt, lo, hi: xm[u][:, kt, lo:hi], KT,
                                each=(lambda kt: pe.wait_ge(xm_ready, 8 * u + kt + 1)) if t == 0 else None)
                    m.then_inc(tiles_done, 1)
            slabs(pe, 12, rkvp)

            def lora(k, u, slot):
                w = ring[:, slot, 0:KT * 256].rearrange("p (kt n) -> p kt n", kt=KT)
                for t in range(2):
                    if 2 * k + t > 2:
                        break
                    pe.wait_ge(free["lora"], 2 * k + t + 1)
                    m = mm_tile(pe, 2 * k + t, lambda kt: w[:, kt, t * P:(t + 1) * P],
                                lambda kt, lo, hi: xm[2 * k + t][:, kt, lo:hi], KT,
                                each=lambda kt: pe.wait_ge(xm_ready, 8 * (3 + 2 * k + t) + kt + 1))
                    m.then_inc(tiles_done, 1)
            slabs(pe, 2, lora)
            pe.wait_ge(free["lora"], 3 + 3)
            pe.sem_inc(rpe.sem, len(rpe.names))
            wide = lambda b: psf[:, b * 512:b * 512 + TOK]

            def two(b, lhsT, rhs):
                for lo, hi in HALVES:
                    m = pe.matmul(wide(b)[:, lo:hi], lhsT, rhs[:, lo:hi], start=True, stop=True)
                return m

            def lora2(steps, d):
                dd = slice(64 * d, 64 * d + 64)
                steps.done(two(4, l2[dd, 0], lhid[dd, 0]), f"w{d}")
                steps.done(two(6, l2[dd, 1], lhid[dd, 1]), f"a{d}")

            def head_lora(j):
                pe.wait_ge(l2_in, j * 16 + 16)
                lora2(hpe, 0)

            def head_norm(j):
                hact.wait(pe, "sq", j)
                hpe.done(two(0, cst("headones"), T[1]), "knorm")
                hpe.next = 0
            head_lora(0)
            head_norm(0)
            with pe.Fori(0, KT) as j:
                J = j + 1
                ract.wait(pe, "varln", j)
                rpe.done(two(2, l2[:, 2], lhid[:, 2]), "gate")

                def tr(src, b0, label, before):
                    for g, (c0, c1) in enumerate(GR):
                        before(g)
                        for c in range(c0, c1):
                            m = pe.transpose(PS[:, b0 + g, (c - c0) * P:(c - c0 + 1) * P], src[:, c], cst("ident"))
                        rpe.done(m, f"{label}{g}")
                hdve.wait(pe, "vT1", j)
                hdve.wait(pe, "kmax", j)
                tr(BY[1], 0, "V", lambda g: ract.wait(pe, "gate", J) if g == 2 else None)
                hact.wait(pe, "tha0", j)
                lora2(rpe, 1)
                for d in range(2):
                    rdve.wait(pe, f"K1{d}", J)
                    tr(KX[d], 0, f"Kt{d}", lambda g: rdve.wait(pe, "Ark04", J) if d else ract.wait(pe, f"V{g}", J))
                    rdve.wait(pe, f"B1{d}", J)
                    if d == 0:
                        ract.wait(pe, "tha1", J)
                    tr(BY[d], 3, f"Bt{d}", lambda g: rdve.wait(pe, f"Arb0{g}", J) if d else None)
                    for nm, src, banks in (("GK", KX[d], (6, 7, 0, 1, 2)), ("GB", BY[d], (3, 4, 5, 6, 7))):
                        for q in range(5):
                            b = banks[q]
                            if nm == "GK" and b >= 6 and d:
                                rdve.wait(pe, f"Arb0{b-3}", J)
                            if nm == "GK" and b < 3:
                                ract.wait(pe, f"Kt{d}{b}", J)
                            if nm == "GB" and b < 6:
                                ract.wait(pe, f"Bt{d}{b-3}", J)
                            if nm == "GB" and b >= 6:
                                rdve.wait(pe, f"Ark{d}{b-6}", J)
                            for i in range(2):
                                c = 2 * q + i
                                m = pe.matmul(PS[:, b, i * 192:(i + 1) * 192], src[:, c], QR[d][:, c, :], start=True, stop=True)
                            rpe.done(m, f"{nm}{d}{q}")
                for d in range(2):
                    for nm, b0, src in (("MV", 0, MkT[d]), ("KV", 3, Ktok[d])):
                        for g, (c0, c1) in enumerate(GR):
                            if d:
                                (ract if nm == "MV" else rdve).wait(pe, f"{nm}0{g}", J)
                            else:
                                rdve.wait(pe, f"Ark1{g+2}" if nm == "MV" else f"Arb1{g}", J)
                            for c in range(c0, c1):
                                m = pe.matmul(PS[:, b0 + g, (c - c0) * P:(c - c0 + 1) * P], src[:, c], Vbd[:, c], start=True, stop=True)
                            rpe.done(m, f"{nm}{d}{g}")
                rdve.wait(pe, "rkk", J)
                rdve.wait(pe, "Arb14", J)
                rpe.done(two(6, cst("headones"), T[5]), "bonus")
                ract.wait(pe, "MV10", J)
                ract.wait(pe, "MV11", J)
                rpool.wait(pe, "Ark", J)
                for c in range(C64):
                    for h in range(2):
                        hs = slice(64 * h, 64 * h + 64)
                        m = pe.matmul(wide(0)[hs, c * HD:(c + 1) * HD], Vbd[:, c, hs], Ark[0][:, c], start=True, stop=True)
                rpe.done(m, "yV")
                for n, lv in enumerate(LEVELS):
                    for ph in ("X", "Y", "Z"):
                        for d in range(2):
                            for g, (c0, c1) in enumerate(GR):
                                b = d * 3 + g
                                if ph == "X":
                                    if n == 0:
                                        (rdve if d else rpool).wait(pe, f"XT2{d}", J)
                                        rdve.wait(pe, "y0", J)
                                        if d == 0 and g == 2:
                                            ract.wait(pe, "MV12", J)
                                        if d:
                                            rdve.wait(pe, f"KV1{g}", J)
                                    else:
                                        rdve.wait(pe, f"Z{LEVELS[n-1]}{d}{g}", J)
                                elif ph == "Y":
                                    ract.wait(pe, f"X{lv}{d}{g}", J)
                                    if n == 0:
                                        rpool.wait(pe, f"LTI{d}", J)
                                else:
                                    rdve.wait(pe, f"Y{lv}{d}{g}", J)
                                for c in range(c0, c1):
                                    o = PS[:, b, (c - c0) * P:(c - c0 + 1) * P]
                                    if ph == "X":
                                        m = pe.transpose(o, XT[d][:, c], cst("ident"))
                                    elif ph == "Y":
                                        m = pe.matmul(o, LT[d][:, c], KX[d][:, c], start=True, stop=True)
                                    else:
                                        m = pe.matmul(o, BY[d][:, c], XT[d][:, c], start=True, stop=True)
                                rpe.done(m, f"{ph}{lv}{d}{g}")
                for d in range(2):
                    for g in range(3):
                        ract.wait(pe, f"Z64{d}{g}", J)
                pe.wait_ge(st_in, j * 16 + 16)
                now = lambda t: St_odd if t % 2 else St
                ybank = lambda t, i: i if t < 2 else 2 + i
                for t in range(8):
                    mine = chain_steps(t)
                    for i in mine:
                        d, cs = CHAINS[i]
                        if t:
                            rdve.wait(pe, f"S{t-1}{i}", J)
                            if t < 3:
                                rdve.wait(pe, f"y{t-1}{i}", J)
                        rpe.done(pe.matmul(PS[:, i, 0:P], QR[d][:, cs[t], 0:P], now(t)[:, i], start=True, stop=True), f"rhs{t}{i}")
                    for i in mine:
                        d, cs = CHAINS[i]
                        rdve.wait(pe, f"rhs{t}{i}", J)
                        rpe.done(pe.matmul(PS[:, i, 0:P], XT[d][:, cs[t]], RU[:, i], start=True, stop=True), f"U{t}{i}")
                    for i in mine:
                        d, cs = CHAINS[i]
                        ract.wait(pe, f"U{t}{i}", J)
                        rpe.done(pe.matmul(PS[:, 4 + i, 0:P], Btok[d][:, cs[t]], RU[:, i], start=True, stop=True), f"S{t}{i}")
                    for i in mine:
                        d, cs = CHAINS[i]
                        c = cs[t]
                        if t > 2:
                            rdve.wait(pe, f"y{t-1}{i}", J)
                        if t == 2:
                            rdve.wait(pe, f"y{t-1}{i+2}", J)
                        for h in range(2):
                            hs = slice(64 * h, 64 * h + 64)
                            yo = PS[hs, ybank(t, i), 128:128 + HD]
                            pe.matmul(yo, now(t)[:, i, hs], QR[d][:, c, P:192], start=True, stop=False)
                            m = pe.matmul(yo, RU[:, i, hs], Arb[d][:, c], start=False, stop=True)
                        rpe.done(m, f"y{t}{i}")
                rdve.wait(pe, "y71", J)
                rpe.done(two(0, cst("headmean"), T[4]), "mean")
                head_lora(J)
                ract.wait(pe, "ysq", J)
                rpe.done(two(2, cst("headmean"), T[3]), "var")
                head_norm(J)
                rpe.next = 0
            rdve.wait(pe, "yg", KT)
            dense8(4, gk, "rout")
            norm(3)
            pe.wait_ge(free["rout"], 3 + 8)
            for kt in range(KT):
                pe.wait_ge(norm_done, 48 + 2 * kt + 2)
                for lo, hi in HALVES:
                    m = pe.matmul(psf[0:NE, lo:hi], wrouter[:, kt, :], hn2[:, kt, lo:hi], start=kt == 0, stop=kt == KT - 1)
            m.then_inc(logits_rows, 1)

            def token_major(n):
                if n >= 5:
                    pe.wait_ge(hnt_ready, n - 4)
                c, half = n // 2, n % 2
                for t in range(4):
                    m = pe.transpose(PS[:, 3 + n % 5, t * P:(t + 1) * P], hn2[:, half * 4 + t, c * P:(c + 1) * P], cst("ident"))
                m.then_inc(hnt_t, 1)
            token_major(0)
            pe.wait_ge(logits_copied, 1)
            for c in range(CH):
                m = pe.transpose(PS[:, 2, c * NE:(c + 1) * NE], logit_rows[0:NE, c * P:(c + 1) * P], cst("ident", slice(0, NE))[:, 0:NE])
            m.then_inc(logits_full, 1)
            for n in range(1, 5):
                token_major(n)
            pe.wait_ge(onehot_ready, 1)
            oh = one_hot.rearrange("p c e -> p (c e)")
            pe.matmul(PS[:, 0, 0:CH * NE], cst("strict0"), oh, start=True, stop=False)
            for back in range(1, CH):
                pe.matmul(PS[:, 0, back * NE:CH * NE], cst("ones"), oh[:, 0:(CH - back) * NE], start=False, stop=back == CH - 1)
            for c in range(CH):
                m = pe.matmul(PS[:, 1, 0:NE], cst("ones"), one_hot[:, c], start=c == 0, stop=c == CH - 1)
            m.then_inc(counted, 1)
            for n in range(5, 2 * CH):
                token_major(n)
            n0 = slab_n["pe"]
            pe.wait_ge(routes_ready, 1)
            dense = pe.value_load(rows_i[0:1, 2 * CH:2 * CH + 1], min_val=0, max_val=1)
            with pe.If(dense):
                pe.wait_ge(hnt_ready, 2 * CH)
                pe.wait_ge(comb_ready, 1)
                for e in range(NE):
                    pe.wait_ge(free["cb"], e + 1)
                    for c in range(CH):
                        m = pe.matmul(acc(e % 3)[:, c * P:(c + 1) * P], comb_w[:, c, e:e + 1].to_broadcast([P, P]), cst("ident"),
                                      start=True, stop=True)
                    m.then_inc(cb_full, 1)
                pe.wait_ge(free["cb"], 3 + NE)
                with pe.Fori(0, NE) as e:
                    for k in range(15):
                        slot = (n0 + k) % RING
                        pe.wait_ge(slab_ready[slot], e * 80 + 16 * ((n0 + k) // RING + 1))
                        if k < ET:
                            w = ring[:, slot, 0:KT * 256].rearrange("p (kt n) -> p kt n", kt=KT)
                        else:
                            w = ring[:, slot, :].rearrange("p (kt n) -> p kt n", kt=ET)
                        for t in range(2):
                            tile = 2 * k + t
                            a = tile % 3
                            if k < ET:
                                if tile < 3:
                                    pe.wait_ge(free["moed"], e * 8 + (1 + tile))
                                elif tile % 2 == 0:
                                    pe.wait_ge(free["moeu"], e * ET + (tile - 4) // 2 + 1)
                                else:
                                    pe.wait_ge(free["moeg"], e * ET + (tile - 3) // 2 + 1)
                                m = mm_tile(pe, a, lambda kt: w[:, kt, t * P:(t + 1) * P], lambda kt, lo, hi: hn2[:, kt, lo:hi], KT)
                            else:
                                o = tile - 2 * ET
                                last = None
                                if o == 1:
                                    pe.wait_ge(free["moeg"], e * ET + ET)
                                elif o < 3:
                                    pe.wait_ge(free["moeu"], e * ET + (tile - 4) // 2 + 1)
                                if o == 0:
                                    pe.wait_ge(hid_ready, e * ET + ET - 1)
                                if o >= 3:
                                    pe.wait_ge(free["moed"], e * 8 + (o + 1))
                                if o == 0:
                                    last = lambda: pe.wait_ge(hid_ready, e * ET + ET)
                                m = mm_tile(pe, a, lambda kt: w[:, kt, t * P:(t + 1) * P], lambda kt, lo, hi: hid[:, kt, lo:hi], ET, last)
                            m.then_inc(tiles_done, 1)
            with pe.Else():
                with pe.Fori(0, NE) as e:
                    pe.wait_ge(xg_in, e * 32 + 32)
                    for i in range(4):
                        if i == 2:
                            pe.wait_ge(yo_dve, e * 2 + 2)
                        for t in range(2):
                            b0 = t * 256
                            kts = slice((2 * i + t) * P, (2 * i + t + 1) * P)
                            pe.transpose(PS[:, (1, 2, 6, 7)[i], b0:b0 + P], xg[:, 0, kts], cst("ident"))
                            m = pe.transpose(PS[:, (1, 2, 6, 7)[i], b0 + P:b0 + CAP], xg[0:CAP - P, 1, kts],
                                             cst("ident", slice(0, CAP - P))[:, 0:CAP - P])
                        m.then_inc(xg_t, 1)
                    for k in range(15):
                        slot = (n0 + k) % RING
                        pe.wait_ge(slab_ready[slot], e * 80 + 16 * ((n0 + k) // RING + 1))
                        if k < ET:
                            w = ring[:, slot, 0:KT * 256].rearrange("p (kt n) -> p kt n", kt=KT)
                            pe.wait_ge(pair_used, e * ET + (max(k - 3, 0) + 1))
                            for t in range(2):
                                for kt in range(KT):
                                    if k == 0 and t == 0 and kt % 2 == 0:
                                        pe.wait_ge(xe_dve if kt % 4 else xe_act, e * 2 + (kt // 4 + 1))
                                    m = pe.matmul(PS[:, k % 4, t * CAP:(t + 1) * CAP], w[:, kt, t * P:(t + 1) * P], xe[:, kt],
                                                  start=kt == 0, stop=kt == KT - 1)
                                m.then_inc(tiles_done, 1)
                        else:
                            w = ring[:, slot, :].rearrange("p (kt n) -> p kt n", kt=ET)
                            o = k - ET
                            for t in range(2):
                                if o == 0:
                                    pe.wait_ge(yo_dve if t else yo_act, e * 2 + 1)
                                else:
                                    pe.wait_ge(yf_dve if t else yf_act, e * 4 + o)
                                for f in range(ET):
                                    if o == 0 and t == 0 and f in (0, ET - 1):
                                        pe.wait_ge(pair_used, e * ET + (f and ET or ET - 1) + 1)
                                    m = pe.matmul(PS[:, 4 + t, 0:CAP], w[:, f, t * P:(t + 1) * P], hide[:, f, :],
                                                  start=f == 0, stop=f == ET - 1)
                                m.then_inc(tiles_done, 1)
                    for half in range(2):
                        pe.wait_ge(yf_act, e * 4 + (2 * half + 2))
                        pe.wait_ge(yf_dve, e * 4 + (2 * half + 2))
                        if half == 0:
                            pe.wait_ge(yf_act, e * 4 + 4)
                        for rows in range(2):
                            n = (P, CAP - P)[rows]
                            for t in range(4):
                                m = pe.transpose(PS[0:n, 4 + 2 * rows + half, t * P:(t + 1) * P],
                                                 yf[:, 4 * half + t, rows * P:rows * P + n], cst("ident"))
                        m.then_inc(yo_t, 1)
                for kt in range(KT):
                    if kt >= 3:
                        pe.wait_ge(outs_used, kt - 2)
                    for c in range(CH):
                        if kt == 0:
                            pe.wait_ge(combine, 2 * c + 2)
                        m = pe.transpose(acc(kt % 3)[:, c * P:(c + 1) * P], hnt[:, c, kt * P:(kt + 1) * P], cst("ident"))
                    m.then_inc(outs_t, 1)
            norm(4)

        @block.scalar
        def _(act):
            def norm_a(n, buf, done=None, at=0):
                for kt in range(KT):
                    if done:
                        act.wait_ge(done, at + kt + 1)
                    act.activation(buf[:, kt], x[:, kt], ACT.Square).then_inc(norm_sq, 1)
                act.wait_ge(norm_sum, n + 1)
                act.activation(rstd[:], stats, ACT.Ln, bias=cst("eps"), scale=1.0 / D).then_inc(norm_ln, 1)
                act.wait_ge(norm_ln, n + 1)
                act.activation(rstd[:], rstd[:], ACT.Exp, scale=-0.5).then_inc(norm_std, 1)

            act.wait_ge(loaded, 64)
            act.wait_ge(cond_zero, 1)
            act.activation(scond[:, :, 0:2], vcol("cond", 0, 2 * KT).rearrange("p (a b) -> p a b", b=2), ACT.Silu).then_inc(cond_ready, 1)
            norm_a(0, hn)

            def copy_rows(group, row, bank):
                act.wait_ge(ada_used, group * 4 + 4)
                act.activation(ada_rows[:, row], PS[:, bank, 0:256], ACT.Copy).then_inc(ada_copied, 1)
            for g in range(3):
                copy_rows(g, g, g)

            def norm_b(n, buf, layer, which):
                for kt in range(KT):
                    act.wait_ge(norm_x, 8 * n + kt + 1)
                    for s, (lo, hi) in enumerate(HALVES):
                        act.activation(buf[:, kt, lo:hi], buf[:, kt, lo:hi], ACT.Identity,
                                       bias=mods[:, layer, 3 * which, kt, s:s + 1],
                                       scale=gs[:, layer, which, kt, s:s + 1]).then_inc(norm_done, 1)

            act.wait_ge(mods_ready, 1)
            norm_b(0, hn, 0, 0)
            credit(act, free["in"], 3)

            def one(k, u):
                for t in range(2):
                    n = 2 * k + t if isinstance(k, int) else k * 2 + t
                    tile_done(act, "in", n)
                    zz = z[:, n] if isinstance(n, int) else z[:, bass.ds(n, 1)].rearrange("p a n -> p (a n)")
                    a0 = CONST["in_scale"][0]
                    sc = const[:, a0 + n:a0 + n + 1] if isinstance(n, int) else const[:, bass.ds(n + a0, 1)]
                    act.activation(zz, acc((2 * u + t) % 3), ACT.Identity, bias=b_in_col(n), scale=sc).then_inc(free["in"], 1)

            def b_in_col(n):
                return bs_in[:, n:n + 1] if isinstance(n, int) else bs_in[:, bass.ds(n, 1)]

            def late_rows(group, row):
                act.wait_ge(ada_done, group - 1)
                copy_rows(group, row, 6)
            with act.Fori(0, 4) as lap:
                for u in range(3):
                    one(lap * 3 + u, u)
                    if u < 2:
                        late_rows(lap * 2 + (3 + u), u)
            one(12, 0)
            late_rows(11, 0)
            act.wait_ge(free["in"], 3 + IN_TILES)
            act.wait_ge(zeroed, 2)
            for n, (c, kind) in enumerate(VK):
                mpe.wait(act, f"T{c}{kind}")
                dst = ktok[:, c] if kind == "k" else vaug[:, c, 4 * int(kind[1]):4 * int(kind[1]) + 4, 0:DV]
                src = PS[:, n % 6, :] if kind == "k" else PS[:, n % 6, :].rearrange("p (h n) -> p h n", h=4)
                mact.done(act.activation(dst, src, ACT.Copy), f"T{c}{kind}")
            R = slice(0, 64)
            mact.done(act.activation(tmp_row[R], gf[R], ACT.Abs), "absf")
            mact.wait(act, "absf")
            mact.done(act.activation(tmp_row[R], tmp_row[R], ACT.Exp, scale=-1.0), "expf")
            mact.wait(act, "expf")
            mact.done(act.activation(tmp_row[R], tmp_row[R], ACT.Ln, bias=1.0), "lnf")
            mdve.wait(act, "m11")
            mdve.wait(act, "g")
            mact.done(act.activation(gi[R], gf[R], ACT.Exp, scale=-1.0), "em")
            mdve.wait(act, "gend1")
            for c in range(CH):
                mact.done(act.activation(winter_r[R, c * P:(c + 1) * P], negG[R, c * P:(c + 1) * P], ACT.Exp,
                                         bias=mprev[R, c:c + 1]), f"winter{c}")
            for c in range(CH):
                mact.done(act.activation(ws_r[R, c * P:(c + 1) * P], g_row[R, c * P:(c + 1) * P], ACT.Exp,
                                         bias=gend[R, c:c + 1]), f"ws{c}")
            mact.done(act.activation(dec[R], dec[R], ACT.Exp), "dec")
            for n, (d, c) in enumerate(MGRP):
                for g in range(2):
                    mpe.wait(act, f"D{n}{g}")
                    if n:
                        mpe.wait(act, f"num{n-1}{g}")
                    mact.done(act.activation(Wt[:, g].rearrange("p h n -> p (h n)"), PS[:, 0, :], ACT.Exp), f"W{n}{g}")
            mact.done(act.activation(o_.rearrange("p a n -> p (a n)"), o_.rearrange("p a n -> p (a n)"), ACT.Sigmoid), "sigo")
            mdve.wait(act, "h91")
            mpe.wait(act, "C9")
            for c in range(CH):
                if c >= 2:
                    mdve.wait(act, f"ms{c-2}")
                mact.done(act.activation(sqt[c % 2].rearrange("p h n -> p (h n)"), hs_t[:, c], ACT.Square), f"sq{c}")
            mdve.wait(act, "ms4")
            mact.done(act.activation(ms, ms, ACT.Sqrt, bias=cst("eps"), scale=1.0 / DV), "sd")
            norm_a(1, hn_f, free["mout"], 3)
            act.wait_ge(states_out, 1)
            act.wait_ge(mods_ready, 2)
            norm_b(1, hn_f, 0, 1)
            credit(act, free["ffg"], 1)

            def ffg(k, u, lap):
                tile_done(act, "ff", k * 2)
                act.activation(sg_f[:, u], acc((2 * u) % 3), ACT.Silu).then_inc(free["ffg"], 1)
            repeat(act, FT, ffg)
            norm_a(2, hn1, free["ffd"], 3)
            norm_b(2, hn1, 1, 0)
            credit(act, free["rkv"], 3)

            def rk(i):
                for m in range(6):
                    t = i * 6 + m
                    u, w = m // 2, m % 2
                    tile_done(act, "rkv", t)
                    act.wait_ge(stored[m % 3], i * 32 + 16 * (m // 3 + 1))
                    act.activation(stage[:, m % 3], acc(m % 3), ACT.Copy).then_inc(free["rkv"], 1)
                    act.wait_ge(free["rkv"], t + (1 + 3))
                    act.dma_start(A["rkv_s"][bass.ds(i * 2 + w, 1), :, u, :].rearrange("a p n -> p (a n)"),
                                  stage[:, m % 3]).then_inc(stored[m % 3], 16)
            for s in stored:
                act.sem_inc(s, 16)
            with act.Fori(0, 4) as i:
                rk(i)
            credit(act, free["lora"], 3)
            for t, fn in enumerate((ACT.Tanh, ACT.Copy, ACT.Sigmoid)):
                tile_done(act, "lora", t)
                act.activation(lhid[:, t], acc(t), fn).then_inc(free["lora"], 1)
            act.sem_inc(ract.sem, len(ract.names))
            wide = lambda b: psf[:, b * 512:b * 512 + TOK]

            def head(j):
                hdve.wait(act, "kk0", j)
                hact.done(act.activation(T[1], T[0], ACT.Square), "sq")
                hpe.wait(act, "w0", j)
                hact.done(act.activation(T[5], wide(4), ACT.Tanh, bias=w0h[:, bass.ds(j, 1)], scale=0.5), "thw0")
                hpe.wait(act, "a0", j)
                hact.done(act.activation(T[8], wide(6), ACT.Tanh, bias=w0h[:, bass.ds(j + 2 * KT, 1)], scale=0.5), "tha0")
                hact.next = 0
            head(0)
            with act.Fori(0, KT) as j:
                J = j + 1
                col = lambda t, k0: t[:, bass.ds(j + k0, 1)]
                hdve.wait(act, "kmax", j)
                ract.done(act.activation(T[1], T[1], ACT.Ln, scale=2.0 ** 32), "knln")
                ract.wait(act, "knln", J)
                ract.done(act.activation(T[1], T[1], ACT.Exp, bias=cst("kk_back"), scale=-0.5), "knorm")
                rpe.wait(act, "gate", J)
                rdve.wait(act, "yg", j)
                ract.done(act.activation(T[2], wide(2), ACT.Copy), "gate")
                for g, (c0, c1) in enumerate(GR):
                    rpe.wait(act, f"V{g}", J)
                    ract.done(act.activation(Vbd[:, c0:c1].rearrange("p c n -> p (c n)"), PS[:, g, 0:(c1 - c0) * P], ACT.Copy), f"V{g}")

                def tokens(d):
                    for nm, dst, b0 in (("Kt", Ktok[d], 0), ("Bt", Btok[d], 3)):
                        for g, (c0, c1) in enumerate(GR):
                            rpe.wait(act, f"{nm}{d}{g}", J)
                            ract.done(act.activation(dst[:, c0:c1].rearrange("p c n -> p (c n)"), PS[:, b0 + g, 0:(c1 - c0) * P], ACT.Copy),
                                      f"{nm}{d}{g}")
                for d in range(2):
                    (rdve.wait(act, "ce1", J) if d else hdve.wait(act, "ce0", j))
                    ract.done(act.activation(T[5], T[6], ACT.Exp), f"e1{d}")
                    ract.done(act.activation(T[6], T[6], ACT.Exp, scale=-1.0), f"e2{d}")
                    ract.done(act.activation(T[7], T[7], ACT.Exp), f"e3{d}")
                    ract.wait(act, f"e1{d}", J)
                    e1c = T[5].rearrange("p (c n) -> p c n", c=C64)
                    k = 63 if d == 0 else 0
                    ract.done(act.activation(pend[:, d].unsqueeze(2), e1c[:, :, k:k + 1], ACT.Copy), f"pend{d}")
                    if d == 0:
                        rpe.wait(act, "w1", J)
                        rdve.wait(act, "B10", J)
                        ract.wait(act, "pend0", J)
                        ract.done(act.activation(T[5], wide(4), ACT.Tanh, bias=col(w0h, KT), scale=0.5), "thw1")
                        rpe.wait(act, "a1", J)
                        ract.done(act.activation(T[8], wide(6), ACT.Tanh, bias=col(w0h, 3 * KT), scale=0.5), "tha1")
                    tokens(d)
                for d in range(2):
                    for g, (c0, c1) in enumerate(GR):
                        rpe.wait(act, f"MV{d}{g}", J)
                        ract.done(act.activation(MkT[d][:, c0:c1].rearrange("p c n -> p (c n)"), PS[:, g, 0:(c1 - c0) * P], ACT.Copy), f"MV{d}{g}")
                for lv in LEVELS:
                    for d in range(2):
                        for g, (c0, c1) in enumerate(GR):
                            rpe.wait(act, f"X{lv}{d}{g}", J)
                            ract.done(act.activation(KX[d][:, c0:c1].rearrange("p c n -> p (c n)"),
                                                     PS[:, d * 3 + g, 0:(c1 - c0) * P], ACT.Copy), f"X{lv}{d}{g}")
                    if lv == 64:
                        for d in range(2):
                            for g, (c0, c1) in enumerate(GR):
                                rpe.wait(act, f"Z64{d}{g}", J)
                                ract.done(act.activation(XT[d][:, c0:c1].rearrange("p c n -> p (c n)"),
                                                         PS[:, d * 3 + g, 0:(c1 - c0) * P], ACT.Copy), f"Z64{d}{g}")
                for t in range(8):
                    for i in chain_steps(t):
                        rpe.wait(act, f"U{t}{i}", J)
                        ract.done(act.activation(RU[:, i], PS[:, i, 0:P], ACT.Copy, scale=-1.0), f"U{t}{i}")
                rdve.wait(act, "yc", J)
                ract.done(act.activation(T[3], T[9], ACT.Square), "ysq")
                head(J)
                rpe.wait(act, "var", J)
                ract.done(act.activation(T[3], wide(2), ACT.Ln, bias=cst("ln_eps")), "varln")
                ract.wait(act, "varln", J)
                ract.done(act.activation(T[3], T[3], ACT.Exp, scale=-0.5), "std")
                ract.next = 0
            norm_a(3, hn2, free["rout"], 3)
            norm_b(3, hn2, 1, 1)
            for n in range(2 * CH):
                act.wait_ge(hnt_t, n + 1)
                act.activation(hnt[:, n // 2, (n % 2) * 512:(n % 2) * 512 + 512], PS[:, 3 + n % 5, :], ACT.Copy).then_inc(hnt_ready, 1)
            act.wait_ge(exp_in, 1)
            act.activation(e12, e12, ACT.Exp).then_inc(exp_done, 1)
            act.wait_ge(routes_ready, 1)
            dense = act.value_load(rows_i[0:1, 2 * CH:2 * CH + 1], min_val=0, max_val=1)
            with act.If(dense):
                credit(act, free["cb"], 3)
                for e in range(NE):
                    act.wait_ge(cb_full, e + 1)
                    act.activation(cb[:, e], acc(e % 3), ACT.Copy).then_inc(free["cb"], 1)
                with act.Fori(0, NE) as e:
                    for f in range(ET):
                        tile_done(act, "moe", e * 30 + 2 * f)
                        act.activation(sg[:, f % RING], acc((2 * f) % 3), ACT.Silu).then_inc(free["moeg"], 1)
            with act.Else():
                def rows_of(e, lo, hi):
                    if isinstance(e, int):
                        return A["rows"][e * CAP + lo:e * CAP + hi]
                    return A["rows"][bass.ds(e * CAP + lo, hi - lo)]

                def fetch(e):
                    act.dma_start(xg[:, 0], rows_of(e, 0, P)).then_inc(xg_in, 16)
                    act.dma_start(xg[0:CAP - P, 1], rows_of(e, P, CAP)).then_inc(xg_in, 16)

                credit(act, yo_act, 2)
                credit(act, yo_stored, 32)
                act.wait_ge(scattered, 16 * 2 * CH)
                fetch(0)

                def expert(e, last):
                    for i in (0, 2):
                        act.wait_ge(xg_t, e * 4 + (i + 1))
                        src = PS[:, (1, 2, 6, 7)[i], :].rearrange("p (t n) -> p t n", t=2)[:, :, 0:CAP]
                        act.activation(xe[:, 2 * i:2 * i + 2], src, ACT.Copy).then_inc(xe_act, 1)
                    if not last:
                        act.wait_ge(xg_t, e * 4 + 4)
                        fetch(e + 1)
                    for f in range(ET):
                        tile_done(act, "moe", e * 30 + (2 * f + 1))
                        act.activation(sge[:, f % 4], PS[:, f % 4, 0:CAP], ACT.Silu).then_inc(gate_done, 1)
                    for o in range(4):
                        tile_done(act, "moe", e * 30 + (2 * ET + 2 * o))
                        act.activation(yf[:, 2 * o], PS[:, 4, 0:CAP], ACT.Copy).then_inc(yf_act, 1)
                    for half in range(2):
                        act.wait_ge(yo_t, e * 2 + (half + 1))
                        if half == 0:
                            act.wait_ge(yo_stored, e * 32 + 32)
                        act.activation(yo[:, 0, half * 512:half * 512 + 512], PS[:, 4 + half, :], ACT.Copy).then_inc(yo_act, 1)
                    act.wait_ge(yo_act, e * 2 + 4)
                    act.dma_start(rows_of(e, 0, P), yo[:, 0]).then_inc(yo_stored, 16)
                    act.wait_ge(yo_dve, e * 2 + 4)
                    act.dma_start(rows_of(e, P, CAP), yo[0:CAP - P, 1]).then_inc(yo_stored, 16)
                with act.Fori(0, NE - 1) as e:
                    expert(e, False)
                expert(NE - 1, True)
            norm_a(4, hn2, x_done)

        @block.vector
        def _(dve):
            n_chain = [0]

            def link(ins):
                n_chain[0] += 1
                ins.then_inc(dve_chain, 1)
                dve.wait_ge(dve_chain, n_chain[0])

            def add_square(n, buf, kt):
                dve.wait_ge(norm_sq, 8 * n + kt + 1)
                if 7 * n + kt > 1:
                    dve.wait_ge(norm_add, 7 * n + kt - 1)
                dve.tensor_tensor(buf[:, 0], buf[:, 0], buf[:, kt], ALU.add).then_inc(norm_add, 1)

            def norm_v(n, buf):
                dve.wait_ge(norm_std, n + 1)
                for kt in range(KT):
                    dve.tensor_tensor(buf[:, kt], x[:, kt], rstd[:], ALU.mult).then_inc(norm_x, 1)

            dve.memset(scond[:].rearrange("p a b -> p (a b)"), 0.0).then_inc(cond_zero, 1)
            dve.wait_ge(loaded, 64)
            link(dve.tensor_scalar(w0h[:], vcol("w0", 0, 4 * KT), 0.5, None, ALU.mult))
            link(dve.tensor_scalar(omka[:], vcol("k_a", 0, KT), -1.0, 1.0, ALU.mult, ALU.add))
            a0 = CONST["in_scale"][0]
            link(dve.tensor_tensor(bs_in[:], vcol("b_in", 0, IN_TILES), const[:, a0:a0 + IN_TILES], ALU.mult))
            for kt in range(1, KT):
                add_square(0, hn, kt)
            norm_v(0, hn)
            mf = mods[:].rearrange("p l k t s -> p (l k t) s")

            def ada_columns(group, bank):
                dve.wait_ge(ada_t, group + 1)
                src = PS[:, bank, 0:256].rearrange("p (h q r) -> p q h r", h=2, q=4)[:, :, :, 0:2]
                b0 = VEC["b_ada"][0]
                out = mf[:, bass.ds(group * 8, 8), :].rearrange("p (q h) s -> p q h s", h=2)
                b = vec[:, bass.ds(group * 8 + b0, 8)].rearrange("p (q h) -> p q h", h=2).unsqueeze(3).to_broadcast([P, 4, 2, 2])
                dve.tensor_tensor(out, src, b, ALU.add).then_inc(ada_done, 1)

            def norm_scale(la, w):
                g = vcol("gn1" if w == 0 else "gn2", la * KT, KT)
                link(dve.tensor_scalar(gs[:, la, w], mods[:, la, 3 * w + 1], 1.0, None, ALU.add))
                link(dve.tensor_tensor(gs[:, la, w], gs[:, la, w], g.unsqueeze(2).to_broadcast([P, KT, 2]), ALU.mult))
            for g in range(3):
                ada_columns(g, 3 + g)
            dve.wait_ge(ada_done, 3)
            norm_scale(0, 0)
            dve.sem_inc(mods_ready, 1)
            with dve.Fori(0, 9) as g:
                ada_columns(g + 3, 7)
            dve.wait_ge(ada_done, 12)
            for la, w in ((0, 1), (1, 0), (1, 1)):
                norm_scale(la, w)
            dve.sem_inc(mods_ready, 1)

            def residual_then_squares(name, layer, kind, n, buf):
                for t in range(KT):
                    residual(name, t % 3, t, layer, kind, t).then_inc(free[name], 1)
                    if t > 1:
                        add_square(n, buf, t - 1)
                add_square(n, buf, KT - 1)

            def residual(name, a, t, layer, kind, n):
                tile_done(dve, name, n)
                return gated_add(a, t, layer, kind)

            def gated_add(a, t, layer, kind):
                for s, (lo, hi) in enumerate(HALVES):
                    xs = x[:, t, lo:hi] if isinstance(t, int) else x[:, bass.ds(t, 1), lo:hi].rearrange("p a n -> p (a n)")
                    if isinstance(t, int):
                        ga = mods[:, layer, kind, t, s:s + 1]
                    else:
                        ga = mods[:].rearrange("p l k t s -> p (l k t s)")[:, bass.ds(t * 2 + ((layer * NADA + kind) * KT * 2 + s), 1)]
                    i = dve.scalar_tensor_tensor(out=xs, in0=acc(a)[:, lo:hi], scalar=ga, in1=xs, op0=ALU.mult, op1=ALU.add)
                return i

            dve.wait_ge(zeroed, 2)
            dve.wait_ge(free["in"], 3 + IN_TILES)
            R = slice(0, 64)
            Z0, Z1 = slice(0, 32), slice(32, 64)
            mact.wait(dve, "lnf")
            mdve.done(dve.tensor_scalar(gf[R], gf[R], 0.0, None, ALU.min), "minf")
            mdve.wait(dve, "minf")
            mdve.done(dve.tensor_tensor(gf[R], gf[R], tmp_row[R], ALU.subtract), "lf")
            mdve.wait(dve, "lf")
            mr = cst("mreset")
            mdve.done(dve.tensor_tensor_scan(b_row[Z0], mr[Z0, 0:TOK], gf[Z0], 0.0, ALU.mult, ALU.add), "b0")
            mdve.done(dve.tensor_tensor_scan(b_row[Z1][:, ::-1], mr[Z1, 1:TOK + 1][:, ::-1], gf[Z1][:, ::-1], 0.0, ALU.mult, ALU.add), "b1")
            mdve.wait(dve, "b1")
            mdve.done(dve.tensor_tensor(g_row[R], gi[R], b_row[R], ALU.subtract), "g")
            m0 = vcol("m0", 0)
            Ls, Cs = slice(0, LAT), slice(LAT, TOK)
            mdve.done(dve.tensor_tensor_scan(gm[Z0, Ls], gf[Z0, Ls], gi[Z0, Ls], m0[Z0], ALU.add, ALU.max), "m00")
            mdve.done(dve.tensor_tensor_scan(gm[Z1, Ls][:, ::-1], gf[Z1, Ls][:, ::-1], gi[Z1, Ls][:, ::-1], m0[Z1], ALU.add, ALU.max), "m01")
            mdve.done(dve.tensor_tensor_scan(gm[Z0, Cs], gf[Z0, Cs], gi[Z0, Cs], 0.0, ALU.add, ALU.max), "m10")
            mdve.done(dve.tensor_tensor_scan(gm[Z1, Cs][:, ::-1], gf[Z1, Cs][:, ::-1], gi[Z1, Cs][:, ::-1], 0.0, ALU.add, ALU.max), "m11")
            mdve.wait(dve, "m11")
            mdve.done(dve.tensor_tensor(negG[R], b_row[R], gm[R], ALU.subtract), "negG")
            mdve.wait(dve, "negG")
            mch = gm[:, 0:TOK].rearrange("p (c n) -> p c n", c=CH)
            gch = negG[:, 0:TOK].rearrange("p (c n) -> p c n", c=CH)
            mp = mprev.unsqueeze(2)
            mdve.done(dve.tensor_copy(mp[Z0, 1:4], mch[Z0, 0:3, P - 1:P]), "mprev0")
            mdve.done(dve.tensor_copy(mp[Z1, 0:3], mch[Z1, 1:4, 0:1]), "mprev1")
            mdve.done(dve.tensor_copy(mprev[Z0, 0:1], m0[Z0]), "mprev2")
            mdve.done(dve.tensor_copy(mprev[Z1, 3:4], m0[Z1]), "mprev3")
            mdve.done(dve.memset(mprev[R, 4:5], 0.0), "mprev4")
            mdve.done(dve.tensor_copy(gend.unsqueeze(2)[Z0], gch[Z0, :, P - 1:P]), "mprev5")
            mdve.done(dve.tensor_copy(gend.unsqueeze(2)[Z1], gch[Z1, :, 0:1]), "gend0")
            mdve.wait(dve, "gend0")
            mdve.done(dve.tensor_tensor(dec[R], mprev[R], gend[R], ALU.add), "gend1")
            mact.wait(dve, "dec")
            mdve.done(dve.tensor_tensor(decx[R], cst("ident")[R, 0:64].unsqueeze(1).to_broadcast([64, CH, 64]),
                                        dec[R].unsqueeze(2).to_broadcast([64, CH, 64]), ALU.mult), "decx")
            cw = colw.rearrange("p c k r -> p (c k r)")
            mpe.wait(dve, "cols0")
            mdve.done(dve.tensor_copy(cw[:, 0:512], PS[:, 6, :]), "cols0")
            mpe.wait(dve, "cols1")
            mdve.done(dve.tensor_copy(cw[:, 512:960], PS[:, 7, 0:448]), "cols1")
            mpe.wait(dve, "decb")
            pd = PS[:, 0, 0:CH * 64].rearrange("p (c r) -> p c r", c=CH)
            n = 0
            for half in range(2):
                for d in range(2):
                    hp = slice(64 * half, 64 * half + 64)
                    mdve.done(dve.tensor_copy(decp[hp, :, d, :], pd[hp, :, d * 32 + half:d * 32 + half + 7:2]), f"decp{n}")
                    n += 1
            seen = set()
            for n, (d, c) in enumerate(MGRP):
                seq = 0 if c < 4 else 1
                for g in range(2):
                    mpe.wait(dve, f"S{n}{g}")
                    mact.wait(dve, f"W{n}{g}")
                    wf = Wt[:, g].rearrange("p h n -> p (h n)")
                    mdve.done(dve.tensor_tensor(wf, wf, PS[:, 1, :], ALU.mult), f"P{n}{g}")
                    mpe.wait(dve, f"num{n}{g}")
                    if n or g:
                        mdve.wait(dve, f"h{n}0" if g else f"h{n-1}1")
                    for h in range(4):
                        o = slice((h % 2) * 129, (h % 2) * 129 + 129)
                        row = d * 32 + 2 * h + g
                        i = dve.tensor_scalar(comb[:, h, :], PS[:, 4 + h // 2, o], colw[:, c, 0, row:row + 1], None, ALU.mult)
                        if h == 3:
                            i.then_inc(dve_chain, 1)
                            n_chain[0] += 1
                    dve.wait_ge(dve_chain, n_chain[0])
                    for b in range(2):
                        i = dve.tensor_tensor(comb[:, 2 * b:2 * b + 2, :], comb[:, 2 * b:2 * b + 2, :],
                                              PS[:, 2 + b, 0:258].rearrange("p (h n) -> p h n", h=2), ALU.add)
                    mdve.done(i, f"comb{n}{g}")
                    mdve.wait(dve, f"comb{n}{g}")
                    em = colw[:, c, 2, d * 32 + g:d * 32 + AH:2]
                    dn = comb[:, :, DV:DV + 1]
                    mdve.done(dve.scalar_tensor_tensor(out=rden.unsqueeze(2), in0=dn, scalar=-1.0, in1=dn,
                                                       op0=ALU.mult, op1=ALU.max), f"absd{n}{g}")
                    mdve.wait(dve, f"absd{n}{g}")
                    mdve.done(dve.tensor_tensor(rden, rden, em, ALU.max), f"den{n}{g}")
                    mdve.wait(dve, f"den{n}{g}")
                    mdve.done(dve.reciprocal(rden, rden), f"rden{n}{g}")
                    mdve.wait(dve, f"rden{n}{g}")
                    for h in range(4):
                        o = hs_t[:, c, (2 * h + g) * DV:(2 * h + g + 1) * DV]
                        if (c, g) in seen:
                            i = dve.scalar_tensor_tensor(out=o, in0=comb[:, h, 0:DV], scalar=rden[:, h:h + 1], in1=o,
                                                         op0=ALU.mult, op1=ALU.add)
                        else:
                            i = dve.tensor_scalar(o, comb[:, h, 0:DV], rden[:, h:h + 1], None, ALU.mult)
                    seen.add((c, g))
                    mdve.done(i, f"h{n}{g}")
                mpe.wait(dve, f"C{n}")
                for pair in range(4):
                    s = Cst[:, d, seq, pair * 129:(pair + 1) * 129]
                    i = dve.scalar_tensor_tensor(out=s, in0=s, scalar=decp[:, c, d, pair:pair + 1],
                                                 in1=PS[:, 6 + pair // 2, (pair % 2) * 129:(pair % 2) * 129 + 129],
                                                 op0=ALU.mult, op1=ALU.add)
                mdve.done(i, f"C{n}")
            for c in range(CH):
                mact.wait(dve, f"sq{c}")
                mdve.done(dve.tensor_reduce(ms[:, c], sqt[c % 2], AX.X, ALU.add), f"ms{c}")
            mact.wait(dve, "sd")
            mdve.done(dve.reciprocal(ms, ms), "rs")
            mdve.wait(dve, "rs")
            for c in (0, 2, 4):
                hh = hs_t[:, c].rearrange("p (h n) -> p h n", h=AH)
                mdve.done(dve.tensor_tensor(hh, hh, ms[:, c].unsqueeze(2).to_broadcast([P, AH, DV]), ALU.mult), f"hn{c}")
            mact.wait(dve, "sigo")
            for h in range(AH):
                mpe.wait(dve, f"hT{h}")
                mdve.done(dve.scalar_tensor_tensor(out=o_[:, h], in0=acc(h % 3), scalar=vcol("g_head", h), in1=o_[:, h],
                                                   op0=ALU.mult, op1=ALU.mult), f"mo{h}")
            credit(dve, free["mout"], 3)
            residual_then_squares("mout", 0, 2, 1, hn_f)
            norm_v(1, hn_f)
            credit(dve, free["ffu"], 2)

            def ffu(k, u, lap):
                tile_done(dve, "ff", k * 2 + 1)
                dve.wait_ge(free["ffg"], k + 2)
                h = hid_f[:, k] if isinstance(k, int) else hid_f[:, bass.ds(k, 1)].rearrange("p a n -> p (a n)")
                dve.tensor_tensor(h, sg_f[:, u], acc((2 * u + 1) % 3), ALU.mult).then_inc(free["ffu"], 1)
            repeat(dve, FT, ffu)
            credit(dve, free["ffd"], 3)
            residual_then_squares("ffd", 0, 5, 2, hn1)
            norm_v(2, hn1)

            def grid(a, k0):
                return a[:, k0:k0 + 2, 0:LAT].rearrange("p k (r w) -> p k r w", w=64)
            sub, neg = [], []
            h0, s0 = grid(hn1, 0), grid(xx, 0)
            sub.append((s0[:, :, :, 1:], h0[:, :, :, :-1], h0[:, :, :, 1:])); neg.append((s0[:, :, :, 0:1], h0[:, :, :, 0:1]))
            h0, s0 = grid(hn1, 2), grid(xx, 2)
            sub.append((s0[:, :, :, :-1], h0[:, :, :, 1:], h0[:, :, :, :-1])); neg.append((s0[:, :, :, 63:64], h0[:, :, :, 63:64]))
            sub.append((xx[:, 4:6, 64:LAT], hn1[:, 4:6, 0:LAT - 64], hn1[:, 4:6, 64:LAT])); neg.append((xx[:, 4:6, 0:64], hn1[:, 4:6, 0:64]))
            sub.append((xx[:, 6:8, 0:LAT - 64], hn1[:, 6:8, 64:LAT], hn1[:, 6:8, 0:LAT - 64]))
            neg.append((xx[:, 6:8, LAT - 64:LAT], hn1[:, 6:8, LAT - 64:LAT]))
            sub.append((xx[:, 0:4, LAT + 1:TOK], hn1[:, 0:4, LAT:TOK - 1], hn1[:, 0:4, LAT + 1:TOK]))
            neg.append((xx[:, 0:4, LAT:LAT + 1], hn1[:, 0:4, LAT:LAT + 1]))
            sub.append((xx[:, 4:8, LAT:TOK - 1], hn1[:, 4:8, LAT + 1:TOK], hn1[:, 4:8, LAT:TOK - 1]))
            neg.append((xx[:, 4:8, TOK - 1:TOK], hn1[:, 4:8, TOK - 1:TOK]))

            def shift(pair):
                dve.wait_ge(norm_done, 32 + (8 if pair < 2 else 16))
                for n in (pair, 4 + pair // 2) if pair % 2 == 0 else (pair,):
                    (o, a, b), (on, an) = sub[n], neg[n]
                    dve.tensor_tensor(o, a, b, ALU.subtract).then_inc(xx_ready, 1)
                    dve.tensor_scalar(on, an, -1.0, None, ALU.mult).then_inc(xx_ready, 1)
                dve.wait_ge(xx_ready, (4, 6, 10, 12)[pair])
            for s in range(6):
                if s >= 3:
                    tile_done(dve, "rkv", 19 + 2 * (s - 3))
                for kt in range(KT):
                    if s == 0 and kt % 2 == 0:
                        shift(kt // 2)
                    dve.scalar_tensor_tensor(out=xm[s % 3][:, kt], in0=xx[:, kt], scalar=vcol("mu", s * KT + kt),
                                             in1=hn1[:, kt], op0=ALU.mult, op1=ALU.add).then_inc(xm_ready, 1)
            dve.wait_ge(zero_set, 1)
            tile_done(dve, "lora", 2)
            tile_done(dve, "rkv", 23)
            dve.sem_inc(rdve.sem, len(rdve.names))
            I2 = cst("ident2").unsqueeze(1)
            ch = lambda a: a.rearrange("p (c n) -> p c n", c=C64)

            def log_w_sums(steps, d, lap):
                steps.done(dve.tensor_scalar(T[5], T[5], -DECAY / 2, -DECAY / 2, ALU.mult, ALU.add), f"lw{d}")
                steps.wait(dve, f"lw{d}", lap)
                rev = slice(None, None, -1) if d else slice(None)
                steps.done(dve.tensor_tensor_scan(T[6][:, rev], cst("reset")[:, d:d + TOK][:, rev], T[5][:, rev], 0.0,
                                                  ALU.mult, ALU.add), f"c{d}")
                steps.wait(dve, f"c{d}", lap)
                steps.done(dve.tensor_tensor(T[7], T[6], T[5], ALU.subtract), f"ce{d}")

            def head(j):
                dve.wait_ge(rkv_in, j * 16 + 16)
                kr, vv = rkv[:, 1], rkv[:, 2]
                hdve.done(dve.tensor_scalar(T[0], kr, vec[:, bass.ds(j + VEC["k_k"][0], 1)], None, ALU.mult), "kk0")
                for h in range(2):
                    hp = slice(64 * h, 64 * h + 64)
                    hdve.done(dve.tensor_copy(BY[1][hp, :, 64 * h:64 * h + 64], ch(vv)[hp]), f"vT{h}")
                hact.wait(dve, "thw0", j)
                log_w_sums(hdve, 0, j)
                hpe.wait(dve, "knorm", j)
                hdve.done(dve.tensor_scalar(T[1], psf[:, 0:TOK], 1e-24, None, ALU.max), "kmax")
                hdve.next = 0
            head(0)
            dve.wait_ge(zero_set, 6)
            with dve.Fori(0, KT) as j:
                J = j + 1
                vc = lambda name, k0=0: vec[:, bass.ds(j + (VEC[name][0] + k0), 1)]
                wide = lambda b: psf[:, b * 512:b * 512 + TOK]
                ch = lambda a: a.rearrange("p (c n) -> p c n", c=C64)
                W = lambda name, lap=J: rdve.wait(dve, name, lap)
                rr, kr, vv = rkv[:, 0], rkv[:, 1], rkv[:, 2]
                for d in range(2):
                    kd = T[3] if d == 0 else T[9]
                    if d:
                        ract.wait(dve, "tha1", J)
                        log_w_sums(rdve, 1, J)
                    else:
                        hact.wait(dve, "tha0", j)
                    rdve.done(dve.tensor_scalar(T[8], T[8], 0.5, 0.5, ALU.mult, ALU.add), f"a{d}")
                    W(f"a{d}")
                    rdve.done(dve.tensor_scalar(kd, T[8], vc("k_a"), omka[:, bass.ds(j, 1)], ALU.mult, ALU.add), f"f{d}")
                    W(f"f{d}")
                    rdve.done(dve.tensor_tensor(kd, kd, kr, ALU.mult), f"kd{d}")
                    if d == 0:
                        ract.wait(dve, "knorm", J)
                        rdve.done(dve.tensor_tensor(T[0], T[0], T[1], ALU.mult), "kk")
                    W("kk")
                    rdve.done(dve.tensor_tensor(T[8], T[8], T[0], ALU.mult), f"b{d}")
                    ract.wait(dve, f"e3{d}", J)
                    rdve.done(dve.tensor_tensor(QR[d][:, :, P:192], ch(rr), ch(T[5]), ALU.mult), f"R{d}")
                    W(f"b{d}")
                    if d:
                        rpe.wait(dve, "V2", J)
                    for nm, dst, a, b in (("Q", QR[d], T[0], T[7]), ("K", KX[d], kd, T[6]), ("B", BY[d], T[8], T[6])):
                        for h in range(2):
                            hp = slice(64 * h, 64 * h + 64)
                            rdve.done(dve.tensor_tensor(dst[hp, :, 64 * h:64 * h + 64], ch(a)[hp], ch(b)[hp], ALU.mult), f"{nm}{h}{d}")
                dve.wait_ge(st_loaded, j * 16 + 16)
                dve.memset(St[:, 2:4], 0.0)
                for d in range(2):
                    mst = cst(f"strict{d}").unsqueeze(1).to_broadcast([P, 2, P])
                    minc = cst(f"incl{d}").unsqueeze(1).to_broadcast([P, 2, HD])
                    for nm, M, Ar, banks in (("GK", MkT[d], Ark[d], (6, 7, 0, 1, 2)), ("GB", LT[d], Arb[d], (3, 4, 5, 6, 7))):
                        for q in range(5):
                            rpe.wait(dve, f"{nm}{d}{q}", J)
                            src = PS[:, banks[q], 0:384].rearrange("p (c n) -> p c n", c=2)
                            rdve.done(dve.tensor_tensor(M[:, 2 * q:2 * q + 2], src[:, :, 0:P], mst, ALU.mult),
                                      f"MkT{d}{q}" if nm == "GK" else f"LT{d}{q}")
                            rdve.done(dve.tensor_tensor(Ar[:, 2 * q:2 * q + 2], src[:, :, P:192], minc, ALU.mult),
                                      f"Ark{d}{q}" if nm == "GK" else f"Arb{d}{q}")
                W("LT14")
                rdve.done(dve.tensor_tensor(XT[1], LT[1], cst("nbd2").unsqueeze(1).to_broadcast([P, C64, P]), ALU.mult), "XTa1")
                W("XTa1")
                rdve.done(dve.tensor_tensor(XT[1], XT[1], cst("ident").unsqueeze(1).to_broadcast([P, C64, P]), ALU.add), "XT21")
                rdve.done(dve.tensor_tensor(T[3], T[3], T[9], ALU.add), "kds")
                ract.wait(dve, "pend1", J)
                rdve.done(dve.tensor_scalar(T[5], rr, vc("r_k"), None, ALU.mult), "rk")
                W("rk")
                rdve.done(dve.tensor_tensor(T[5], T[5], T[3], ALU.mult), "rkk")
                for d in range(2):
                    for g, (c0, c1) in enumerate(GR):
                        rpe.wait(dve, f"KV{d}{g}", J)
                        src = PS[:, 3 + g, 0:(c1 - c0) * P].rearrange("p (c n) -> p c n", n=P)
                        rdve.done(dve.tensor_tensor(Ktok[d][:, c0:c1], src, pend[:, d, c0:c1].unsqueeze(2).to_broadcast([P, c1 - c0, P]),
                                                    ALU.mult), f"KV{d}{g}")
                rpe.wait(dve, "bonus", J)
                rdve.done(dve.tensor_tensor(T[4], wide(6), vv, ALU.mult), "yb")
                W("yb")
                rpe.wait(dve, "yV", J)
                rdve.done(dve.tensor_tensor(T[4], T[4], wide(0), ALU.add), "y0")
                for lv in LEVELS:
                    for d in range(2):
                        for g, (c0, c1) in enumerate(GR):
                            rpe.wait(dve, f"Y{lv}{d}{g}", J)
                            src = PS[:, d * 3 + g, 0:(c1 - c0) * P].rearrange("p (c n) -> p c n", n=P)
                            rdve.done(dve.tensor_tensor(BY[d][:, c0:c1], I2.to_broadcast([P, c1 - c0, P]), src, ALU.subtract), f"Y{lv}{d}{g}")
                    if lv < 64:
                        for d in range(2):
                            for g, (c0, c1) in enumerate(GR):
                                rpe.wait(dve, f"Z{lv}{d}{g}", J)
                                src = PS[:, d * 3 + g, 0:(c1 - c0) * P].rearrange("p (c n) -> p c n", n=P)
                                rdve.done(dve.tensor_tensor(XT[d][:, c0:c1], src, cst(f"bd{lv}").unsqueeze(1).to_broadcast([P, c1 - c0, P]),
                                                            ALU.mult), f"Z{lv}{d}{g}")
                W("y0")
                for t in range(8):
                    mine = chain_steps(t)
                    for i in mine:
                        d, cs = CHAINS[i]
                        rpe.wait(dve, f"rhs{t}{i}", J)
                        rdve.done(dve.tensor_tensor(RU[:, i], PS[:, i, 0:P], MkT[d][:, cs[t]], ALU.add), f"rhs{t}{i}")
                    for i in mine:
                        d, cs = CHAINS[i]
                        rdve.done(dve.scalar_tensor_tensor(out=Sp[:, i], in0=(St, St_odd)[t % 2][:, i], scalar=pend[:, d, cs[t]:cs[t] + 1],
                                                           in1=Ktok[d][:, cs[t]], op0=ALU.mult, op1=ALU.add), f"Sp{t}{i}")
                    for i in mine:
                        d, cs = CHAINS[i]
                        W(f"Sp{t}{i}")
                        rpe.wait(dve, f"S{t}{i}", J)
                        rdve.done(dve.scalar_tensor_tensor(out=(St_odd, St)[t % 2][:, i], in0=PS[:, 4 + i, 0:P], scalar=pend[:, d, cs[t]:cs[t] + 1],
                                                           in1=Sp[:, i], op0=ALU.mult, op1=ALU.add), f"S{t}{i}")
                    for i in mine:
                        c = CHAINS[i][1][t]
                        ys = T[4][:, c * HD:(c + 1) * HD]
                        rpe.wait(dve, f"y{t}{i}", J)
                        rdve.done(dve.tensor_tensor(ys, ys, PS[:, i if t < 2 else 2 + i, 128:128 + HD], ALU.add), f"y{t}{i}")
                    W(f"y{t}{chain_steps(t)[-1]}")
                rpe.wait(dve, "mean", J)
                rdve.done(dve.tensor_tensor(T[9], T[4], wide(0), ALU.subtract), "yc")
                head(J)
                ract.wait(dve, "std", J)
                rdve.done(dve.tensor_tensor(T[9], T[9], T[3], ALU.mult), "yn")
                W("yn")
                rdve.done(dve.tensor_scalar(T[9], T[9], vc("ln_g"), vc("ln_b"), ALU.mult, ALU.add), "yl")
                W("yl")
                rdve.done(dve.tensor_tensor(gk[:, bass.ds(j, 1)].rearrange("p a n -> p (a n)"), T[9], T[2], ALU.mult), "yg")
                W("yg")
                rdve.next = 0
            credit(dve, free["rout"], 3)
            residual_then_squares("rout", 1, 2, 3, hn2)
            norm_v(3, hn2)
            br = vcol("b_router", 0, NE)
            cd = cst("code").unsqueeze(1).to_broadcast([P, CH, NE])
            dve.wait_ge(logits_rows, 1)
            dve.tensor_copy(logit_rows[0:NE], psf[0:NE, 0:TOK]).then_inc(logits_copied, 1)
            dve.wait_ge(logits_full, 1)
            link(dve.tensor_tensor(lg, PS[:, 2, 0:CH * NE].rearrange("p (c e) -> p c e", c=CH),
                                   br.unsqueeze(1).to_broadcast([P, CH, NE]), ALU.add))
            wide_ = lambda a: a.unsqueeze(2).to_broadcast([P, CH, NE])

            def top(src, mx, oh):
                link(dve.tensor_reduce(mx, src, AX.X, ALU.max))
                link(dve.tensor_tensor(eq, src, wide_(mx), ALU.is_equal))
                link(dve.tensor_tensor(eq, eq, cd, ALU.mult))
                link(dve.tensor_reduce(e12, eq, AX.X, ALU.max))
                link(dve.tensor_tensor(oh, cd, wide_(e12), ALU.is_equal))
            top(lg, mx1, oh1)
            link(dve.tensor_scalar(l2g, oh1, NEG, None, ALU.mult))
            link(dve.tensor_tensor(l2g, l2g, lg, ALU.add))
            top(l2g, mx2, oh2)
            link(dve.tensor_tensor(one_hot, oh1, oh2, ALU.add))
            dve.sem_inc(onehot_ready, 1)
            link(dve.tensor_tensor(e12, mx2, mx1, ALU.subtract))
            dve.sem_inc(exp_in, 1)
            link(dve.tensor_scalar(eq, cd, float(-CAP), float(NE * CAP), ALU.mult, ALU.add))
            dve.wait_ge(counted, 1)
            link(dve.tensor_tensor(row_of, PS[:, 0, 0:CH * NE].rearrange("p (c e) -> p c e", c=CH), eq, ALU.add))
            for k, oh in enumerate((oh1, oh2)):
                link(dve.tensor_tensor(eq, oh, row_of, ALU.mult))
                link(dve.tensor_reduce(rows_f[:, k], eq, AX.X, ALU.add))
            link(dve.tensor_reduce(over, PS[:, 1, 0:NE], AX.X, ALU.max))
            link(dve.tensor_scalar(over, over, float(CAP), None, ALU.is_gt))
            link(dve.tensor_copy(rows_i[:, 0:2 * CH], rows_f.rearrange("p k c -> p (k c)")))
            link(dve.tensor_copy(rows_i[:, 2 * CH:2 * CH + 1], over))
            dve.sem_inc(routes_ready, 1)
            dve.wait_ge(exp_done, 1)
            link(dve.tensor_scalar(p1, e12, 1.0, None, ALU.add))
            link(dve.reciprocal(p1, p1))
            link(dve.tensor_tensor(p2, e12, p1, ALU.mult))
            dve.wait_ge(routes_ready, 1)
            dense = dve.value_load(rows_i[0:1, 2 * CH:2 * CH + 1], min_val=0, max_val=1)
            with dve.If(dense):
                link(dve.tensor_tensor(oh1, oh1, wide_(p1), ALU.mult))
                link(dve.tensor_tensor(oh2, oh2, wide_(p2), ALU.mult))
                dve.tensor_tensor(comb_w, oh1, oh2, ALU.add).then_inc(comb_ready, 1)
                credit(dve, free["moed"], 3)
                with dve.Fori(0, NE) as e:
                    for f in range(ET):
                        tile_done(dve, "moe", e * 30 + (2 * f + 1))
                        dve.wait_ge(free["moeg"], e * ET + (f + 1))
                        dve.tensor_tensor(hid[:, f], sg[:, f % RING], acc((2 * f + 1) % 3), ALU.mult).then_inc(free["moeu"], 1)
                        dve.wait_ge(free["moeu"], e * ET + (f + 1))
                        dve.tensor_tensor(hid[:, f], hid[:, f], cb[:, bass.ds(e, 1)].rearrange("p a n -> p (a n)"),
                                          ALU.mult).then_inc(hid_ready, 1)
                    for o in range(8):
                        residual("moe", (2 * ET + o) % 3, o, 1, 5, e * 30 + (2 * ET + o)).then_inc(free["moed"], 1)
                dve.wait_ge(free["moed"], 3 + 8 * NE)
                dve.sem_inc(x_done, KT)
            with dve.Else():
                dve.sem_inc(pair_used, 1)
                credit(dve, yo_dve, 2)
                with dve.Fori(0, NE) as e:
                    for i in (1, 3):
                        dve.wait_ge(xg_t, e * 4 + (i + 1))
                        src = PS[:, (1, 2, 6, 7)[i], :].rearrange("p (t n) -> p t n", t=2)[:, :, 0:CAP]
                        dve.tensor_copy(xe[:, 2 * i:2 * i + 2], src).then_inc(xe_dve, 1)
                    for f in range(ET):
                        tile_done(dve, "moe", e * 30 + (2 * f + 1))
                        dve.wait_ge(gate_done, e * ET + (f + 1))
                        dve.tensor_tensor(hide[:, f], sge[:, f % 4], PS[:, f % 4, CAP:2 * CAP], ALU.mult).then_inc(pair_used, 1)
                    for o in range(4):
                        tile_done(dve, "moe", e * 30 + (2 * ET + 2 * o + 1))
                        dve.tensor_copy(yf[:, 2 * o + 1], PS[:, 5, 0:CAP]).then_inc(yf_dve, 1)
                    for half in range(2):
                        dve.wait_ge(yo_t, e * 2 + (half + 1))
                        if half == 0:
                            dve.wait_ge(yo_stored, e * 32 + 32)
                        dve.tensor_copy(yo[0:CAP - P, 1, half * 512:half * 512 + 512], PS[0:CAP - P, 6 + half, :]).then_inc(yo_dve, 1)
                for c in range(CH):
                    dve.wait_ge(gathered[c], 32)
                    dve.tensor_scalar(hnt[:, c], hnt[:, c], p1[:, c:c + 1], None, ALU.mult).then_inc(combine, 1)
                    dve.wait_ge(combine, 2 * c + 1)
                    dve.scalar_tensor_tensor(out=hnt[:, c], in0=out2[:, c], scalar=p2[:, c:c + 1], in1=hnt[:, c],
                                             op0=ALU.mult, op1=ALU.add).then_inc(combine, 1)
                for kt in range(KT):
                    dve.wait_ge(outs_t, kt + 1)
                    gated_add(kt % 3, kt, 1, 5).then_inc(outs_used, 1)
                    dve.wait_ge(outs_used, kt + 1)
                    dve.sem_inc(x_done, 1)
            for kt in range(1, KT):
                add_square(4, hn2, kt)
            dve.wait_ge(norm_std, 5)
            for kt in range(KT):
                dve.scalar_tensor_tensor(out=hn2[:, kt], in0=x[:, kt], scalar=vcol("gf", kt), in1=rstd[:],
                                         op0=ALU.mult, op1=ALU.mult).then_inc(y_ready, 1)
    return nc


def constants():
    c = np.zeros((P, N_CONST), np.float32)
    p, f = np.arange(P)[:, None], np.arange(P)[None, :]

    def put(name, v):
        a, w = CONST[name]
        c[:, a:a + w] = v
    eye = (p == f)
    put("ident", eye)
    put("ident2", 2 * eye)
    put("ones", 1)
    same = (p // HD == f // HD)
    put("headones", same)
    put("headmean", same / HD)
    put("neg0", np.where(p <= f, 0, NEG))
    put("neg1", np.where(p >= f, 0, NEG))
    put("strict0", p < f)
    put("strict1", p > f)
    put("incl0", (p % HD) <= f[:, :HD])
    put("incl1", (p % HD) >= f[:, :HD])
    put("kk_back", 16 * np.log(2))
    put("nbd2", -1.0 * (p // 2 == f // 2))
    for b in (4, 8, 16, 32):
        put(f"bd{b}", p // b == f // b)
    t = np.arange(TOK + 1)[None, :]
    put("reset", t % HD != 0)
    put("mreset", t % P != 0)
    s = np.ones(IN_TILES)
    s[4:8] = DK ** -0.5
    put("in_scale", s)
    put("eps", EPS)
    put("ln_eps", LN_EPS)
    put("code", np.arange(NE, 0, -1))
    return c


def slab8(w):
    n = w.shape[1] // 256
    return w.reshape(KT, P, n, 256).transpose(2, 1, 0, 3).reshape(n, P, KT * 256)


def feat(v):
    return v.reshape(-1, P).T


def layout(i):
    a = {k: np.asarray(v) for k, v in i.items()}
    out = {}
    xs = np.concatenate([a["x_sample"][0], a["x_prompt"][0]])
    out["x"] = np.ascontiguousarray(xs.T.reshape(KT, P, TOK).transpose(1, 0, 2))
    win, bin_ = a["w_m_in"][0], a["b_m_in"][0]
    wi, bi = np.zeros((D, IN_TILES * P), np.float32), np.zeros(IN_TILES * P, np.float32)
    wi[:, :3072], bi[:3072] = win[:, :3072], bin_[:3072]
    for kind in range(2):
        for d in range(2):
            src = 3072 + kind * 16 + d * AH
            dst = (24 + kind) * P + d * 32
            wi[:, dst:dst + AH], bi[dst:dst + AH] = win[:, src:src + AH], bin_[src:src + AH]
    gu = a["w_ff_gu"][0].reshape(D, 2, FT, P).transpose(0, 2, 1, 3).reshape(D, 2 * DFF)
    rkv = a["w_rkv"][0].reshape(3, D, 4, 256).transpose(1, 2, 0, 3).reshape(D, 12 * 256)
    lo = np.zeros((D, 512), np.float32)
    lo[:, 0:64], lo[:, 64:128] = a["w_decay1"][0, 0], a["w_decay1"][0, 1]
    lo[:, 128:192], lo[:, 192:256] = a["w_iclr1"][0, 0], a["w_iclr1"][0, 1]
    lo[:, 256:384] = a["w_gate1"][0]
    eg = a["w_exp_gu"][0].reshape(NE, D, 2, ET, P).transpose(0, 1, 3, 2, 4).reshape(NE, D, 2 * ET * P)
    out["k8"] = np.concatenate([slab8(a["w_ada"][0]), slab8(a["w_ada"][1]), slab8(wi), slab8(a["w_m_out"][0]), slab8(gu),
                                slab8(rkv), slab8(lo), slab8(a["w_rwkv_out"][0])] + [slab8(eg[e]) for e in range(NE)])
    out["ffd"] = np.ascontiguousarray(a["w_ff_down"][0].reshape(FT, P, 8, P).transpose(2, 1, 0, 3).reshape(8, P, SLAB))
    out["exd"] = np.ascontiguousarray(a["w_exp_down"][0].reshape(NE, ET, P, 4, 256).transpose(0, 3, 2, 1, 4).reshape(NE * 4, P, SLAB))
    out["wrouter"] = np.ascontiguousarray(a["w_router"][0].reshape(KT, P, NE).transpose(1, 0, 2))
    l2 = np.stack([a["w_decay2"][0].reshape(P, D), a["w_iclr2"][0].reshape(P, D), a["w_gate2"][0]])
    out["l2"] = np.ascontiguousarray(l2.reshape(3, P, KT, P).transpose(2, 1, 0, 3))
    C0 = np.concatenate([a["state_mlstm_C"][0, 0], a["state_mlstm_n"][0, 0][..., None]], -1)
    out["C0"] = np.ascontiguousarray(C0.reshape(2, 4, 2, DK, DV + 1).transpose(2, 3, 0, 1, 4).reshape(P, 2, 4 * (DV + 1)))
    S = a["state_rwkv_S"][0, 0].reshape(2, KT, 2, HD, HD)
    S0 = np.zeros((KT, P, 2, P), np.float32)
    for h in range(2):
        S0[:, h * HD:(h + 1) * HD, :, h * HD:(h + 1) * HD] = S[:, :, h].transpose(1, 3, 0, 2)
    out["S0"] = S0
    v = np.zeros((P, N_VEC), np.float32)

    def put(name, val):
        at, w = VEC[name]
        v[:, at:at + w] = val
    put("cond", np.stack([feat(a["c"][0]), feat(a["c_ctx"])], -1).reshape(P, 2 * KT))
    for name, key in (("b_ada", "b_ada"), ("gn1", "g_norm1"), ("gn2", "g_norm2"), ("gf", "g_final"), ("g_head", "g_m_head"),
                      ("mu", "mu_rwkv"), ("w0", "w_decay0"), ("a0", "w_iclr0"), ("k_k", "k_k"), ("k_a", "k_a"),
                      ("r_k", "r_k"), ("ln_g", "g_ln_x"), ("ln_b", "b_ln_x")):
        put(name, feat(a[key]))
    put("b_in", feat(bi))
    put("b_router", a["b_router"][0][None, :])
    at = VEC["m0"][0]
    v[0:AH, at], v[32:32 + AH, at] = a["state_mlstm_m"][0, 0, 0], a["state_mlstm_m"][0, 0, 1]
    out["vec"] = v
    out["const"] = constants()
    return out


OUTS = {"y": (P, KT, TOK), "C_out": (P, 2, 4 * (DV + 1)), "m_out": (64, 1), "S_out": (KT, P, 2, P)}


def restore(r):
    y = r["y"].transpose(1, 0, 2).reshape(D, TOK).T
    C = r["C_out"].reshape(2, DK, 2, 4, DV + 1).transpose(2, 3, 0, 1, 4).reshape(2, AH, DK, DV + 1)
    m = r["m_out"][:, 0].reshape(2, 32)[:, :AH]
    S = np.zeros((2, KT, 2, HD, HD), np.float32)
    for h in range(2):
        S[:, :, h] = r["S_out"][:, h * HD:(h + 1) * HD, :, h * HD:(h + 1) * HD].transpose(2, 0, 3, 1)
    c = np.ascontiguousarray
    return (c(y[LAT:][None]), c(y[:LAT][None]), c(C[None, None, ..., :DV]), c(C[None, None, ..., DV]), c(m[None, None]),
            c(S.reshape(1, 1, 2, BH, HD, HD)))


def declare(nc, arrays):
    A = {n: nc.dram_tensor(f"in_{n}", a.shape, F32, kind="ExternalInput").ap() for n, a in arrays.items()}
    A.update({n: nc.dram_tensor(n, s, F32, kind="ExternalOutput").ap() for n, s in OUTS.items()})
    A["rows"] = nc.dram_tensor("expert_rows", (NE * CAP, D), F32, kind="Internal").ap()
    A["rkv_s"] = nc.dram_tensor("rkv_s", (KT, P, 3, TOK), F32, kind="Internal").ap()
    return A


def kernel(**inputs):
    import concourse.bacc as bacc
    from concourse.bass_utils import run_bass_kernel_spmd

    arrays = layout(inputs)
    nc = bacc.Bacc("TRN2", target_bir_lowering=False, num_devices=1)
    build(nc, declare(nc, arrays))
    r = run_bass_kernel_spmd(nc, [{f"in_{n}": v for n, v in arrays.items()}], core_ids=[0])
    return restore(r.results[0])
```
